# Optimizing a Trainium2 kernel written in Bass

```python
import jax
import jax.numpy as jnp
from jax import lax
import numpy as np

D_MODEL = 1024
BATCH = 1
SEQ = 1024
DEPTH = 1

RET_HEADS = 4
RET_HD = 64
GDN_HEADS = 4
GDN_HD = 128
HG_HEADS = 4
HG_HD = 64
RET_W = RET_HEADS * RET_HD
GDN_W = GDN_HEADS * GDN_HD
HG_W = HG_HEADS * HG_HD
MIX_W = RET_W + GDN_W + HG_W
CHUNK = 64
CONV_W = 4
ROPE_BASE = 10000.0
N_GROUPS = 4
EXP_PER_GROUP = 8
N_EXPERTS = N_GROUPS * EXP_PER_GROUP
TOP_K = 2
D_EXPERT = 512
MOE_BLOCK = 256
EPS = 1e-6

_SPLITS = (RET_W,) * 4 + (GDN_W,) * 3 + (GDN_HEADS, GDN_HEADS, GDN_W) + (HG_W,) * 4
IN_W = sum(_SPLITS)
_SPLIT_IDX = tuple(int(v) for v in np.cumsum(_SPLITS)[:-1])

kernel_name = 'hybrid_ret_gdn_hgrn2_hmoe'

def rms_norm(x, g):
    xf = x.astype(jnp.float32)
    y = xf * lax.rsqrt(jnp.mean(xf * xf, axis=-1, keepdims=True) + EPS)
    return (y * g.astype(jnp.float32)).astype(x.dtype)

def head_norm(o, gain):
    o = o * lax.rsqrt(jnp.mean(o * o, axis=-1, keepdims=True) + EPS)
    return o * gain.astype(jnp.float32)

def l2norm(t):
    return t * lax.rsqrt(jnp.sum(t * t, axis=-1, keepdims=True) + EPS)

def rotary(t, pos):
    d = t.shape[-1]
    inv = ROPE_BASE ** (-jnp.arange(0, d, 2, dtype=jnp.float32) / d)
    ang = pos.astype(jnp.float32)[:, None] * inv[None, :]
    cos = jnp.cos(ang)[None, :, None, :]
    sin = jnp.sin(ang)[None, :, None, :]
    t1, t2 = t[..., : d // 2], t[..., d // 2:]
    return jnp.concatenate([t1 * cos - t2 * sin, t1 * sin + t2 * cos], axis=-1)

def causal_conv(x, w):
    c = x.shape[-1]
    y = lax.conv_general_dilated(x, w[:, None, :].astype(x.dtype), window_strides=(1,),
                                 padding=[(CONV_W - 1, 0)],
                                 dimension_numbers=('NWC', 'WIO', 'NWC'),
                                 feature_group_count=c)
    return jax.nn.silu(y)

def to_chunks(t):
    b, s, h, d = t.shape
    return t.reshape(b, s // CHUNK, CHUNK, h, d).transpose(0, 3, 1, 2, 4)

def from_chunks(t):
    b, h, n, c, d = t.shape
    return t.transpose(0, 2, 3, 1, 4).reshape(b, n * c, h, d)

def retention(q, k, v):
    h = q.shape[2]
    log_gamma = jnp.log(1.0 - 2.0 ** (-5.0 - jnp.arange(h, dtype=jnp.float32)))
    q = to_chunks(q)
    k = to_chunks(k) * (RET_HD ** -0.5)
    v = to_chunks(v)
    idx = jnp.arange(CHUNK, dtype=jnp.float32)
    diff = idx[:, None] - idx[None, :]
    causal = diff >= 0
    dmat = jnp.where(causal, jnp.exp(log_gamma[:, None, None] * jnp.where(causal, diff, 0.0)), 0.0)
    scores = jnp.einsum('bhncd,bhnsd->bhncs', q, k) * dmat[None, :, None]
    o = jnp.einsum('bhncs,bhnse->bhnce', scores, v)
    zeta = jnp.exp(log_gamma[:, None] * (CHUNK - 1.0 - idx))
    kv = jnp.einsum('bhnsd,hs,bhnse->bhnde', k, zeta, v)
    chunk_decay = jnp.exp(log_gamma * CHUNK)[None, :, None, None]

    def step(state, kv_n):
        return state * chunk_decay + kv_n, state

    _, prev = lax.scan(step, jnp.zeros_like(kv[:, :, 0]), jnp.moveaxis(kv, 2, 0))
    prev = jnp.moveaxis(prev, 0, 2)
    xi = jnp.exp(log_gamma[:, None] * (idx + 1.0))
    o = o + jnp.einsum('bhncd,hc,bhnde->bhnce', q, xi, prev)
    return from_chunks(o)

def gated_delta_rule(q, k, v, g, beta):
    dk = q.shape[-1]
    q = to_chunks(q) * (dk ** -0.5)
    k = to_chunks(k)
    v = to_chunks(v)
    dv = v.shape[-1]
    g = to_chunks(g[..., None])[..., 0]
    beta = to_chunks(beta[..., None])[..., 0]
    big_g = jnp.cumsum(g, axis=-1)
    causal = jnp.tril(jnp.ones((CHUNK, CHUNK), dtype=bool))
    strict = jnp.tril(jnp.ones((CHUNK, CHUNK), dtype=bool), -1)
    gamma = jnp.exp(jnp.where(causal, big_g[..., :, None] - big_g[..., None, :], -jnp.inf))
    kk = jnp.einsum('bhncd,bhnsd->bhncs', k, k)
    a_mat = jnp.where(strict, beta[..., :, None] * kk * gamma, 0.0) + jnp.eye(CHUNK, dtype=jnp.float32)
    rhs = jnp.concatenate([v * beta[..., None], k * (beta * jnp.exp(big_g))[..., None]], axis=-1)
    sol = lax.linalg.triangular_solve(a_mat, rhs, left_side=True, lower=True, unit_diagonal=True)
    u, w = sol[..., :dv], sol[..., dv:]
    qk = jnp.einsum('bhncd,bhnsd->bhncs', q, k) * gamma
    q_dec = q * jnp.exp(big_g)[..., None]
    k_dec = k * jnp.exp(big_g[..., -1:] - big_g)[..., None]
    g_last = jnp.exp(big_g[..., -1])

    def step(state, inp):
        u_n, w_n, qk_n, qd_n, kd_n, gl_n = inp
        v_new = u_n - jnp.einsum('bhcd,bhde->bhce', w_n, state)
        o = jnp.einsum('bhcd,bhde->bhce', qd_n, state) + jnp.einsum('bhcs,bhse->bhce', qk_n, v_new)
        state = state * gl_n[..., None, None] + jnp.einsum('bhcd,bhce->bhde', kd_n, v_new)
        return state, o

    xs = tuple(jnp.moveaxis(t, 2, 0) for t in (u, w, qk, q_dec, k_dec, g_last))
    s0 = jnp.zeros((q.shape[0], q.shape[1], dk, dv), jnp.float32)
    _, o = lax.scan(step, s0, xs)
    return from_chunks(jnp.moveaxis(o, 0, 2))

def hgrn2(q, k, v, g):
    q, k, v, g = to_chunks(q), to_chunks(k), to_chunks(v), to_chunks(g)
    big_g = jnp.cumsum(g, axis=3)
    causal = jnp.tril(jnp.ones((CHUNK, CHUNK), dtype=bool))[:, :, None]

    def step(state, inp):
        q_n, k_n, v_n, g_n = inp
        gd = g_n[:, :, :, None, :] - g_n[:, :, None, :, :]
        decay = jnp.exp(jnp.where(causal, gd, -jnp.inf))
        att = jnp.einsum('bhcd,bhcsd,bhsd->bhcs', q_n, decay, k_n)
        o = jnp.einsum('bhcs,bhse->bhce', att, v_n) + jnp.einsum('bhcd,bhde->bhce', q_n * jnp.exp(g_n), state)
        g_last = g_n[:, :, -1]
        state = state * jnp.exp(g_last)[..., None] + jnp.einsum(
            'bhsd,bhse->bhde', k_n * jnp.exp(g_last[:, :, None] - g_n), v_n)
        return state, o

    xs = tuple(jnp.moveaxis(t, 2, 0) for t in (q, k, v, big_g))
    s0 = jnp.zeros((q.shape[0], q.shape[1], q.shape[-1], v.shape[-1]), jnp.float32)
    _, o = lax.scan(step, s0, xs)
    return from_chunks(jnp.moveaxis(o, 0, 2))

def hybrid_mixer(h, w_in, w_out, conv_w, a_log, dt_bias, ret_g, gdn_g, hg_g, lb, pos):
    b, s, _ = h.shape
    f32 = jnp.float32
    proj = h @ w_in
    (rq, rk, rv, rg, dq, dk, dv, da, db, dz, hq, hf, hi, hgt) = jnp.split(proj, _SPLIT_IDX, axis=-1)

    def heads(t, n):
        return t.astype(f32).reshape(b, s, n, -1)

    r = retention(rotary(heads(rq, RET_HEADS), pos), rotary(heads(rk, RET_HEADS), pos), heads(rv, RET_HEADS))
    r = head_norm(r, ret_g.reshape(RET_HEADS, RET_HD)) * jax.nn.silu(heads(rg, RET_HEADS))

    qkv = causal_conv(jnp.concatenate([dq, dk, dv], axis=-1), conv_w)
    cq, ck, cv = jnp.split(qkv, (GDN_W, 2 * GDN_W), axis=-1)
    decay = -jnp.exp(a_log.astype(f32)) * jax.nn.softplus(da.astype(f32) + dt_bias.astype(f32))
    beta = jax.nn.sigmoid(db.astype(f32))
    d = gated_delta_rule(l2norm(heads(cq, GDN_HEADS)), l2norm(heads(ck, GDN_HEADS)),
                         heads(cv, GDN_HEADS), decay, beta)
    d = head_norm(d, gdn_g) * jax.nn.silu(heads(dz, GDN_HEADS))

    lbf = lb.astype(f32)
    fgate = lbf + (1.0 - lbf) * jax.nn.sigmoid(hf.astype(f32))
    c = hgrn2(jax.nn.silu(heads(hq, HG_HEADS)),
              (1.0 - fgate).reshape(b, s, HG_HEADS, HG_HD),
              heads(hi, HG_HEADS),
              jnp.log(fgate).reshape(b, s, HG_HEADS, HG_HD))
    c = head_norm(c, hg_g.reshape(HG_HEADS, HG_HD)) * jax.nn.silu(heads(hgt, HG_HEADS))

    mixed = jnp.concatenate([r.reshape(b, s, RET_W), d.reshape(b, s, GDN_W), c.reshape(b, s, HG_W)], axis=-1)
    return mixed.astype(h.dtype) @ w_out

def hier_moe(h, w_rg, w_re, w_gate, w_up, w_down):
    b, s, dm = h.shape
    t = b * s
    xt = h.reshape(t, dm)
    pg = jax.nn.softmax((xt @ w_rg).astype(jnp.float32), axis=-1)
    pg_top, grp = lax.top_k(pg, 1)
    el = (xt @ w_re).astype(jnp.float32).reshape(t, N_GROUPS, EXP_PER_GROUP)
    el_sel = jnp.take_along_axis(el, grp[:, :, None], axis=1)[:, 0]
    pe = jax.nn.softmax(el_sel, axis=-1)
    top_p, top_i = lax.top_k(pe, TOP_K)
    top_p = top_p / jnp.sum(top_p, axis=-1, keepdims=True)
    weights = pg_top * top_p
    expert = grp * EXP_PER_GROUP + top_i

    n_assign = t * TOP_K
    e_flat = expert.reshape(n_assign)
    t_flat = jnp.repeat(jnp.arange(t, dtype=jnp.int32), TOP_K)
    w_flat = weights.reshape(n_assign)
    order = jnp.argsort(e_flat)
    e_sorted = e_flat[order]
    counts = jnp.zeros((N_EXPERTS,), jnp.int32).at[e_flat].add(1)
    padded = (counts + MOE_BLOCK - 1) // MOE_BLOCK * MOE_BLOCK
    start_raw = jnp.cumsum(counts) - counts
    ends_pad = jnp.cumsum(padded)
    start_pad = ends_pad - padded
    dest = start_pad[e_sorted] + jnp.arange(n_assign, dtype=jnp.int32) - start_raw[e_sorted]
    n_blocks = (n_assign + N_EXPERTS * (MOE_BLOCK - 1) + MOE_BLOCK - 1) // MOE_BLOCK
    n_slots = n_blocks * MOE_BLOCK
    slot_tok = jnp.full((n_slots,), t, jnp.int32).at[dest].set(t_flat[order])
    slot_w = jnp.zeros((n_slots,), jnp.float32).at[dest].set(w_flat[order])
    block_exp = jnp.minimum(
        jnp.searchsorted(ends_pad, jnp.arange(n_blocks, dtype=jnp.int32) * MOE_BLOCK, side='right'),
        N_EXPERTS - 1)
    x_pad = jnp.concatenate([xt, jnp.zeros((1, dm), xt.dtype)], axis=0)

    def run_block(args):
        tok, e = args
        xb = x_pad[tok]
        hb = jax.nn.silu(xb @ w_gate[e]) * (xb @ w_up[e])
        return hb @ w_down[e]

    yb = lax.map(run_block, (slot_tok.reshape(n_blocks, MOE_BLOCK), block_exp))
    yb = yb.reshape(n_slots, dm)
    y = jax.ops.segment_sum(yb * slot_w[:, None].astype(yb.dtype), slot_tok, num_segments=t + 1)[:t]
    return y.reshape(b, s, dm)

def setup_inputs(seed: int = 0) -> dict:
    key = jax.random.key(seed)
    ks = jax.random.split(key, 20)
    f32 = jnp.float32

    def nrm(k, shape, scale):
        return jax.random.normal(k, shape, f32) * scale

    return {
        'x': nrm(ks[0], (BATCH, SEQ, D_MODEL), 1.0),
        'w_in': nrm(ks[1], (DEPTH, D_MODEL, IN_W), D_MODEL ** -0.5),
        'w_out': nrm(ks[2], (DEPTH, MIX_W, D_MODEL), MIX_W ** -0.5),
        'gdn_conv': nrm(ks[3], (DEPTH, CONV_W, 3 * GDN_W), CONV_W ** -0.5),
        'gdn_a_log': jnp.log(jax.random.uniform(ks[4], (DEPTH, GDN_HEADS), f32, 1.0, 16.0)),
        'gdn_dt_bias': nrm(ks[5], (DEPTH, GDN_HEADS), 0.5) - 2.0,
        'ret_norm': 1.0 + nrm(ks[6], (DEPTH, RET_W), 0.02),
        'gdn_norm': 1.0 + nrm(ks[7], (DEPTH, GDN_HD), 0.02),
        'hgrn_norm': 1.0 + nrm(ks[8], (DEPTH, HG_W), 0.02),
        'hgrn_lower_bounds': nrm(ks[9], (DEPTH, HG_W), 0.5),
        'attn_norm': 1.0 + nrm(ks[10], (DEPTH, D_MODEL), 0.02),
        'ffn_norm': 1.0 + nrm(ks[11], (DEPTH, D_MODEL), 0.02),
        'router_group': nrm(ks[12], (DEPTH, D_MODEL, N_GROUPS), D_MODEL ** -0.5),
        'router_expert': nrm(ks[13], (DEPTH, D_MODEL, N_EXPERTS), D_MODEL ** -0.5),
        'w_gate': nrm(ks[14], (DEPTH, N_EXPERTS, D_MODEL, D_EXPERT), D_MODEL ** -0.5),
        'w_up': nrm(ks[15], (DEPTH, N_EXPERTS, D_MODEL, D_EXPERT), D_MODEL ** -0.5),
        'w_down': nrm(ks[16], (DEPTH, N_EXPERTS, D_EXPERT, D_MODEL), D_EXPERT ** -0.5),
        'final_norm': 1.0 + nrm(ks[17], (D_MODEL,), 0.02),
    }

def reference(x, w_in, w_out, gdn_conv, gdn_a_log, gdn_dt_bias, ret_norm, gdn_norm, hgrn_norm,
              hgrn_lower_bounds, attn_norm, ffn_norm, router_group, router_expert,
              w_gate, w_up, w_down, final_norm):
    pos = jnp.arange(x.shape[1], dtype=jnp.int32)
    lb_all = jnp.cumsum(jax.nn.softmax(hgrn_lower_bounds.astype(jnp.float32), axis=0), axis=0)
    lb_all = lb_all - lb_all[0:1]
    h = x
    for l in range(DEPTH):
        h = h + hybrid_mixer(rms_norm(h, attn_norm[l]), w_in[l], w_out[l], gdn_conv[l], gdn_a_log[l],
                             gdn_dt_bias[l], ret_norm[l], gdn_norm[l], hgrn_norm[l], lb_all[l], pos)
        h = h + hier_moe(rms_norm(h, ffn_norm[l]), router_group[l], router_expert[l],
                         w_gate[l], w_up[l], w_down[l])
    return rms_norm(h, final_norm)


_drawn_inputs = setup_inputs


def setup_inputs(seed=0):
    import zlib

    import numpy as np

    out = dict(_drawn_inputs(seed))
    spreads = {}
    factors = {'ret_norm': 16.064,
     'gdn_norm': 13.272,
     'hgrn_norm': 18.575,
     'final_norm': 8.275,
     'ffn_norm': 4.179}
    for name, (base, spread) in spreads.items():
        noise = np.random.default_rng([zlib.crc32(name.encode()), seed]).standard_normal(out[name].shape)
        drawn = base * np.exp(spread * noise) if base else spread * noise
        out[name] = jnp.asarray(drawn.astype(out[name].dtype))
    for name, factor in factors.items():
        out[name] = (out[name] * factor).astype(out[name].dtype)
    return out
```

```python
from contextlib import ExitStack

import numpy as np
import concourse.bass as bass
from concourse import mybir

F32 = mybir.dt.float32
I32 = mybir.dt.int32
ALU = mybir.AluOpType
ACT = mybir.ActivationFunctionType
AX = mybir.AxisListType

P = 128
SEQ = 1024
DM = 1024
NT = SEQ // P
KD = DM // P
IN_W = 4104
C_RQ, C_RV, C_RG = 0, 512, 768
C_DQ, C_DA, C_DB, C_DZ = 1024, 2560, 2564, 2568
C_HQ, C_HI, C_HG = 3080, 3592, 3848
GROUPS = ((1024, 0), (1536, 0), (2048, 0), (3080, 0), (0, 0), (2560, 8), (512, 0), (3592, 0))
NG = len(GROUPS)
GW = 512
NE, NGRP, EPG, DE = 32, 4, 8, 512
KE = DE // P
BLK = 128
NB_MAX = 48
NB_MIN = 16
EPS = 1e-6
BIG = 1e30
LEVELS = 7
RET_GAMMA = [1.0 - 2.0 ** (-5.0 - h) for h in range(4)]


def const_layout():
    at, off = {}, 0
    for name, n in (("ident", 128), ("tri", 128), ("dmat", 512), ("xi", 256), ("zeta", 256), ("rdec", 2),
                    ("pair", 128), ("neg_up", 128), ("pos_low", 128), ("m0neg", 128), ("m0negT", 128),
                    ("lev", 8 * 128), ("ones", 128), ("stri", 128), ("iota", 32), ("biota", NB_MAX), ("pcol", 1),
                    ("c128", 8)):
        at[name] = (off, n)
        off += n
    return at, off


def host_consts():
    at, n = const_layout()
    c = np.zeros((P, n), np.float32)

    def put(name, a):
        o, w = at[name]
        c[:, o:o + w] = np.asarray(a, np.float32).reshape(P, w)

    p, f = np.arange(P)[:, None], np.arange(P)[None, :]
    put("ident", p == f)
    put("tri", p <= f)
    put("stri", p < f)
    put("ones", np.ones((P, P)))
    lg = np.log(np.array(RET_GAMMA))
    d = np.zeros((P, 4, P))
    for h in range(4):
        d[:, h] = np.where(f >= p, np.exp(lg[h] * np.maximum(f - p, 0)), 0) * 0.125
    put("dmat", d[:, [0, 2, 1, 3]])
    xi = np.zeros((P, 2, P))
    dec = np.zeros((P, 2))
    for j in range(2):
        for q in range(2):
            xi[64 * q:64 * q + 64, j] = np.exp(lg[2 * j + q] * (np.arange(P) + 1))[None]
            dec[64 * q:64 * q + 64, j] = np.exp(lg[2 * j + q] * P)
    put("xi", xi)
    put("rdec", dec)
    put("zeta", np.repeat(np.exp(lg[None] * (P - 1 - np.arange(P))[:, None]) * 0.125, 64, axis=1))
    put("pair", (p // 64) == (f // 64))
    put("neg_up", np.where(f >= p, 0, -BIG))
    put("pos_low", np.where(f < p, 0, BIG))
    lev = np.zeros((P, 8, P))
    for l in range(LEVELS):
        m = 2 ** l
        lev[:, l] = (p // (2 * m) == f // (2 * m)) & (p % (2 * m) < m) & (f % (2 * m) >= m)
    lev[:, 7] = p == f
    put("lev", lev)
    put("m0negT", -lev[:, 0])
    put("m0neg", -lev[:, 0].T)
    put("iota", np.broadcast_to(np.arange(32) - 64, (P, 32)))
    put("biota", np.broadcast_to(np.arange(NB_MAX), (P, NB_MAX)))
    put("pcol", np.arange(P))
    put("c128", np.broadcast_to(np.arange(8) * BLK, (P, 8)))
    return c


def host_rotary():
    inv = (np.float32(10000.0) ** (-np.arange(0, 64, 2, dtype=np.float32) / np.float32(64))).astype(np.float32)
    ang = np.arange(SEQ, dtype=np.float32)[:, None] * inv[None]
    cos, sin = np.cos(ang), np.sin(ang)
    return np.concatenate([cos, cos, -sin, sin], axis=1).astype(np.float32)


def bc(ap, n):
    return ap.unsqueeze(ap.ndim).to_broadcast(list(ap.shape) + [n])


def heads(ap, n):
    return ap.unsqueeze(1).to_broadcast([ap.shape[0], n, ap.shape[1]])


def build(nc, a, out, hn_d, h_d, y_d, slot_d):
    ctx = ExitStack()
    with ctx:
        def sb(name, shape, dt=F32):
            return ctx.enter_context(nc.sbuf_tensor(name, shape, dt))

        sems = {}

        def sem(name):
            if name not in sems:
                sems[name] = ctx.enter_context(nc.semaphore(name))
            return sems[name]

        C_AT, C_N = const_layout()
        cst = sb("cst", [P, C_N])

        def cn(name):
            o, w = C_AT[name]
            return cst[:, o:o + w]

        ident = cn("ident")
        g1c = sb("g1c", [P, KD])
        g2c = sb("g2c", [P, KD])
        gmc = sb("gmc", [P, KD])
        convw = sb("convw", [P, 4, 12])
        abrow = sb("abrow", [P, 8])
        lbc = sb("lbc", [P, 2])
        lbw = sb("lbw", [P, 4, 2])
        wr = sb("wr", [P, KD, 36])
        xin = sb("xin", [P, DM])
        junk = sb("junk", [P, DM])
        hbuf = sb("hbuf", [P, DM])
        sc = sb("sc", [P, 160])
        lg = sb("lg", [P, NT, 36])

        BIG_N = 45400
        big = sb("big", [P, BIG_N])
        used = [0]

        def part(n):
            o = used[0]
            used[0] += n
            assert used[0] <= BIG_N, used[0]
            return big[:, o:o + n]

        def three(ap, x, y):
            return ap.rearrange("p (a b) -> p a b", a=x, b=y)

        wg = [part(KD * 520) for _ in range(2)]
        wout = three(part(KD * DM), KD, DM)
        pj = part(IN_W)
        cb = three(part(12 * 131), 12, 131)
        cy = three(part(1536), 12, 128)
        ce = part(1536)
        xnT = three(part(1024), KD, P)
        gt = part(1024)
        rot = part(512)
        rtab = part(128)
        rqT = three(part(512), 4, P)
        rqX = three(part(256), 2, P)
        rkz = part(256)
        rA = three(part(512), 4, P)
        hatt = three(part(512), 4, P)
        SrB = three(part(256), 2, P)
        ShB = three(part(256), 2, P)
        S = three(part(512), 4, P)
        Dm, Dl, Dg, A, T, U, Zs, khat, khT, kb, kdec, vb, qkm = [three(part(512), 4, P) for _ in range(13)]
        gBr, nwT, vn = Zs, khT, Dm
        hr = part(512)
        he = part(512)
        hG = three(part(256), 2, P)
        hE = part(LEVELS * 256)
        hQ = part(LEVELS * 256)
        hqg = three(part(256), 2, P)
        hkd = three(part(256), 2, P)
        hkT = part(256)
        obuf = part(1024)
        hnb = part(1024)
        rtmp = three(hQ[:, 1024:1536], 4, P)
        mT = three(hE[:, 0:1024], KD, P)
        mix_used = used[0]
        used[0] = 0
        wexp = [[three(part(4096), KD, DE), three(part(4096), KD, DE), three(part(4096), KE, DM)] for _ in range(2)]
        xg = [part(DM) for _ in range(2)]
        xT = three(part(DM), KD, P)
        eg = part(DE)
        hact = part(DE)
        hT = three(part(DE), KE, P)
        yo = [part(DM) for _ in range(2)]
        moe_used = used[0]
        el, oh1, oh2, cnd, rk = [three(part(256), NT, 32) for _ in range(5)]
        goh, gex = [three(part(NGRP * NT), NT, NGRP) for _ in range(2)]
        gm, m1, m2_, e2, ri = [part(NT) for _ in range(5)]
        cnt, nblk, incl, base = [part(NE) for _ in range(4)]
        cmp_ = part(NB_MAX * 32)
        used[0] = 0
        cm_y1 = [part(DM) for _ in range(2)]
        cm_y2 = [part(DM) for _ in range(2)]
        cm_h = [part(DM) for _ in range(2)]
        cm_o = [part(DM) for _ in range(2)]
        fgain = part(DM)
        mrun = sb("mrun", [P, NT + 1, 32])
        w12 = sb("w12", [P, 2, NT])
        dst = sb("dst", [P, 2, NT])
        dsti = sb("dsti", [P, 2, NT], I32)
        toki = sb("toki", [P, NT], I32)
        blkt = sb("blkt", [P, NB_MAX + 2])
        blki = sb("blki", [P, NB_MAX + 2], I32)
        slots = sb("slots", [P, NB_MAX], I32)
        zrow = mrun[:, 0:NT, :].rearrange("p a b -> p (a b)")
        idxs = [sb(f"idx{k}", [P, 1], I32) for k in range(2)]

        ps = [ctx.enter_context(nc.psum_tensor(f"ps{k}", [P, 512], F32)) for k in range(8)]

        def b4(k):
            return ps[k][:, :].rearrange("p (a b) -> p a b", a=4)

        ssx, mx, rx, tx_ = [sc[:, k:k + 1] for k in range(4)]
        dax, dae, dl, gcol, beta, gc, eG, eGL, ekd, bG, dxx = [sc[:, 8 + 4 * k:12 + 4 * k] for k in range(11)]
        mqk, rqk, tqk = [sc[:, 56 + 8 * k:64 + 8 * k] for k in range(3)]
        mh, rh, th_, sh = [sc[:, 80 + 16 * k:96 + 16 * k] for k in range(4)]
        ehGL = sc[:, 144:146]
        ss2, m2, r2, t2 = [sc[:, 150 + k:151 + k] for k in range(4)]
        sg4 = sc[:, 154:158]
        negA, lbv, oml = lbw[:, 0:2, :].rearrange("p a b -> p (a b)"), lbw[:, 2, :], lbw[:, 3, :]
        lbt = sb("lbt", [P, 4, 2])

        w_view = a["w_in"][0].rearrange("(k p) n -> p k n", p=P)
        x_view = a["x"][0].rearrange("(t p) d -> t p d", p=P)
        hn_v = hn_d.rearrange("(t p) d -> t p d", p=P)
        h_v = h_d.rearrange("(t p) d -> t p d", p=P)
        out_v = out[0].rearrange("(t p) d -> t p d", p=P)
        rot_v = a["rotary"].rearrange("(t p) d -> t p d", p=P)

        PER = {"proj_filled": NG, "proj_copied": NG, "x_loaded": 16, "xres_loaded": 16, "rot_loaded": 16,
               "hn_stored": 32, "UT": LEVELS, "Z": LEVELS - 1, "Zs": LEVELS - 1, "dU": LEVELS - 1,
               "dT": LEVELS - 2, "tconv": 3, "tm": 2, "t2": 2, "tx": 2, "hA": 4, "hatt": 4}

        def at(name, i, k=None):
            per = PER.get(name, 1)
            return i * per + (per if k is None else k)

        class Engine:

            def __init__(self, eng, chain, per):
                self.eng, self.chain, self.per, self.c, self.base = eng, chain, per, 0, 0

            def wait(self, name, i, k=None):
                self.eng.wait_ge(sem(name), at(name, i, k))

            def link(self, ins):
                self.c += 1
                ins.then_inc(sem(self.chain), 1)
                self.eng.wait_ge(sem(self.chain), self.base + self.c)

            def start(self, base):
                self.c, self.base = 0, base

            def end(self):
                assert self.c == self.per, (self.chain, self.c)

        N_PARAMS = 16 * 18
        DVE_LINKS, ACT_LINKS = 62, 5
        block = ctx.enter_context(nc.Block())

        @block.sync
        def _(sp):
            loads = [0]

            def ld(dst_, src):
                loads[0] += 16
                sp.dma_start(dst_, src).then_inc(sem("params_loaded"), 16)

            ld(cst[:, :], a["consts"])
            sp.dma_start(xin[:, :], x_view[0]).then_inc(sem("x_loaded"), 16)
            with nc.allow_non_contiguous_dma(reason="small parameter vectors"):
                ld(g1c[:, :], a["attn_norm"][0].rearrange("(k p) -> p k", p=P))
                ld(g2c[:, :], a["ffn_norm"][0].rearrange("(k p) -> p k", p=P))
                ld(gmc[:, 0:2], a["ret_norm"][0].rearrange("(k p) -> p k", p=P))
                gd = a["gdn_norm"][0].rearrange("(p o) -> p o", o=1)
                for h in range(4):
                    ld(gmc[:, 2 + h:3 + h], gd)
                ld(gmc[:, 6:8], a["hgrn_norm"][0].rearrange("(k p) -> p k", p=P))
                ld(lbc[:, :], a["hgrn_lower_bounds"][0].rearrange("(k p) -> p k", p=P))
                for j in range(4):
                    ld(convw[:, j, :], a["gdn_conv"][0, j].rearrange("(k p) -> p k", p=P))
                ld(abrow[:, 0:4], a["gdn_a_log"].to_broadcast([P, 4]))
                ld(abrow[:, 4:8], a["gdn_dt_bias"].to_broadcast([P, 4]))
                ld(wr[:, :, 0:4], a["router_group"][0].rearrange("(k p) n -> p k n", p=P))
            ld(wr[:, :, 4:36], a["router_expert"][0].rearrange("(k p) n -> p k n", p=P))
            assert loads[0] == N_PARAMS, loads[0]

            def load_w(t, n, nxt):
                if nxt or n >= 2:
                    sp.wait_ge(sem("proj_filled"), at("proj_filled", t, n - 1))
                c0, extra = GROUPS[n]
                w = GW + extra
                sp.dma_start(three(wg[n % 2][:, 0:KD * w], KD, w), w_view[:, :, c0:c0 + w]) \
                    .then_inc(sem(f"w_in_loaded{n % 2}"), 16)

            def tile_steps(i, nxt):
                if nxt:
                    sp.wait_ge(sem("xsc"), i + 1)
                    sp.dma_start(xin[:, :], x_view[i + 1]).then_inc(sem("x_loaded"), 16)
                    sp.wait_ge(sem("rot"), i + 1)
                    sp.dma_start(rtab, rot_v[i + 1]).then_inc(sem("rot_loaded"), 16)
                sp.wait_ge(sem("hbuf_free"), i + 1)
                sp.dma_start(hbuf[:, :], x_view[i]).then_inc(sem("xres_loaded"), 16)
                if nxt:
                    for n in range(NG):
                        load_w(i + 1, n, True)
                sp.wait_ge(sem("h_ready"), i + 1)
                sp.dma_start(h_v[i], hbuf[:, :]).then_inc(sem("hn_stored"), 16)
                sp.wait_ge(sem("hn_ready"), i + 1)
                sp.dma_start(hn_v[i], hnb).then_inc(sem("hn_stored"), 16)
                sp.wait_ge(sem("hn_stored"), at("hn_stored", i))
                sp.sem_inc(sem("hbuf_free"), 1)

            for n in range(NG):
                load_w(0, n, False)
                if n == 3:
                    sp.dma_start(wout, a["w_out"][0].rearrange("(k p) n -> p k n", p=P)) \
                        .then_inc(sem("w_out_loaded"), 16)
            sp.dma_start(rtab, rot_v[0]).then_inc(sem("rot_loaded"), 16)
            sp.sem_inc(sem("hbuf_free"), 1)
            with sp.Fori(0, NT - 1) as i:
                tile_steps(i, True)
            tile_steps(NT - 1, False)

            sp.wait_ge(sem("logits"), NT)
            sp.wait_ge(sem("blk_ready"), 1)
            pairs = sp.value_load(blki[0:1, NB_MAX:NB_MAX + 1], min_val=NB_MIN // 2, max_val=NB_MAX // 2)

            def load_expert(b, par, first):
                e = sp.value_load(blki[0:1, bass.ds(b, 1)], min_val=0, max_val=NE - 1)
                if not first:
                    sp.wait_ge(sem("gu_done"), b - 1)
                for m, name in enumerate(("w_gate", "w_up")):
                    sp.dma_start(wexp[par][m], a[name][0, e].rearrange("(k p) n -> p k n", p=P)) \
                        .then_inc(sem(f"gu_loaded{par}"), 16)
                if not first:
                    sp.wait_ge(sem("down_done"), b - 1)
                sp.dma_start(wexp[par][2], a["w_down"][0, e].rearrange("(k p) n -> p k n", p=P)) \
                    .then_inc(sem(f"down_loaded{par}"), 16)

            load_expert(0, 0, True)
            load_expert(1, 1, True)
            with sp.Fori(1, pairs) as q:
                load_expert(2 * q, 0, False)
                load_expert(2 * q + 1, 1, False)

            sp.wait_ge(sem("y_stored0"), pairs * 16 + 16)
            sp.wait_ge(sem("y_stored1"), pairs * 16 + 16)
            sp.dma_start(fgain, a["final_norm"].partition_broadcast(P)).then_inc(sem("fgain_loaded"), 16)
            for t in range(NT):
                if t >= 2:
                    sp.wait_ge(sem("c_sum"), t - 1)
                sp.dma_start(cm_h[t % 2], h_v[t]).then_inc(sem(f"ch_loaded{t % 2}"), 16)

        @block.tensor
        def _(pe):
            t_ = nc.tensor
            E = Engine(pe, "pe_chain", 0)

            def transposes(bank, blocks, name):
                for k, blk in enumerate(blocks):
                    last = t_.transpose(ps[bank][:, k * P:(k + 1) * P], blk, ident)
                last.then_inc(sem(name), 1)

            def each_head(bank, lhs, rhs, name):
                for h in range(4):
                    last = t_.matmul(b4(bank)[:, h, :], lhs[:, h, :], rhs[:, h, :], start=True, stop=True)
                last.then_inc(sem(name), 1)

            def cols(ap, k0, n):
                return [ap[:, k * P:(k + 1) * P] for k in range(k0, k0 + n)]

            def x_transposes(t):
                E.wait("xsc", t)
                transposes(6, cols(junk, 0, 4), "tx")
                transposes(7, cols(junk, 4, 4), "tx")

            def project(t, n, nxt):
                c0, extra = GROUPS[n]
                w = GW + extra
                if n == 0:
                    E.wait("xnT", t)
                pe.wait_ge(sem(f"w_in_loaded{n % 2}"), t * 64 + 16 * (n // 2 + 1))
                if nxt or n >= 2:
                    E.wait("proj_copied", t, n - 1)
                wv = three(wg[n % 2][:, 0:KD * w], KD, w)
                if extra:
                    for k in range(KD):
                        last = t_.matmul(ps[3][:, 0:8], xnT[:, k, :], wv[:, k, 0:8], start=k == 0, stop=k == KD - 1)
                    last.then_inc(sem("ab_filled"), 1)
                for k in range(KD):
                    last = t_.matmul(ps[6 + n % 2][:, :], xnT[:, k, :], wv[:, k, extra:w], start=k == 0,
                                     stop=k == KD - 1)
                last.then_inc(sem("proj_filled"), 1)

            def two_heads_out(bank, qx, Sx, att, v0):
                for j in range(2):
                    t_.matmul(ps[bank][:, j * P:(j + 1) * P], qx[:, j, :], Sx[:, j, :], start=True, stop=False)
                    for q in range(2):
                        c = v0 + P * j + 64 * q
                        t_.matmul(ps[bank][:, j * P + 64 * q:j * P + 64 * q + 64], att[:, 2 * q + j, :],
                                  pj[:, c:c + 64], start=False, stop=q == 1)

            def mixer(i, nxt):
                def group(n):
                    if nxt:
                        project(i + 1, n, True)

                E.wait("proj_copied", i)
                transposes(0, cols(pj, C_DQ // P, 4), "tconv")
                transposes(1, cols(pj, C_DQ // P + 4, 4), "tconv")
                transposes(2, cols(pj, C_DQ // P + 8, 4), "tconv")
                transposes(3, [pj[:, C_HQ + k * P:C_HQ + (k + 1) * P] for k in range(4)], "th")
                E.wait("rot", i)
                transposes(4, cols(rot, 0, 4), "tr")
                if nxt:
                    x_transposes(i + 1)
                E.wait("cb_in", i)
                E.wait("gBr", i)
                for h in range(4):
                    last = t_.matmul(b4(0)[:, h, :], gBr[:, h, :], cn("tri"), start=True, stop=True)
                t_.matmul(ps[5][:, 0:4], cn("tri"), gcol, start=True, stop=True).then_inc(sem("Gsum"), 1)
                E.wait("rqT", i)
                for q in range(2):
                    for j in range(2):
                        last = t_.matmul(ps[1 + q][:, j * P:(j + 1) * P], rqT[64 * q:64 * q + 64, 2 + j, :],
                                         rqT[64 * q:64 * q + 64, j, :], start=True, stop=True)
                last.then_inc(sem("rS"), 1)
                group(0)
                group(1)
                E.wait("cs", i)
                E.wait("hraw", i)
                transposes(3, [cy[:, 4 + k, :] for k in range(4)], "ktok")
                transposes(4, [cy[:, 8 + k, :] for k in range(4)], "vtok")
                E.wait("csq", i)
                cq = ce[:, 0:1024].rearrange("p (a b) -> p a b", a=8)
                for h in range(8):
                    last = t_.matmul(ps[5][:, 8 + h:9 + h], cq[:, h, :], cn("ones")[:, 0:1], start=True, stop=True)
                last.then_inc(sem("ssq"), 1)
                E.wait("rA", i)
                E.wait("rqX", i)
                two_heads_out(1, rqX, SrB, rA, C_RV)
                for j in range(2):
                    last = t_.matmul(ps[2][:, j * P:(j + 1) * P], rkz[:, j * P:(j + 1) * P],
                                     pj[:, C_RV + P * j:C_RV + P * j + P], start=True, stop=True)
                last.then_inc(sem("rOU"), 1)
                group(2)
                E.wait("khat", i)
                transposes(3, [khat[:, h, :] for h in range(4)], "tkh")
                group(3)
                E.wait("khT", i)
                E.wait("vb", i)
                each_head(4, khT, khT, "kk")
                E.wait("gam", i)
                each_head(0, khT, cy, "qk")
                E.wait("A", i)
                transposes(3, [A[:, h, :] for h in range(4)], "tA")
                for l in range(1, LEVELS):
                    E.wait("UT", i, l)
                    each_head(0, A, U, "Z")
                    if l <= 4:
                        E.wait("hKQ" if l == 1 else "hatt", i, max(l - 1, 1))
                        if l == 1:
                            E.wait("r_out", i)
                        for q in range(2):
                            rows = slice(64 * q, 64 * q + 64)
                            for m in range(2):
                                lev = 2 * (l - 1) + m
                                for j in range(2):
                                    o = (2 * lev + j) * P
                                    if lev < LEVELS:
                                        kq, qq = hE[rows, o:o + P], hQ[rows, o:o + P]
                                    else:
                                        kq, qq = he[rows, 256 + j * P:384 + j * P], hr[rows, j * P:(j + 1) * P]
                                    last = t_.matmul(ps[1 + q][:, (2 * m + j) * P:(2 * m + j + 1) * P], kq, qq,
                                                     start=True, stop=True)
                        last.then_inc(sem("hA"), 1)
                    if l == 2:
                        group(4)
                    if l == 4:
                        group(5)
                    if l == 5:
                        if nxt:
                            E.wait("proj_copied", i + 1, 6)
                        transposes(3, [hkd[:, j, :] for j in range(2)], "thk")
                    if l == 6:
                        E.wait("hatt", i, 4)
                        two_heads_out(1, hqg, ShB, hatt, C_HI)
                        E.wait("hkT", i)
                        for j in range(2):
                            last = t_.matmul(ps[2][:, j * P:(j + 1) * P], hkT[:, j * P:(j + 1) * P],
                                             pj[:, C_HI + P * j:C_HI + P * j + P], start=True, stop=True)
                        last.then_inc(sem("hOU"), 1)
                    E.wait("Zs", i, l)
                    each_head(4, T, Zs, "dU")
                    if l < LEVELS - 1:
                        each_head(5, Zs, T, "dT")
                E.wait("UT", i, LEVELS)
                each_head(0, kb, U, "wT")
                group(6)
                E.wait("nwT", i)
                for h in range(4):
                    t_.matmul(b4(4)[:, h, :], U[:, h, :], vb[:, h, :], start=True, stop=False)
                    last = t_.matmul(b4(4)[:, h, :], nwT[:, h, :], S[:, h, :], start=False, stop=True)
                last.then_inc(sem("vnew"), 1)
                each_head(5, cy, S, "o1")
                E.wait("vn", i)
                each_head(0, qkm, vn, "o2")
                each_head(3, kdec, vn, "dS")
                group(7)
                E.wait("mixed", i)
                transposes(1, cols(obuf, 0, 4), "tm")
                transposes(2, cols(obuf, 4, 4), "tm")
                E.wait("mT", i)
                for n in range(2):
                    for k in range(KD):
                        last = t_.matmul(ps[4 + n][:, :], mT[:, k, :], wout[:, k, n * 512:(n + 1) * 512],
                                         start=k == 0, stop=k == KD - 1)
                last.then_inc(sem("wo"), 1)
                E.wait("hn_ready", i)
                transposes(0, cols(hnb, 0, 4), "t2")
                transposes(3, cols(hnb, 4, 4), "t2")
                E.wait("h2T", i)
                for k in range(KD):
                    last = t_.matmul(ps[5][:, 32:68], mT[:, k, :], wr[:, k, :], start=k == 0, stop=k == KD - 1)
                last.then_inc(sem("rt"), 1)

            pe.wait_ge(sem("params_loaded"), N_PARAMS)
            x_transposes(0)
            for n in range(NG):
                project(0, n, False)
            pe.wait_ge(sem("w_out_loaded"), 16)
            pe.wait_ge(sem("zeroed"), 1)
            with pe.Fori(0, NT - 1) as i:
                mixer(i, True)
            mixer(NT - 1, False)

            pe.wait_ge(sem("picked"), 1)
            t_.matmul(ps[0][:, 0:256], cn("stri"), cnd, start=True, stop=False)
            t_.matmul(ps[0][:, 0:256], cn("ones"), mrun[:, 0:NT, :], start=False, stop=True)
            t_.matmul(ps[1][:, 0:32], cn("ones"), mrun[:, NT, :], start=True, stop=True).then_inc(sem("ranks"), 1)

            pe.wait_ge(sem("blk_ready"), 1)
            pairs = pe.value_load(blki[0:1, NB_MAX:NB_MAX + 1], min_val=NB_MIN // 2, max_val=NB_MAX // 2)
            last_pair = pe.value_load(blki[0:1, NB_MAX + 1:NB_MAX + 2], min_val=NB_MIN // 2 - 1,
                                      max_val=NB_MAX // 2 - 1)

            def x_block(b, q, par):
                pe.wait_ge(sem(f"tok_loaded{par}"), q * 16 + 16)
                for k in range(KD):
                    last = t_.transpose(ps[k // 4][:, (k % 4) * P:(k % 4 + 1) * P], xg[par][:, k * P:(k + 1) * P],
                                        ident)
                last.then_inc(sem("xt_done"), 1)

            def gate_up(b, q, par):
                pe.wait_ge(sem("xT_ready"), b + 1)
                pe.wait_ge(sem(f"gu_loaded{par}"), q * 32 + 32)
                for m, name in enumerate(("g_done", "gu_done")):
                    for k in range(KD):
                        last = t_.matmul(ps[2 + m][:, :], xT[:, k, :], wexp[par][m][:, k, :], start=k == 0,
                                         stop=k == KD - 1)
                    last.then_inc(sem(name), 1)

            def h_block(b):
                pe.wait_ge(sem("hact_ready"), b + 1)
                for k in range(KE):
                    last = t_.transpose(ps[4][:, k * P:(k + 1) * P], hact[:, k * P:(k + 1) * P], ident)
                last.then_inc(sem("ht_done"), 1)

            def down(b, q, par):
                pe.wait_ge(sem("hT_ready"), b + 1)
                pe.wait_ge(sem(f"down_loaded{par}"), q * 16 + 16)
                for n in range(2):
                    for k in range(KE):
                        last = t_.matmul(ps[5 + n][:, :], hT[:, k, :], wexp[par][2][:, k, n * 512:(n + 1) * 512],
                                         start=k == 0, stop=k == KE - 1)
                last.then_inc(sem("down_done"), 1)

            x_block(0, 0, 0)
            gate_up(0, 0, 0)
            x_block(1, 0, 1)
            h_block(0)
            with pe.Fori(1, pairs) as q:
                gate_up(2 * q - 1, q - 1, 1)
                x_block(2 * q, q, 0)
                down(2 * q - 2, q - 1, 0)
                h_block(2 * q - 1)
                gate_up(2 * q, q, 0)
                x_block(2 * q + 1, q, 1)
                pe.wait_ge(sem("y0_ready"), 2 * q - 1)
                pe.wait_ge(sem("y1_ready"), 2 * q - 1)
                down(2 * q - 1, q - 1, 1)
                pe.wait_ge(sem("y0_ready"), 2 * q)
                pe.wait_ge(sem("y1_ready"), 2 * q)
                h_block(2 * q)
            gate_up(last_pair * 2 + 1, last_pair, 1)
            down(last_pair * 2, last_pair, 0)
            h_block(last_pair * 2 + 1)
            pe.wait_ge(sem("y0_ready"), last_pair * 2 + 1)
            pe.wait_ge(sem("y1_ready"), last_pair * 2 + 1)
            down(last_pair * 2 + 1, last_pair, 1)

        @block.scalar
        def _(act):
            s = nc.scalar
            E = Engine(act, "act_chain", ACT_LINKS)

            def rsqrt_start(m, y, name, done, i):
                E.wait(name, i)
                E.link(s.activation(y, m, ACT.Ln))
                s.activation(y, y, ACT.Exp, scale=-0.5).then_inc(sem(done), 1)

            def x_square(t, nxt):
                if nxt:
                    E.wait("tx", t - 1)
                E.wait("x_loaded", t)
                s.activation(junk[:, :], xin[:, :], ACT.Square, accum_out=ssx).then_inc(sem("x_sq"), 1)

            def copy_group(t, n):
                c0, extra = GROUPS[n]
                E.wait("proj_filled", t, n + 1)
                if extra:
                    E.wait("ab_filled", t)
                    s.activation(pj[:, c0:c0 + extra], ps[3][:, 0:extra], ACT.Copy)
                s.activation(pj[:, c0 + extra:c0 + extra + GW], ps[6 + n % 2][:, :], ACT.Copy) \
                    .then_inc(sem("proj_copied"), 1)

            def mixer(i, nxt):
                def group(n):
                    if nxt:
                        copy_group(i + 1, n)

                if nxt:
                    x_square(i + 1, True)
                E.wait("hist", i)
                for k in range(3):
                    E.wait("tconv", i, k + 1)
                    last = s.activation(cb[:, 4 * k:4 * k + 4, 3:131], b4(k), ACT.Copy)
                last.then_inc(sem("cb_in"), 1)
                E.wait("dax", i)
                E.link(s.activation(dae, dax, ACT.Exp, scale=-1.0))
                s.activation(dl, dae, ACT.Ln, bias=1.0)
                s.activation(beta, pj[:, C_DB:C_DB + 4], ACT.Exp, scale=-1.0).then_inc(sem("dl"), 1)
                if nxt:
                    rsqrt_start(mx, rx, "x_m", "x_y0", i + 1)
                E.wait("th", i)
                s.activation(he, ps[3][:, :], ACT.Exp, scale=-1.0)
                s.activation(hr, ps[3][:, :], ACT.Copy).then_inc(sem("hraw"), 1)
                E.wait("tr", i)
                s.activation(rqT, b4(4), ACT.Copy).then_inc(sem("rqT"), 1)
                s.activation(gt[:, 0:256], pj[:, C_RG:C_RG + 256], ACT.Exp, scale=-1.0)
                s.activation(gt[:, 256:768], pj[:, C_DZ:C_DZ + 512], ACT.Exp, scale=-1.0)
                s.activation(gt[:, 768:1024], pj[:, C_HG:C_HG + 256], ACT.Exp, scale=-1.0).then_inc(sem("gexp"), 1)
                E.wait("cy", i)
                s.activation(ce, cy, ACT.Exp, scale=-1.0).then_inc(sem("cexp"), 1)
                E.wait("Dg", i)
                s.activation(Dl, Dl, ACT.Exp)
                s.activation(Dg, Dg, ACT.Exp, scale=-1.0)
                s.activation(eG, gc, ACT.Exp)
                s.activation(ekd, Dm[:, :, P - 1], ACT.Exp)
                s.activation(eGL, b4(0)[:, :, P - 1], ACT.Exp).then_inc(sem("gam"), 1)
                group(0)
                group(1)
                E.wait("cs", i)
                s.activation(ce[:, 0:1024], cy[:, 0:8, :], ACT.Square).then_inc(sem("csq"), 1)
                E.wait("hf", i)
                s.activation(he[:, 0:256], hr[:, 256:512], ACT.Ln).then_inc(sem("hln"), 1)
                rsqrt_start(mqk, rqk, "mqk", "qk_y0", i)
                E.wait("hlev", i)
                s.activation(hE, hE, ACT.Exp)
                s.activation(hqg, hG, ACT.Exp)
                for j in range(2):
                    s.activation(hkd[:, j, :], hG[:, j, :], ACT.Exp, scale=-1.0, bias=hG[:, j, P - 1:P])
                s.activation(ehGL, hG[:, :, P - 1], ACT.Exp).then_inc(sem("hexp"), 1)
                E.wait("rOU", i)
                s.activation(obuf[:, 0:256], ps[1][:, 0:256], ACT.Copy).then_inc(sem("r_out"), 1)
                group(2)
                E.wait("tkh", i)
                s.activation(khT, b4(3), ACT.Copy).then_inc(sem("khT"), 1)
                group(3)
                if nxt:
                    E.wait("rot", i)
                group(4)
                if nxt:
                    E.wait("gate", i)
                group(5)
                E.wait("thk", i)
                s.activation(hkT, ps[3][:, 0:256], ACT.Copy).then_inc(sem("hkT"), 1)
                E.wait("hOU", i)
                s.activation(obuf[:, 768:1024], ps[1][:, 0:256], ACT.Copy).then_inc(sem("h_out"), 1)
                E.wait("wT", i)
                s.activation(nwT, b4(0), ACT.Copy, scale=-1.0).then_inc(sem("nwT"), 1)
                group(6)
                E.wait("vnew", i)
                s.activation(vn, b4(4), ACT.Copy).then_inc(sem("vn"), 1)
                group(7)
                E.wait("od", i)
                s.activation(hQ[:, 0:1024], obuf, ACT.Square).then_inc(sem("o_sq"), 1)
                rsqrt_start(mh, rh, "mh", "h_y0", i)
                E.wait("h_ready", i)
                s.activation(hnb, hbuf[:, :], ACT.Square, accum_out=ss2).then_inc(sem("h_sq"), 1)
                rsqrt_start(m2, r2, "m2", "n_y0", i)
                E.wait("rt", i)
                s.activation(lg[:, i, :], ps[5][:, 32:68], ACT.Copy).then_inc(sem("logits"), 1)

            act.wait_ge(sem("params_loaded"), N_PARAMS)
            act.wait_ge(sem("lb_shifted"), 1)
            s.activation(lbt[:, 1, :], lbt[:, 0, :], ACT.Exp)
            s.activation(negA, abrow[:, 0:4], ACT.Exp).then_inc(sem("param_exp"), 1)
            x_square(0, False)
            rsqrt_start(mx, rx, "x_m", "x_y0", 0)
            for n in range(NG):
                copy_group(0, n)
            with act.Fori(0, NT - 1) as i:
                E.start(i * ACT_LINKS + 1)
                mixer(i, True)
                E.end()
            E.start((NT - 1) * ACT_LINKS + 1)
            mixer(NT - 1, False)

            act.wait_ge(sem("r_shift"), 1)
            s.activation(gex, gex, ACT.Exp)
            s.activation(e2, e2, ACT.Exp).then_inc(sem("r_exp"), 1)

            act.wait_ge(sem("y_zeroed"), 64)
            act.wait_ge(sem("blk_ready"), 1)
            pairs = act.value_load(blki[0:1, NB_MAX:NB_MAX + 1], min_val=NB_MIN // 2, max_val=NB_MAX // 2)
            last_pair = act.value_load(blki[0:1, NB_MAX + 1:NB_MAX + 2], min_val=NB_MIN // 2 - 1,
                                      max_val=NB_MAX // 2 - 1)
            act.sem_inc(sem("y_stored0"), 16)
            act.sem_inc(sem("y_stored1"), 16)

            def silu_exp(b):
                act.wait_ge(sem("g_done"), b + 1)
                s.activation(eg, ps[2][:, :], ACT.Exp, scale=-1.0).then_inc(sem("eg"), 1)

            def h_copy(b):
                act.wait_ge(sem("ht_done"), b + 1)
                s.activation(hT, b4(4), ACT.Copy).then_inc(sem("hT_ready"), 1)

            def y_left(b, q, par):
                act.wait_ge(sem("down_done"), b + 1)
                act.wait_ge(sem(f"y_stored{par}"), q * 16 + 16)
                s.activation(yo[par][:, 0:512], ps[5][:, :], ACT.Copy).then_inc(sem("y0_ready"), 1)

            def y_store(b, par):
                act.wait_ge(sem("y0_ready"), b + 1)
                act.wait_ge(sem("y1_ready"), b + 1)
                act.dma_start(y_d[bass.ds(b * BLK, BLK), :], yo[par]).then_inc(sem(f"y_stored{par}"), 16)

            silu_exp(0)
            h_copy(0)
            with act.Fori(1, pairs) as q:
                silu_exp(2 * q - 1)
                y_left(2 * q - 2, q - 1, 0)
                h_copy(2 * q - 1)
                y_store(2 * q - 2, 0)
                silu_exp(2 * q)
                y_left(2 * q - 1, q - 1, 1)
                h_copy(2 * q)
                y_store(2 * q - 1, 1)
            silu_exp(last_pair * 2 + 1)
            y_left(last_pair * 2, last_pair, 0)
            h_copy(last_pair * 2 + 1)
            y_store(last_pair * 2, 0)
            y_left(last_pair * 2 + 1, last_pair, 1)
            y_store(last_pair * 2 + 1, 1)

            for t in range(NT):
                act.wait_ge(sem("c_sum"), t + 1)
                s.activation(cm_y1[t % 2], cm_o[t % 2], ACT.Square, accum_out=ssx).then_inc(sem("c_sq"), 1)
                act.wait_ge(sem("c_m"), t + 1)
                s.activation(rx, mx, ACT.Ln).then_inc(sem("c_root"), 1)
                act.wait_ge(sem("c_root"), 2 * t + 1)
                s.activation(rx, rx, ACT.Exp, scale=-0.5).then_inc(sem("c_root"), 1)
                act.wait_ge(sem("c_out"), t + 1)
                act.dma_start(out_v[t], cm_o[t % 2]).then_inc(sem(f"out_stored{t % 2}"), 16)
            for par in range(2):
                act.wait_ge(sem(f"out_stored{par}"), 16 * (NT // 2))

        @block.vector
        def _(dve):
            v = nc.vector
            E = Engine(dve, "dve_chain", DVE_LINKS)
            link = E.link

            def tt(o, x, y, op):
                return v.tensor_tensor(o, x, y, op)

            def refine(m, y, tmp, name, i):
                E.wait(name, i)
                link(tt(tmp, y, y, ALU.mult))
                link(tt(tmp, tmp, m, ALU.mult))
                link(v.tensor_scalar(tmp, tmp, -0.5, 1.5, ALU.mult, ALU.add))
                return tt(y, y, tmp, ALU.mult)

            def x_mean(t):
                E.wait("x_sq", t)
                v.tensor_scalar(mx, ssx, 1.0 / DM, EPS, ALU.mult, ALU.add).then_inc(sem("x_m"), 1)

            def x_scale(t):
                link(refine(mx, rx, tx_, "x_y0", t))
                v.tensor_scalar(junk[:, :], xin[:, :], rx, None, ALU.mult).then_inc(sem("xsc"), 1)

            def x_gain(t):
                E.wait("tx", t)
                tt(xnT[:, 0:4, :], b4(6), bc(g1c[:, 0:4], P), ALU.mult)
                tt(xnT[:, 4:8, :], b4(7), bc(g1c[:, 4:8], P), ALU.mult).then_inc(sem("xnT"), 1)

            def mixer(i, nxt):
                E.wait("proj_copied", i)
                da = pj[:, C_DA:C_DA + 4]
                link(tt(dxx, da, abrow[:, 4:8], ALU.add))
                v.scalar_tensor_tensor(dax, dxx, -1.0, dxx, ALU.mult, ALU.max).then_inc(sem("dax"), 1)
                if nxt:
                    x_mean(i + 1)
                E.wait("rot_loaded", i)
                qk = pj[:, 0:512].rearrange("p (h d) -> p h d", h=8)
                ro = rot.rearrange("p (h d) -> p h d", h=8)
                rt = rtmp.rearrange("p a b -> p (a b)").rearrange("p (h d) -> p h d", h=8)
                tt(ro, qk, heads(rtab[:, 0:64], 8), ALU.mult)
                tt(rt[:, :, 0:32], qk[:, :, 32:64], heads(rtab[:, 64:96], 8), ALU.mult)
                link(tt(rt[:, :, 32:64], qk[:, :, 0:32], heads(rtab[:, 96:128], 8), ALU.mult))
                tt(ro, ro, rt, ALU.add).then_inc(sem("rot"), 1)
                E.wait("dl", i)
                link(v.scalar_tensor_tensor(dl, dxx, 0.0, dl, ALU.max, ALU.add))
                link(tt(gcol, dl, negA, ALU.mult))
                v.tensor_copy(gBr, bc(gcol, P)).then_inc(sem("gBr"), 1)
                link(v.tensor_scalar(beta, beta, 1.0, None, ALU.add))
                link(v.reciprocal(beta, beta))
                if nxt:
                    x_scale(i + 1)
                E.wait("rot", i)
                tt(rkz, rot[:, 256:512], cn("zeta"), ALU.mult)
                E.wait("cb_in", i)
                for j in range(4):
                    for k in range(12):
                        if j == 0:
                            last = v.tensor_scalar(cy[:, k, :], cb[:, k, 0:P], convw[:, 0, k:k + 1], None, ALU.mult)
                        else:
                            last = v.scalar_tensor_tensor(cy[:, k, :], cb[:, k, j:j + P], convw[:, j, k:k + 1],
                                                          cy[:, k, :], ALU.mult, ALU.add)
                    if j < 3:
                        link(last)
                last.then_inc(sem("cy"), 1)
                v.tensor_copy(cb[:, :, 0:3], cb[:, :, 128:131]).then_inc(sem("hist"), 1)
                if nxt:
                    x_gain(i + 1)
                E.wait("Gsum", i)
                link(v.tensor_copy(gc, ps[5][:, 0:4]))
                link(tt(Dm, b4(0), bc(gc, P), ALU.subtract))
                link(v.tensor_scalar(Dl, Dm, 0.0, None, ALU.min))
                tt(Dl, Dl, heads(cn("neg_up"), 4), ALU.add)
                link(v.tensor_scalar(Dg, Dm, 0.0, None, ALU.max))
                tt(Dg, Dg, heads(cn("pos_low"), 4), ALU.add).then_inc(sem("Dg"), 1)
                E.wait("rqT", i)
                tt(rqX, rqT[:, 0:2, :], three(cn("xi"), 2, P), ALU.mult).then_inc(sem("rqX"), 1)
                E.wait("rS", i)
                for q in range(2):
                    last = tt(rA[:, 2 * q:2 * q + 2, :], three(ps[1 + q][:, 0:256], 2, P),
                              three(cn("dmat")[:, 256 * q:256 * q + 256], 2, P), ALU.mult)
                last.then_inc(sem("rA"), 1)
                E.wait("cexp", i)
                cyf = cy.rearrange("p a b -> p (a b)")
                link(v.tensor_scalar(ce, ce, 1.0, None, ALU.add))
                link(v.reciprocal(ce, ce))
                tt(cyf, cyf, ce, ALU.mult).then_inc(sem("cs"), 1)
                E.wait("hraw", i)
                link(v.tensor_scalar(he, he, 1.0, None, ALU.add))
                link(v.reciprocal(he, he))
                for j in range(2):
                    last = v.tensor_scalar(hr[:, 256 + P * j:384 + P * j], he[:, 256 + P * j:384 + P * j],
                                           oml[:, j:j + 1], lbv[:, j:j + 1], ALU.mult, ALU.add)
                link(last)
                tt(hr[:, 0:256], hr[:, 0:256], he[:, 0:256], ALU.mult)
                link(v.tensor_scalar(he[:, 256:512], hr[:, 256:512], -1.0, 1.0, ALU.mult, ALU.add))
                v.tensor_scalar(hr[:, 256:512], hr[:, 256:512], 2.0 ** -64, None, ALU.max).then_inc(sem("hf"), 1)
                E.wait("gexp", i)
                link(v.tensor_scalar(gt, gt, 1.0, None, ALU.add))
                link(v.reciprocal(gt, gt))
                tt(gt[:, 0:256], gt[:, 0:256], pj[:, C_RG:C_RG + 256], ALU.mult)
                tt(gt[:, 256:768], gt[:, 256:768], pj[:, C_DZ:C_DZ + 512], ALU.mult)
                tt(gt[:, 768:1024], gt[:, 768:1024], pj[:, C_HG:C_HG + 256], ALU.mult).then_inc(sem("gate"), 1)
                v.memset(hatt, 0.0)
                E.wait("ssq", i)
                v.tensor_scalar(mqk, ps[5][:, 8:16], 1.0, EPS, ALU.mult, ALU.add).then_inc(sem("mqk"), 1)
                E.wait("hln", i)
                for j in range(2):
                    last = v.tensor_tensor_scan(hG[:, j, :], cn("ones"), he[:, j * P:(j + 1) * P], 0.0, ALU.mult,
                                                ALU.add)
                link(last)
                hGf = hG.rearrange("p a b -> p (a b)")
                for l in range(LEVELS):
                    m = 2 ** l
                    g3 = hGf.rearrange("p (n b) -> p n b", b=2 * m)
                    last = tt(hE[:, 256 * l:256 * l + 256].rearrange("p (n b) -> p n b", b=2 * m), g3,
                              bc(g3[:, :, m - 1], 2 * m), ALU.subtract)
                link(last)
                v.scalar_tensor_tensor(hE, hE, -1.0, hE, ALU.mult, ALU.min).then_inc(sem("hlev"), 1)
                E.wait("rOU", i)
                link(tt(SrB, SrB, bc(cn("rdec"), P), ALU.mult))
                link(tt(three(rkz, 2, P), three(ps[2][:, 0:256], 2, P), heads(cn("pair"), 2), ALU.mult))
                tt(SrB, SrB, three(rkz, 2, P), ALU.add).then_inc(sem("r_state"), 1)
                link(refine(mqk, rqk, tqk, "qk_y0", i))
                E.wait("ktok", i)
                tt(khat, b4(3), bc(rqk[:, 4:8], P), ALU.mult).then_inc(sem("khat"), 1)
                E.wait("vtok", i)
                tt(vb, b4(4), bc(beta, P), ALU.mult).then_inc(sem("vb"), 1)
                E.wait("gam", i)
                link(tt(bG, beta, eG, ALU.mult))
                E.wait("khat", i)
                tt(kb, khat, bc(bG, P), ALU.mult)
                tt(kdec, khat, bc(ekd, P), ALU.mult)
                E.wait("kk", i)
                link(tt(A, b4(4), Dg, ALU.mult))
                tt(A, A, bc(beta, P), ALU.mult).then_inc(sem("A"), 1)
                E.wait("qk", i)
                tt(qkm, b4(0), Dl, ALU.mult).then_inc(sem("qkm"), 1)
                E.wait("A", i)
                link(tt(T, A, heads(cn("m0neg"), 4), ALU.mult))
                tt(T, T, heads(ident, 4), ALU.add)
                E.wait("tA", i)
                link(tt(U, b4(3), heads(cn("m0negT"), 4), ALU.mult))
                tt(U, U, heads(ident, 4), ALU.add).then_inc(sem("UT"), 1)
                E.wait("hexp", i)
                hE3, hQ3 = three(hE, LEVELS, 256), three(hQ, LEVELS, 256)
                tt(hQ3, hE3, heads(hr[:, 0:256], LEVELS), ALU.mult)
                tt(hqg, hqg, three(hr[:, 0:256], 2, P), ALU.mult)
                link(tt(hkd, hkd, three(he[:, 256:512], 2, P), ALU.mult))
                tt(hE3, hE3, heads(he[:, 256:512], LEVELS), ALU.mult).then_inc(sem("hKQ"), 1)
                for l in range(1, LEVELS):
                    E.wait("Z", i, l)
                    tt(Zs, b4(0), heads(cn("lev")[:, l * P:(l + 1) * P], 4), ALU.mult).then_inc(sem("Zs"), 1)
                    if l <= 4:
                        E.wait("hA", i, l)
                        lev = 2 * (l - 1)
                        mask0 = heads(cn("lev")[:, lev * P:(lev + 1) * P], 2)
                        mask1 = heads(cn("lev")[:, (lev + 1) * P:(lev + 2) * P].bitcast(I32), 2)
                        for q in range(2):
                            last = tt(khat[:, 2 * q:2 * q + 2, :], three(ps[1 + q][:, 0:256], 2, P), mask0, ALU.mult)
                        for q in range(2):
                            last = v.copy_predicated(hatt[:, 2 * q:2 * q + 2, :], mask1,
                                                     three(ps[1 + q][:, 256:512], 2, P))
                        link(last)
                        last = tt(hatt, hatt, khat, ALU.add)
                        last.then_inc(sem("hatt"), 1)
                    E.wait("dU", i, l)
                    last = tt(U, U, b4(4), ALU.subtract)
                    if l < LEVELS - 1:
                        E.wait("dT", i, l)
                        last = tt(T, T, b4(5), ALU.subtract)
                    last.then_inc(sem("UT"), 1)
                E.wait("hOU", i)
                link(tt(ShB, ShB, bc(ehGL, P), ALU.mult))
                link(tt(three(he[:, 0:256], 2, P), three(ps[2][:, 0:256], 2, P), heads(cn("pair"), 2), ALU.mult))
                link(tt(ShB, ShB, three(he[:, 0:256], 2, P), ALU.add))
                link(v.tensor_scalar(sg4, rqk[:, 0:4], 128.0 ** -0.5, None, ALU.mult))
                od = three(obuf[:, 256:768], 4, P)
                E.wait("o1", i)
                link(tt(od, b4(5), bc(eG, P), ALU.mult))
                E.wait("o2", i)
                link(tt(od, od, b4(0), ALU.add))
                E.wait("r_out", i)
                E.wait("h_out", i)
                tt(od, od, bc(sg4, P), ALU.mult).then_inc(sem("od"), 1)
                link(tt(S, S, bc(eGL, P), ALU.mult))
                E.wait("dS", i)
                link(tt(S, S, b4(3), ALU.add))
                E.wait("o_sq", i)
                link(v.reduce_sum(sh, hQ[:, 0:1024].rearrange("p (a b) -> p a b", a=16), AX.X))
                link(v.reduce_sum(th_[:, 0:4], sh[:, 4:12].rearrange("p (a b) -> p a b", a=4), AX.X))
                v.tensor_scalar(mh, sh, 1.0 / 64, EPS, ALU.mult, ALU.add)
                link(v.tensor_scalar(sh, sh, 1.0 / 64, EPS, ALU.mult, ALU.add))
                v.tensor_scalar(mh[:, 4:12].rearrange("p (a b) -> p a b", a=4), bc(th_[:, 0:4], 2), 1.0 / P, EPS,
                                ALU.mult, ALU.add).then_inc(sem("mh"), 1)
                link(refine(mh, rh, th_, "h_y0", i))
                o16 = obuf.rearrange("p (a b) -> p a b", a=16)
                link(tt(o16, o16, bc(rh, 64), ALU.mult))
                tt(obuf, obuf, gt, ALU.mult).then_inc(sem("mixed"), 1)
                E.wait("tm", i, 1)
                tt(mT[:, 0:4, :], b4(1), bc(gmc[:, 0:4], P), ALU.mult)
                E.wait("tm", i)
                tt(mT[:, 4:8, :], b4(2), bc(gmc[:, 4:8], P), ALU.mult).then_inc(sem("mT"), 1)
                E.wait("xres_loaded", i)
                E.wait("wo", i)
                tt(hbuf[:, 0:512], hbuf[:, 0:512], ps[4][:, :], ALU.add)
                tt(hbuf[:, 512:1024], hbuf[:, 512:1024], ps[5][:, :], ALU.add).then_inc(sem("h_ready"), 1)
                E.wait("h_sq", i)
                v.tensor_scalar(m2, ss2, 1.0 / DM, EPS, ALU.mult, ALU.add).then_inc(sem("m2"), 1)
                link(refine(m2, r2, t2, "n_y0", i))
                v.tensor_scalar(hnb, hbuf[:, :], r2, None, ALU.mult).then_inc(sem("hn_ready"), 1)
                E.wait("t2", i, 1)
                tt(mT[:, 0:4, :], b4(0), bc(g2c[:, 0:4], P), ALU.mult)
                E.wait("t2", i)
                tt(mT[:, 4:8, :], b4(3), bc(g2c[:, 4:8], P), ALU.mult).then_inc(sem("h2T"), 1)

            dve.wait_ge(sem("params_loaded"), N_PARAMS)
            v.tensor_tensor(lbt[:, 0, :], lbc[:, :], lbc[:, :], ALU.subtract).then_inc(sem("lb_shifted"), 1)
            dve.wait_ge(sem("param_exp"), 1)
            link(v.reciprocal(lbt[:, 2, :], lbt[:, 1, :]))
            link(v.tensor_tensor(lbt[:, 3, :], lbt[:, 1, :], lbt[:, 2, :], ALU.mult))
            link(v.tensor_tensor(lbv, lbt[:, 3, :], lbt[:, 3, :], ALU.subtract))
            v.tensor_scalar(oml, lbv, -1.0, 1.0, ALU.mult, ALU.add)
            v.tensor_scalar(negA, negA, -1.0, None, ALU.mult)
            v.memset(cb[:, :, 0:3], 0.0).then_inc(sem("hist"), 1)
            v.memset(SrB, 0.0)
            v.memset(ShB, 0.0)
            v.memset(S, 0.0).then_inc(sem("zeroed"), 1)
            x_mean(0)
            x_scale(0)
            x_gain(0)
            SETUP = E.c
            with dve.Fori(0, NT - 1) as i:
                E.start(i * DVE_LINKS + SETUP)
                mixer(i, True)
                E.end()
            E.start((NT - 1) * DVE_LINKS + SETUP)
            mixer(NT - 1, False)

            chain = [0]

            def seq(ins):
                chain[0] += 1
                ins.then_inc(sem("route_chain"), 1)
                dve.wait_ge(sem("route_chain"), chain[0])

            def first_of(onehot, values, top, width):
                io = cn("iota")[:, 0:width]
                seq(tt(onehot, values, bc(top, width), ALU.is_equal))
                seq(tt(onehot, onehot, heads(io, NT), ALU.mult))
                seq(v.tensor_reduce(ri, onehot, AX.X, ALU.min))
                seq(tt(onehot, heads(io, NT), bc(ri, width), ALU.is_equal))

            dve.wait_ge(sem("logits"), NT)
            gl = lg[:, :, 0:NGRP]
            seq(v.reduce_max(gm, gl, AX.X))
            seq(tt(gex, gl, bc(gm, NGRP), ALU.subtract))
            first_of(goh, gl, gm, NGRP)
            seq(v.tensor_scalar(goh, goh, BIG, -BIG, ALU.mult, ALU.add))
            seq(tt(el.rearrange("p t (g e) -> p t g e", g=NGRP),
                   lg[:, :, NGRP:].rearrange("p t (g e) -> p t g e", g=NGRP), bc(goh, EPG), ALU.add))
            seq(v.reduce_max(m1, el, AX.X))
            first_of(oh1, el, m1, NE)
            seq(tt(cnd, oh1, oh1, ALU.mult))
            elf, cf = (x.rearrange("p a b -> p (a b)") for x in (el, cnd))
            seq(v.scalar_tensor_tensor(elf, cf, -BIG, elf, ALU.mult, ALU.add))
            seq(v.reduce_max(m2_, el, AX.X))
            first_of(oh2, el, m2_, NE)
            tt(e2, m2_, m1, ALU.subtract).then_inc(sem("r_shift"), 1)
            seq(tt(cnd, oh1, oh2, ALU.add))
            dve.wait_ge(sem("y_zeroed"), 64)
            seq(v.memset(mrun[:, 0, :], 0.0))
            for t in range(NT):
                seq(tt(mrun[:, t + 1, :], mrun[:, t, :], cnd[:, t, :], ALU.add))
            v.engine_nop().then_inc(sem("picked"), 1)
            dve.wait_ge(sem("r_exp"), 1)
            seq(v.reduce_sum(gm, gex, AX.X))
            seq(v.reciprocal(gm, gm))
            seq(v.tensor_scalar(m1, e2, 1.0, None, ALU.add))
            seq(v.reciprocal(m1, m1))
            seq(tt(w12[:, 0, :], gm, m1, ALU.mult))
            seq(tt(w12[:, 1, :], w12[:, 0, :], e2, ALU.mult))
            dve.wait_ge(sem("ranks"), 1)
            seq(v.tensor_copy(cnt, ps[1][:, 0:32]))
            c8 = cmp_[:, 0:256].rearrange("p (a b) -> p a b", a=32)
            seq(tt(c8, bc(cnt, 8), heads(cn("c128"), 32), ALU.is_gt))
            seq(v.reduce_sum(nblk, c8, AX.X))
            seq(v.tensor_tensor_scan(incl, cn("ones")[:, 0:32], nblk, 0.0, ALU.mult, ALU.add))
            seq(tt(base, incl, nblk, ALU.subtract))
            seq(v.tensor_scalar(base, base, float(BLK), None, ALU.mult))
            seq(tt(rk, ps[0][:, 0:256].rearrange("p (a b) -> p a b", a=NT), heads(base, NT), ALU.add))
            for k, oh in enumerate((oh1, oh2)):
                seq(tt(el, oh, rk, ALU.mult))
                seq(v.reduce_sum(dst[:, k, :], el, AX.X))
            v.tensor_copy(dsti[:, :, :], dst[:, :, :]).then_inc(sem("dst_ready"), 1)
            c48 = cmp_.rearrange("p (a b) -> p a b", a=NB_MAX)
            seq(tt(c48, heads(incl, NB_MAX), bc(cn("biota"), NE), ALU.is_le))
            seq(v.reduce_sum(blkt[:, 0:NB_MAX], c48, AX.X))
            seq(v.tensor_scalar(blkt[:, 0:NB_MAX], blkt[:, 0:NB_MAX], float(NE - 1), None, ALU.min))
            seq(v.tensor_scalar(cmp_[:, 0:NB_MAX // 2], cn("biota")[:, 0:NB_MAX // 2], 2.0, incl[:, NE - 1:NE],
                                ALU.mult, ALU.is_lt))
            seq(v.reduce_sum(blkt[:, NB_MAX:NB_MAX + 1], cmp_[:, 0:NB_MAX // 2], AX.X))
            seq(v.tensor_scalar(blkt[:, NB_MAX + 1:NB_MAX + 2], blkt[:, NB_MAX:NB_MAX + 1], -1.0, None, ALU.add))
            v.tensor_copy(blki[:, :], blkt[:, :]).then_inc(sem("blk_ready"), 1)
            dve.wait_ge(sem("blk_ready"), 1)
            pairs = dve.value_load(blki[0:1, NB_MAX:NB_MAX + 1], min_val=NB_MIN // 2, max_val=NB_MAX // 2)
            last_pair = dve.value_load(blki[0:1, NB_MAX + 1:NB_MAX + 2], min_val=NB_MIN // 2 - 1,
                                      max_val=NB_MAX // 2 - 1)

            def x_gain2(b):
                dve.wait_ge(sem("xt_done"), b + 1)
                tt(xT[:, 0:4, :], b4(0), bc(g2c[:, 0:4], P), ALU.mult)
                tt(xT[:, 4:8, :], b4(1), bc(g2c[:, 4:8], P), ALU.mult).then_inc(sem("xT_ready"), 1)

            def swiglu(b):
                dve.wait_ge(sem("eg"), b + 1)
                v.tensor_scalar(eg, eg, 1.0, None, ALU.add).then_inc(sem("swiglu_step"), 1)
                dve.wait_ge(sem("swiglu_step"), b * 3 + 1)
                v.reciprocal(eg, eg).then_inc(sem("swiglu_step"), 1)
                dve.wait_ge(sem("swiglu_step"), b * 3 + 2)
                tt(eg, eg, ps[2][:, :], ALU.mult).then_inc(sem("swiglu_step"), 1)
                dve.wait_ge(sem("swiglu_step"), b * 3 + 3)
                dve.wait_ge(sem("gu_done"), b + 1)
                tt(hact, eg, ps[3][:, :], ALU.mult).then_inc(sem("hact_ready"), 1)

            def y_right(b, q, par):
                dve.wait_ge(sem("down_done"), b + 1)
                dve.wait_ge(sem(f"y_stored{par}"), q * 16 + 16)
                v.tensor_copy(yo[par][:, 512:1024], ps[6][:, :]).then_inc(sem("y1_ready"), 1)

            x_gain2(0)
            swiglu(0)
            x_gain2(1)
            with dve.Fori(1, pairs) as q:
                swiglu(2 * q - 1)
                x_gain2(2 * q)
                y_right(2 * q - 2, q - 1, 0)
                swiglu(2 * q)
                x_gain2(2 * q + 1)
                y_right(2 * q - 1, q - 1, 1)
            swiglu(last_pair * 2 + 1)
            y_right(last_pair * 2, last_pair, 0)
            y_right(last_pair * 2 + 1, last_pair, 1)

            dve.wait_ge(sem("fgain_loaded"), 16)
            cc = [0]

            def cseq(ins):
                cc[0] += 1
                ins.then_inc(sem("comb_chain"), 1)
                dve.wait_ge(sem("comb_chain"), cc[0])

            for t in range(NT):
                b = t % 2
                dve.wait_ge(sem(f"rows_loaded{b}"), 32 * (t // 2 + 1))
                dve.wait_ge(sem(f"ch_loaded{b}"), 16 * (t // 2 + 1))
                if t >= 2:
                    dve.wait_ge(sem(f"out_stored{b}"), 16 * (t // 2))
                cseq(v.scalar_tensor_tensor(cm_o[b], cm_y1[b], w12[:, 0, t:t + 1], cm_h[b], ALU.mult, ALU.add))
                v.scalar_tensor_tensor(cm_o[b], cm_y2[b], w12[:, 1, t:t + 1], cm_o[b], ALU.mult, ALU.add) \
                    .then_inc(sem("c_sum"), 1)
                dve.wait_ge(sem("c_sq"), t + 1)
                v.tensor_scalar(mx, ssx, 1.0 / DM, EPS, ALU.mult, ALU.add).then_inc(sem("c_m"), 1)
                dve.wait_ge(sem("c_root"), 2 * t + 2)
                cseq(tt(tx_, rx, rx, ALU.mult))
                cseq(tt(tx_, tx_, mx, ALU.mult))
                cseq(v.tensor_scalar(tx_, tx_, -0.5, 1.5, ALU.mult, ALU.add))
                cseq(tt(rx, rx, tx_, ALU.mult))
                v.scalar_tensor_tensor(cm_o[b], cm_o[b], rx, fgain, ALU.mult, ALU.mult).then_inc(sem("c_out"), 1)

        @block.gpsimd
        def _(pool):
            g = nc.gpsimd
            g.iota(toki[:, :], [[P, NT]], base=0, channel_multiplier=1).then_inc(sem("tok_ids"), 1)
            g.memset(slots[:, :], 0).then_inc(sem("slot_zero"), 1)
            pool.wait_ge(sem("tok_ids"), 1)
            pool.wait_ge(sem("slot_zero"), 1)
            pool.dma_start(slot_d.rearrange("(p b) o -> p (b o)", p=P), slots[:, :]).then_inc(sem("slots_zeroed"), 16)
            g.memset(zrow, 0.0).then_inc(sem("slot_zero"), 1)
            pool.wait_ge(sem("slot_zero"), 2)
            pool.wait_ge(sem("xsc"), 2)
            spare = y_d[NB_MIN * BLK:, :].rearrange("(p a) (h c) -> p (a h) c", p=P, c=256)
            rows = spare.shape[1] // 4
            for k in range(4):
                pool.dma_start(spare[:, k * rows:(k + 1) * rows, :],
                               heads(zrow, rows)).then_inc(sem("y_zeroed"), 16)
            pool.wait_ge(sem("slots_zeroed"), 16)
            pool.wait_ge(sem("y_zeroed"), 64)
            pool.wait_ge(sem("dst_ready"), 1)
            for k in range(2):
                for t in range(NT):
                    g.indirect_dma_start(slot_d, bass.IndirectOffsetOnAxis(ap=dsti[:, k, t:t + 1], axis=0),
                                         toki[:, t:t + 1], None).then_inc(sem("slots_set"), 16)
            pool.wait_ge(sem("slots_set"), 16 * 2 * NT)
            with nc.allow_non_contiguous_dma(reason="the slot table is transposed"):
                pool.dma_start(slots[:, :], slot_d.rearrange("(b p) o -> p (b o)", p=P)) \
                    .then_inc(sem("slots_loaded"), 16)
            pool.wait_ge(sem("slots_loaded"), 16)
            pool.wait_ge(sem("hn_stored"), 32 * NT)
            pool.wait_ge(sem("blk_ready"), 1)
            pairs = pool.value_load(blki[0:1, NB_MAX:NB_MAX + 1], min_val=NB_MIN // 2, max_val=NB_MAX // 2)

            def gather(b, par, first):
                if not first:
                    pool.wait_ge(sem("xt_done"), b - 1)
                g.tensor_copy(idxs[par][:, :], slots[:, bass.ds(b, 1)]).then_inc(sem("idx_ready"), 1)
                pool.wait_ge(sem("idx_ready"), b + 1)
                pool.sem_inc(sem("idx_seen"), 1)
                g.indirect_dma_start(xg[par], None, hn_d, bass.IndirectOffsetOnAxis(ap=idxs[par][:, :], axis=0)) \
                    .then_inc(sem(f"tok_loaded{par}"), 16)

            gather(0, 0, True)
            gather(1, 1, True)
            with pool.Fori(1, pairs) as q:
                gather(2 * q, 0, False)
                gather(2 * q + 1, 1, False)

            pool.wait_ge(sem("y_stored0"), pairs * 16 + 16)
            pool.wait_ge(sem("y_stored1"), pairs * 16 + 16)
            pool.sem_inc(sem("idx_seen"), 1)
            for t in range(NT):
                if t >= 2:
                    pool.wait_ge(sem("c_sq"), t - 1)
                for k, rows in enumerate((cm_y1, cm_y2)):
                    g.indirect_dma_start(rows[t % 2], None, y_d,
                                         bass.IndirectOffsetOnAxis(ap=dsti[:, k, t:t + 1], axis=0)) \
                        .then_inc(sem(f"rows_loaded{t % 2}"), 16)


IN_NAMES = ("x", "w_in", "w_out", "gdn_conv", "gdn_a_log", "gdn_dt_bias", "ret_norm", "gdn_norm", "hgrn_norm",
            "hgrn_lower_bounds", "attn_norm", "ffn_norm", "router_group", "router_expert", "w_gate", "w_up", "w_down",
            "final_norm")


def kernel(**inputs):
    import numpy as _np
    import concourse.bacc as _bacc
    from concourse import mybir as _mybir
    from concourse.bass_utils import run_bass_kernel_spmd as _run

    nc = _bacc.Bacc("TRN2", target_bir_lowering=False, num_devices=1)
    arrays, aps = {}, {}
    given = {n: _np.ascontiguousarray(inputs[n]) for n in IN_NAMES}
    given["consts"] = host_consts()
    given["rotary"] = host_rotary()
    for name, arr in given.items():
        arrays[f"in_{name}"] = arr
        aps[name] = nc.dram_tensor(f"in_{name}", arr.shape, _mybir.dt.from_np(arr.dtype), kind="ExternalInput").ap()
    out = nc.dram_tensor("out_0", (1, SEQ, DM), F32, kind="ExternalOutput").ap()
    hn_d = nc.dram_tensor("hn_rows", (SEQ, DM), F32, kind="Internal").ap()
    h_d = nc.dram_tensor("h_rows", (SEQ, DM), F32, kind="Internal").ap()
    y_d = nc.dram_tensor("y_rows", (NB_MAX * BLK, DM), F32, kind="Internal").ap()
    slot_d = nc.dram_tensor("slot_tokens", (NB_MAX * BLK, 1), I32, kind="Internal").ap()
    build(nc, aps, out, hn_d, h_d, y_d, slot_d)
    r = _run(nc, [arrays], core_ids=[0])
    return r.results[0]["out_0"]
```

```python
from contextlib import ExitStack

import numpy as np
import concourse.bass as bass
from concourse import mybir

F32 = mybir.dt.float32
I32 = mybir.dt.int32
ALU = mybir.AluOpType
ACT = mybir.ActivationFunctionType
AX = mybir.AxisListType

P = 128
SEQ = 1024
DM = 1024
NT = SEQ // P
KD = DM // P
IN_W = 4104
C_RQ, C_RV, C_RG = 0, 512, 768
C_DQ, C_DA, C_DB, C_DZ = 1024, 2560, 2564, 2568
C_HQ, C_HI, C_HG = 3080, 3592, 3848
GROUPS = ((1024, 0), (1536, 0), (2048, 0), (3080, 0), (0, 0), (2560, 8), (512, 0), (3592, 0))
NG = len(GROUPS)
GW = 512
NE, NGRP, EPG, DE = 32, 4, 8, 512
KE = DE // P
BLK = 128
NB_MAX = 48
NB_MIN = 16
EPS = 1e-6
BIG = 1e30
LEVELS = 7
RSQRT_MAGIC = float(0x5F3759DF)
RET_GAMMA = [1.0 - 2.0 ** (-5.0 - h) for h in range(4)]


def const_layout():
    at, off = {}, 0
    for name, n in (("ident", 128), ("tri", 128), ("dmat", 512), ("xi", 256), ("zeta", 256), ("rdec", 2),
                    ("pair", 128), ("neg_up", 128), ("pos_low", 128), ("m0neg", 128), ("m0negT", 128),
                    ("lev", 8 * 128), ("ones", 128), ("stri", 128), ("iota", 32), ("biota", NB_MAX), ("pcol", 1),
                    ("c128", 8)):
        at[name] = (off, n)
        off += n
    return at, off


def host_consts():
    at, n = const_layout()
    c = np.zeros((P, n), np.float32)

    def put(name, a):
        o, w = at[name]
        c[:, o:o + w] = np.asarray(a, np.float32).reshape(P, w)

    p, f = np.arange(P)[:, None], np.arange(P)[None, :]
    put("ident", p == f)
    put("tri", p <= f)
    put("stri", p < f)
    put("ones", np.ones((P, P)))
    lg = np.log(np.array(RET_GAMMA))
    d = np.zeros((P, 4, P))
    for h in range(4):
        d[:, h] = np.where(f >= p, np.exp(lg[h] * np.maximum(f - p, 0)), 0) * 0.125
    put("dmat", d[:, [0, 2, 1, 3]])
    xi = np.zeros((P, 2, P))
    dec = np.zeros((P, 2))
    for j in range(2):
        for q in range(2):
            xi[64 * q:64 * q + 64, j] = np.exp(lg[2 * j + q] * (np.arange(P) + 1))[None]
            dec[64 * q:64 * q + 64, j] = np.exp(lg[2 * j + q] * P)
    put("xi", xi)
    put("rdec", dec)
    put("zeta", np.repeat(np.exp(lg[None] * (P - 1 - np.arange(P))[:, None]) * 0.125, 64, axis=1))
    put("pair", (p // 64) == (f // 64))
    put("neg_up", np.where(f >= p, 0, -BIG))
    put("pos_low", np.where(f < p, 0, BIG))
    lev = np.zeros((P, 8, P))
    for l in range(LEVELS):
        m = 2 ** l
        lev[:, l] = (p // (2 * m) == f // (2 * m)) & (p % (2 * m) < m) & (f % (2 * m) >= m)
    lev[:, 7] = p == f
    put("lev", lev)
    put("m0negT", -lev[:, 0])
    put("m0neg", -lev[:, 0].T)
    put("iota", np.broadcast_to(np.arange(32) - 64, (P, 32)))
    put("biota", np.broadcast_to(np.arange(NB_MAX), (P, NB_MAX)))
    put("pcol", np.arange(P))
    put("c128", np.broadcast_to(np.arange(8) * BLK, (P, 8)))
    return c


def host_rotary():
    inv = (np.float32(10000.0) ** (-np.arange(0, 64, 2, dtype=np.float32) / np.float32(64))).astype(np.float32)
    ang = np.arange(SEQ, dtype=np.float32)[:, None] * inv[None]
    cos, sin = np.cos(ang), np.sin(ang)
    return np.concatenate([cos, cos, -sin, sin], axis=1).astype(np.float32)


def bc(ap, n):
    return ap.unsqueeze(ap.ndim).to_broadcast(list(ap.shape) + [n])


def heads(ap, n):
    return ap.unsqueeze(1).to_broadcast([ap.shape[0], n, ap.shape[1]])


def build(nc, a, out, hn_d, h_d, y_d):
    ctx = ExitStack()
    with ctx:
        def sb(name, shape, dt=F32):
            return ctx.enter_context(nc.sbuf_tensor(name, shape, dt))

        sems = {}

        def sem(name):
            if name not in sems:
                sems[name] = ctx.enter_context(nc.semaphore(name))
            return sems[name]

        C_AT, C_N = const_layout()
        cst = sb("cst", [P, C_N])

        def cn(name):
            o, w = C_AT[name]
            return cst[:, o:o + w]

        ident = cn("ident")
        g1c = sb("g1c", [P, KD])
        g2c = sb("g2c", [P, KD])
        gmc = sb("gmc", [P, KD])
        convw = sb("convw", [P, 4, 12])
        abrow = sb("abrow", [P, 8])
        lbc = sb("lbc", [P, 2])
        lbw = sb("lbw", [P, 4, 2])
        wr = sb("wr", [P, KD, 36])
        xin = sb("xin", [P, DM])
        junk = sb("junk", [P, DM])
        hbuf = sb("hbuf", [P, DM])
        sc = sb("sc", [P, 192])
        lg = sb("lg", [P, NT, 36])

        BIG_N = 45400
        big = sb("big", [P, BIG_N])
        used = [0]

        def part(n):
            o = used[0]
            used[0] += n
            assert used[0] <= BIG_N, used[0]
            return big[:, o:o + n]

        def three(ap, x, y):
            return ap.rearrange("p (a b) -> p a b", a=x, b=y)

        wg = [part(KD * 520) for _ in range(2)]
        wout = three(part(KD * DM), KD, DM)
        pj = part(IN_W)
        cb = three(part(12 * 131), 12, 131)
        cy = three(part(1536), 12, 128)
        ce = part(1536)
        xnT = three(part(1024), KD, P)
        gt = part(1024)
        rot = part(512)
        rtab = part(128)
        rqT = three(part(512), 4, P)
        rqX = three(part(256), 2, P)
        rkz = part(256)
        rA = three(part(512), 4, P)
        hatt = three(part(512), 4, P)
        SrB = three(part(256), 2, P)
        ShB = three(part(256), 2, P)
        S = three(part(512), 4, P)
        Dm, Dl, Dg, A, T, U, Zs, khat, khT, kb, kdec, vb, qkm = [three(part(512), 4, P) for _ in range(13)]
        gBr, nwT, vn = Zs, khT, Dm
        hr = part(512)
        he = part(512)
        hG = three(part(256), 2, P)
        hE = part(LEVELS * 256)
        hQ = part(LEVELS * 256)
        hqg = three(part(256), 2, P)
        hkd = three(part(256), 2, P)
        hkT = part(256)
        obuf = part(1024)
        hnb = part(1024)
        rtmp = three(hQ[:, 1024:1536], 4, P)
        mT = three(hE[:, 0:1024], KD, P)
        mix_used = used[0]
        x_all = wout.rearrange("p a b -> p (a b)").rearrange("p (t d) -> p t d", t=NT)
        x_junk = hE[:, 0:DM]
        used[0] = 0
        wexp = [[three(part(4096), KD, DE), three(part(4096), KD, DE), three(part(4096), KE, DM)] for _ in range(2)]
        xg = [part(DM) for _ in range(2)]
        xT = three(part(DM), KD, P)
        eg = part(DE)
        hact = part(DE)
        hT = three(part(DE), KE, P)
        yo = [part(DM) for _ in range(2)]
        moe_used = used[0]
        el, oh1, oh2, cnd, rk = [three(part(256), NT, 32) for _ in range(5)]
        goh, gex = [three(part(NGRP * NT), NT, NGRP) for _ in range(2)]
        gm, m1, m2_, e2, ri = [part(NT) for _ in range(5)]
        cnt, nblk, incl, base = [part(NE) for _ in range(4)]
        cmp_ = part(NB_MAX * 32)
        count_row = part(P)
        in_pos = three(part(2 * NT * P), 2 * NT, P)
        in_blk = three(part(2 * NT * NB_MAX), 2 * NT, NB_MAX)
        posi, blockn = [part(2 * NT).bitcast(I32) for _ in range(2)]
        posf, blockf = [part(2 * NT) for _ in range(2)]
        tokf = part(NT)
        used[0] = 0
        cm_y1 = [part(DM) for _ in range(NT)]
        cm_y2 = [part(DM) for _ in range(NT)]
        assert used[0] <= 2 * 3 * 4096
        used[0] = moe_used
        cm_h = three(part(NT * DM), NT, DM)
        fgain = part(DM)
        mrun = sb("mrun", [P, NT + 1, 32])
        w12 = sb("w12", [P, 2, NT])
        dst = sb("dst", [P, 2, NT])
        dsti = sb("dsti", [P, 2, NT], I32)
        blkt = sb("blkt", [P, NB_MAX + 2])
        blki = sb("blki", [P, NB_MAX + 2], I32)
        slots = sb("slots", [P, NB_MAX], I32)
        zrow = mrun[:, 0:NT, :].rearrange("p a b -> p (a b)")
        idxs = [sb(f"idx{k}", [P, 1], I32) for k in range(2)]

        ps = [ctx.enter_context(nc.psum_tensor(f"ps{k}", [P, 512], F32)) for k in range(8)]

        def b4(k):
            return ps[k][:, :].rearrange("p (a b) -> p a b", a=4)

        ssx, mx, rx, tx_ = [sc[:, 160 + NT * k:160 + NT * (k + 1)] for k in range(4)]
        dax, dae, dl, gcol, beta, gc, eG, eGL, ekd, bG, dxx = [sc[:, 8 + 4 * k:12 + 4 * k] for k in range(11)]
        mqk, rqk, tqk = [sc[:, 56 + 8 * k:64 + 8 * k] for k in range(3)]
        mh, rh, th_, sh = [sc[:, 80 + 16 * k:96 + 16 * k] for k in range(4)]
        ehGL = sc[:, 144:146]
        ss2, m2, r2, t2 = [sc[:, 150 + k:151 + k] for k in range(4)]
        sg4 = sc[:, 154:158]
        negA, lbv, oml = lbw[:, 0:2, :].rearrange("p a b -> p (a b)"), lbw[:, 2, :], lbw[:, 3, :]
        lbt = sb("lbt", [P, 4, 2])

        w_view = a["w_in"][0].rearrange("(k p) n -> p k n", p=P)
        x_view = a["x"][0].rearrange("(t p) d -> t p d", p=P)
        hn_v = hn_d.rearrange("(t p) d -> t p d", p=P)
        h_v = h_d.rearrange("(t p) d -> t p d", p=P)
        out_v = out[0].rearrange("(t p) d -> t p d", p=P)
        rot_v = a["rotary"].rearrange("(t p) d -> t p d", p=P)

        PER = {"proj_filled": NG, "proj_copied": NG, "x_loaded": 16, "xres_loaded": 16, "rot_loaded": 16,
               "hn_stored": 32, "UT": LEVELS, "Z": LEVELS - 1, "Zs": LEVELS - 1, "dU": LEVELS - 1,
               "dT": LEVELS - 2, "tconv": 3, "tm": 2, "t2": 2, "tx": 2, "hA": 4, "hatt": 4}

        def at(name, i, k=None):
            per = PER.get(name, 1)
            return i * per + (per if k is None else k)

        class Engine:

            def __init__(self, eng, chain, per):
                self.eng, self.chain, self.per, self.c, self.base = eng, chain, per, 0, 0

            def wait(self, name, i, k=None):
                self.eng.wait_ge(sem(name), at(name, i, k))

            def link(self, ins):
                self.c += 1
                ins.then_inc(sem(self.chain), 1)
                self.eng.wait_ge(sem(self.chain), self.base + self.c)

            def start(self, base):
                self.c, self.base = 0, base

            def end(self):
                assert self.c == self.per, (self.chain, self.c)

        N_PARAMS = 16 * 18
        DVE_LINKS, ACT_LINKS = 74, 1
        block = ctx.enter_context(nc.Block())

        @block.sync
        def _(sp):
            loads = [0]

            def ld(dst_, src):
                loads[0] += 16
                sp.dma_start(dst_, src).then_inc(sem("params_loaded"), 16)

            ld(cst[:, :], a["consts"])
            sp.dma_start(xin[:, :], x_view[0]).then_inc(sem("x_loaded"), 16)
            with nc.allow_non_contiguous_dma(reason="small parameter vectors"):
                ld(g1c[:, :], a["attn_norm"][0].rearrange("(k p) -> p k", p=P))
                ld(g2c[:, :], a["ffn_norm"][0].rearrange("(k p) -> p k", p=P))
                ld(gmc[:, 0:2], a["ret_norm"][0].rearrange("(k p) -> p k", p=P))
                gd = a["gdn_norm"][0].rearrange("(p o) -> p o", o=1)
                for h in range(4):
                    ld(gmc[:, 2 + h:3 + h], gd)
                ld(gmc[:, 6:8], a["hgrn_norm"][0].rearrange("(k p) -> p k", p=P))
                ld(lbc[:, :], a["hgrn_lower_bounds"][0].rearrange("(k p) -> p k", p=P))
                for j in range(4):
                    ld(convw[:, j, :], a["gdn_conv"][0, j].rearrange("(k p) -> p k", p=P))
                ld(abrow[:, 0:4], a["gdn_a_log"].to_broadcast([P, 4]))
                ld(abrow[:, 4:8], a["gdn_dt_bias"].to_broadcast([P, 4]))
                ld(wr[:, :, 0:4], a["router_group"][0].rearrange("(k p) n -> p k n", p=P))
            ld(wr[:, :, 4:36], a["router_expert"][0].rearrange("(k p) n -> p k n", p=P))
            assert loads[0] == N_PARAMS, loads[0]

            def load_w(t, n, nxt):
                if nxt or n >= 2:
                    sp.wait_ge(sem("proj_filled"), at("proj_filled", t, n - 1))
                c0, extra = GROUPS[n]
                w = GW + extra
                sp.dma_start(three(wg[n % 2][:, 0:KD * w], KD, w), w_view[:, :, c0:c0 + w]) \
                    .then_inc(sem(f"w_in_loaded{n % 2}"), 16)

            def tile_steps(i, nxt, nxt2):
                if nxt2:
                    sp.wait_ge(sem("xsc"), i + 2)
                    sp.dma_start(xin[:, :], x_view[i + 2]).then_inc(sem("x_loaded"), 16)
                if nxt:
                    sp.wait_ge(sem("rot"), i + 1)
                    sp.dma_start(rtab, rot_v[i + 1]).then_inc(sem("rot_loaded"), 16)
                sp.wait_ge(sem("hbuf_free"), i + 1)
                sp.dma_start(hbuf[:, :], x_view[i]).then_inc(sem("xres_loaded"), 16)
                if nxt:
                    for n in range(NG):
                        load_w(i + 1, n, True)
                sp.wait_ge(sem("h_ready"), i + 1)
                sp.dma_start(h_v[i], hbuf[:, :]).then_inc(sem("hn_stored"), 16)
                sp.wait_ge(sem("hn_ready"), i + 1)
                sp.dma_start(hn_v[i], hnb).then_inc(sem("hn_stored"), 16)
                sp.wait_ge(sem("hn_stored"), at("hn_stored", i))
                sp.sem_inc(sem("hbuf_free"), 1)

            load_w(0, 0, False)
            load_w(0, 1, False)
            sp.dma_start(x_all, a["x"][0].rearrange("(t p) d -> p t d", p=P)).then_inc(sem("x_all_loaded"), 16)
            sp.wait_ge(sem("xsc"), 1)
            sp.dma_start(xin[:, :], x_view[1]).then_inc(sem("x_loaded"), 16)
            sp.dma_start(rtab, rot_v[0]).then_inc(sem("rot_loaded"), 16)
            for n in range(2, NG):
                load_w(0, n, False)
            sp.wait_ge(sem("x_sq"), 2)
            sp.dma_start(wout, a["w_out"][0].rearrange("(k p) n -> p k n", p=P)).then_inc(sem("w_out_loaded"), 16)
            sp.sem_inc(sem("hbuf_free"), 1)
            with sp.Fori(0, NT - 2) as i:
                tile_steps(i, True, True)
            tile_steps(NT - 2, True, False)
            tile_steps(NT - 1, False, False)

            sp.wait_ge(sem("logits"), NT)
            sp.wait_ge(sem("blk_ready"), 1)
            pairs = sp.value_load(blki[0:1, NB_MAX:NB_MAX + 1], min_val=NB_MIN // 2, max_val=NB_MAX // 2)

            def load_expert(b, par, first):
                e = sp.value_load(blki[0:1, bass.ds(b, 1)], min_val=0, max_val=NE - 1)
                if not first:
                    sp.wait_ge(sem("gu_done"), b - 1)
                for m, name in enumerate(("w_gate", "w_up")):
                    sp.dma_start(wexp[par][m], a[name][0, e].rearrange("(k p) n -> p k n", p=P)) \
                        .then_inc(sem(f"gu_loaded{par}"), 16)
                if not first:
                    sp.wait_ge(sem("down_done"), b - 1)
                sp.dma_start(wexp[par][2], a["w_down"][0, e].rearrange("(k p) n -> p k n", p=P)) \
                    .then_inc(sem(f"down_loaded{par}"), 16)

            load_expert(0, 0, True)
            load_expert(1, 1, True)
            sp.wait_ge(sem("slots_ready"), 1)
            sp.dma_start(cm_h, h_d.rearrange("(t p) d -> p t d", p=P)).then_inc(sem("ch_loaded"), 16)
            sp.dma_start(fgain, a["final_norm"].partition_broadcast(P)).then_inc(sem("ch_loaded"), 16)
            with sp.Fori(1, pairs) as q:
                load_expert(2 * q, 0, False)
                load_expert(2 * q + 1, 1, False)

        @block.tensor
        def _(pe):
            t_ = nc.tensor
            E = Engine(pe, "pe_chain", 0)

            def transposes(bank, blocks, name):
                for k, blk in enumerate(blocks):
                    last = t_.transpose(ps[bank][:, k * P:(k + 1) * P], blk, ident)
                last.then_inc(sem(name), 1)

            def each_head(bank, lhs, rhs, name):
                for h in range(4):
                    last = t_.matmul(b4(bank)[:, h, :], lhs[:, h, :], rhs[:, h, :], start=True, stop=True)
                last.then_inc(sem(name), 1)

            def cols(ap, k0, n):
                return [ap[:, k * P:(k + 1) * P] for k in range(k0, k0 + n)]

            def x_transposes(t):
                E.wait("xsc", t)
                transposes(6, cols(junk, 0, 4), "tx")
                transposes(7, cols(junk, 4, 4), "tx")

            def project(t, n, nxt, k0, k1):
                c0, extra = GROUPS[n]
                w = GW + extra
                if k0 == 0:
                    if n == 0:
                        E.wait("xnT", t)
                    pe.wait_ge(sem(f"w_in_loaded{n % 2}"), t * 64 + 16 * (n // 2 + 1))
                    if nxt or n >= 2:
                        E.wait("proj_copied", t, n - 1)
                wv = three(wg[n % 2][:, 0:KD * w], KD, w)
                for k in range(k0, k1):
                    last = t_.matmul(ps[6 + n % 2][:, :], xnT[:, k, :], wv[:, k, extra:w], start=k == 0,
                                     stop=k == KD - 1)
                if k1 == KD:
                    for k in range(KD if extra else 0):
                        last = t_.matmul(ps[3][:, 0:8], xnT[:, k, :], wv[:, k, 0:8], start=k == 0, stop=k == KD - 1)
                    last.then_inc(sem("proj_filled"), 1)

            def two_heads_out(bank, qx, Sx, att, v0):
                for j in range(2):
                    t_.matmul(ps[bank][:, j * P:(j + 1) * P], qx[:, j, :], Sx[:, j, :], start=True, stop=False)
                    for q in range(2):
                        c = v0 + P * j + 64 * q
                        t_.matmul(ps[bank][:, j * P + 64 * q:j * P + 64 * q + 64], att[:, 2 * q + j, :],
                                  pj[:, c:c + 64], start=False, stop=q == 1)

            def mixer(i, nxt):
                def group(n, k0=0, k1=KD):
                    if nxt:
                        project(i + 1, n, True, k0, k1)

                E.wait("proj_copied", i)
                transposes(0, cols(pj, C_DQ // P, 4), "tconv")
                transposes(1, cols(pj, C_DQ // P + 4, 4), "tconv")
                transposes(2, cols(pj, C_DQ // P + 8, 4), "tconv")
                transposes(3, [pj[:, C_HQ + k * P:C_HQ + (k + 1) * P] for k in range(4)], "th")
                if nxt:
                    x_transposes(i + 1)
                E.wait("rot", i)
                transposes(4, cols(rot, 0, 4), "tr")
                group(0)
                E.wait("cb_in", i)
                E.wait("rqT", i)
                for q in range(2):
                    for j in range(2):
                        last = t_.matmul(ps[1 + q][:, j * P:(j + 1) * P], rqT[64 * q:64 * q + 64, 2 + j, :],
                                         rqT[64 * q:64 * q + 64, j, :], start=True, stop=True)
                last.then_inc(sem("rS"), 1)
                group(1)
                E.wait("gBr", i)
                for h in range(4):
                    last = t_.matmul(b4(0)[:, h, :], gBr[:, h, :], cn("tri"), start=True, stop=True)
                t_.matmul(ps[5][:, 0:4], cn("tri"), gcol, start=True, stop=True).then_inc(sem("Gsum"), 1)
                E.wait("hraw", i)
                E.wait("cs", i)
                transposes(3, [cy[:, 4 + k, :] for k in range(4)], "ktok")
                transposes(4, [cy[:, 8 + k, :] for k in range(4)], "vtok")
                group(2, 0, 2)
                E.wait("csq", i)
                E.wait("gc", i)
                cq = ce[:, 0:1024].rearrange("p (a b) -> p a b", a=8)
                for h in range(8):
                    last = t_.matmul(ps[5][:, 8 + h:9 + h], cq[:, h, :], cn("ones")[:, 0:1], start=True, stop=True)
                last.then_inc(sem("ssq"), 1)
                E.wait("rA", i)
                E.wait("rqX", i)
                two_heads_out(1, rqX, SrB, rA, C_RV)
                for j in range(2):
                    last = t_.matmul(ps[2][:, j * P:(j + 1) * P], rkz[:, j * P:(j + 1) * P],
                                     pj[:, C_RV + P * j:C_RV + P * j + P], start=True, stop=True)
                last.then_inc(sem("rOU"), 1)
                group(2, 2, 8)
                E.wait("khat", i)
                transposes(3, [khat[:, h, :] for h in range(4)], "tkh")
                group(3, 0, 2)
                E.wait("khT", i)
                E.wait("vb", i)
                each_head(4, khT, khT, "kk")
                E.wait("gam", i)
                each_head(0, khT, cy, "qk")
                group(3, 2, 3)
                E.wait("A", i)
                transposes(3, [A[:, h, :] for h in range(4)], "tA")
                group(3, 3, 8)
                for l in range(1, LEVELS):
                    E.wait("UT", i, l)
                    each_head(0, A, U, "Z")
                    if l <= 4:
                        E.wait("hKQ" if l == 1 else "hatt", i, max(l - 1, 1))
                        if l == 1:
                            E.wait("r_out", i)
                            E.wait("r_state", i)
                        for q in range(2):
                            rows = slice(64 * q, 64 * q + 64)
                            for m in range(2):
                                lev = 2 * (l - 1) + m
                                for j in range(2):
                                    o = (2 * lev + j) * P
                                    if lev < LEVELS:
                                        kq, qq = hE[rows, o:o + P], hQ[rows, o:o + P]
                                    else:
                                        kq, qq = he[rows, 256 + j * P:384 + j * P], hr[rows, j * P:(j + 1) * P]
                                    last = t_.matmul(ps[1 + q][:, (2 * m + j) * P:(2 * m + j + 1) * P], kq, qq,
                                                     start=True, stop=True)
                        last.then_inc(sem("hA"), 1)
                    if l == 5:
                        transposes(3, [hkd[:, j, :] for j in range(2)], "thk")
                        group(5, 0, 1)
                    if l == 6:
                        E.wait("hatt", i, 4)
                        two_heads_out(1, hqg, ShB, hatt, C_HI)
                        E.wait("hkT", i)
                        for j in range(2):
                            last = t_.matmul(ps[2][:, j * P:(j + 1) * P], hkT[:, j * P:(j + 1) * P],
                                             pj[:, C_HI + P * j:C_HI + P * j + P], start=True, stop=True)
                        last.then_inc(sem("hOU"), 1)
                    E.wait("Zs", i, l)
                    each_head(4, T, Zs, "dU")
                    if l < LEVELS - 1:
                        each_head(5, Zs, T, "dT")
                    if l <= 4:
                        group(4, 2 * l - 2, 2 * l)
                    else:
                        group(5, 2 * l - 9, 2 * l - 7)
                E.wait("UT", i, LEVELS)
                each_head(0, kb, U, "wT")
                group(5, 5, 8)
                E.wait("nwT", i)
                for h in range(4):
                    t_.matmul(b4(4)[:, h, :], U[:, h, :], vb[:, h, :], start=True, stop=False)
                    last = t_.matmul(b4(4)[:, h, :], nwT[:, h, :], S[:, h, :], start=False, stop=True)
                last.then_inc(sem("vnew"), 1)
                each_head(5, cy, S, "o1")
                E.wait("vn", i)
                each_head(0, qkm, vn, "o2")
                if nxt:
                    E.wait("proj_copied", i + 1, 6)
                each_head(3, kdec, vn, "dS")
                group(6)
                E.wait("mixed", i)
                transposes(1, cols(obuf, 0, 4), "tm")
                transposes(2, cols(obuf, 4, 4), "tm")
                group(7, 0, 2)
                E.wait("mT", i)
                for n in range(2):
                    for k in range(KD):
                        last = t_.matmul(ps[4 + n][:, :], mT[:, k, :], wout[:, k, n * 512:(n + 1) * 512],
                                         start=k == 0, stop=k == KD - 1)
                last.then_inc(sem("wo"), 1)
                group(7, 2, 6)
                E.wait("hn_ready", i)
                transposes(0, cols(hnb, 0, 4), "t2")
                transposes(3, cols(hnb, 4, 4), "t2")
                group(7, 6, 8)
                E.wait("h2T", i)
                for k in range(KD):
                    last = t_.matmul(ps[5][:, 32:68], mT[:, k, :], wr[:, k, :], start=k == 0, stop=k == KD - 1)
                last.then_inc(sem("rt"), 1)

            pe.wait_ge(sem("params_loaded"), N_PARAMS)
            x_transposes(0)
            for n in range(NG):
                project(0, n, False, 0, KD)
            pe.wait_ge(sem("w_out_loaded"), 16)
            pe.wait_ge(sem("zeroed"), 1)
            with pe.Fori(0, NT - 1) as i:
                mixer(i, True)
            mixer(NT - 1, False)

            pe.wait_ge(sem("picked"), 1)
            t_.matmul(ps[0][:, 0:256], cn("stri"), cnd, start=True, stop=False)
            t_.matmul(ps[0][:, 0:256], cn("ones"), mrun[:, 0:NT, :], start=False, stop=True)
            t_.matmul(ps[1][:, 0:32], cn("ones"), mrun[:, NT, :], start=True, stop=True).then_inc(sem("ranks"), 1)
            pe.wait_ge(sem("dst_ready"), 1)
            for k in range(2 * NT):
                last = t_.matmul(ps[2][:, 0:NB_MAX], in_pos[:, k, :], in_blk[:, k, :], start=k == 0,
                                 stop=k == 2 * NT - 1)
            last.then_inc(sem("slots_summed"), 1)

            pe.wait_ge(sem("blk_ready"), 1)
            pairs = pe.value_load(blki[0:1, NB_MAX:NB_MAX + 1], min_val=NB_MIN // 2, max_val=NB_MAX // 2)
            last_pair = pe.value_load(blki[0:1, NB_MAX + 1:NB_MAX + 2], min_val=NB_MIN // 2 - 1,
                                      max_val=NB_MAX // 2 - 1)

            def x_block(b, q, par):
                pe.wait_ge(sem(f"tok_loaded{par}"), q * 16 + 16)
                for k in range(KD):
                    last = t_.transpose(ps[k // 4][:, (k % 4) * P:(k % 4 + 1) * P], xg[par][:, k * P:(k + 1) * P],
                                        ident)
                last.then_inc(sem("xt_done"), 1)

            def gate_up(b, q, par):
                pe.wait_ge(sem("xT_ready"), b + 1)
                pe.wait_ge(sem(f"gu_loaded{par}"), q * 32 + 32)
                for m, name in enumerate(("g_done", "gu_done")):
                    for k in range(KD):
                        last = t_.matmul(ps[2 + m][:, :], xT[:, k, :], wexp[par][m][:, k, :], start=k == 0,
                                         stop=k == KD - 1)
                    last.then_inc(sem(name), 1)

            def h_block(b):
                pe.wait_ge(sem("hact_ready"), b + 1)
                for k in range(KE):
                    last = t_.transpose(ps[4][:, k * P:(k + 1) * P], hact[:, k * P:(k + 1) * P], ident)
                last.then_inc(sem("ht_done"), 1)

            def down(b, q, par):
                pe.wait_ge(sem("hT_ready"), b + 1)
                pe.wait_ge(sem(f"down_loaded{par}"), q * 16 + 16)
                for n in range(2):
                    for k in range(KE):
                        last = t_.matmul(ps[5 + n][:, :], hT[:, k, :], wexp[par][2][:, k, n * 512:(n + 1) * 512],
                                         start=k == 0, stop=k == KE - 1)
                last.then_inc(sem("down_done"), 1)

            x_block(0, 0, 0)
            gate_up(0, 0, 0)
            x_block(1, 0, 1)
            h_block(0)
            with pe.Fori(1, pairs) as q:
                gate_up(2 * q - 1, q - 1, 1)
                x_block(2 * q, q, 0)
                down(2 * q - 2, q - 1, 0)
                h_block(2 * q - 1)
                gate_up(2 * q, q, 0)
                x_block(2 * q + 1, q, 1)
                pe.wait_ge(sem("y0_ready"), 2 * q - 1)
                pe.wait_ge(sem("y1_ready"), 2 * q - 1)
                down(2 * q - 1, q - 1, 1)
                pe.wait_ge(sem("y0_ready"), 2 * q)
                pe.wait_ge(sem("y1_ready"), 2 * q)
                h_block(2 * q)
            gate_up(last_pair * 2 + 1, last_pair, 1)
            down(last_pair * 2, last_pair, 0)
            h_block(last_pair * 2 + 1)
            pe.wait_ge(sem("y0_ready"), last_pair * 2 + 1)
            pe.wait_ge(sem("y1_ready"), last_pair * 2 + 1)
            down(last_pair * 2 + 1, last_pair, 1)

        @block.scalar
        def _(act):
            s = nc.scalar
            E = Engine(act, "act_chain", ACT_LINKS)

            def copy_group(t, n):
                c0, extra = GROUPS[n]
                E.wait("proj_filled", t, n + 1)
                if extra:
                    s.activation(pj[:, c0:c0 + extra], ps[3][:, 0:extra], ACT.Copy)
                s.activation(pj[:, c0 + extra:c0 + extra + GW], ps[6 + n % 2][:, :], ACT.Copy) \
                    .then_inc(sem("proj_copied"), 1)

            def mixer(i, nxt):
                def group(n):
                    if nxt:
                        copy_group(i + 1, n)

                E.wait("hist", i)
                for k in range(3):
                    E.wait("tconv", i, k + 1)
                    last = s.activation(cb[:, 4 * k:4 * k + 4, 3:131], b4(k), ACT.Copy)
                last.then_inc(sem("cb_in"), 1)
                E.wait("th", i)
                s.activation(he[:, 256:512], ps[3][:, 256:512], ACT.Exp, scale=-1.0)
                s.activation(he[:, 0:256], ps[3][:, 0:256], ACT.Tanh, scale=0.5)
                s.activation(hr, ps[3][:, :], ACT.Copy).then_inc(sem("hraw"), 1)
                E.wait("tr", i)
                s.activation(rqT, b4(4), ACT.Copy).then_inc(sem("rqT"), 1)
                E.wait("dax", i)
                E.link(s.activation(dae, dax, ACT.Exp, scale=-1.0))
                s.activation(beta, pj[:, C_DB:C_DB + 4], ACT.Exp, scale=-1.0)
                s.activation(gt[:, 0:256], pj[:, C_RG:C_RG + 256], ACT.Tanh, scale=0.5)
                s.activation(gt[:, 256:768], pj[:, C_DZ:C_DZ + 512], ACT.Tanh, scale=0.5)
                s.activation(gt[:, 768:1024], pj[:, C_HG:C_HG + 256], ACT.Tanh, scale=0.5).then_inc(sem("gexp"), 1)
                s.activation(dl, dae, ACT.Ln, bias=1.0).then_inc(sem("dl"), 1)
                E.wait("hf", i)
                s.activation(he[:, 0:256], hr[:, 256:512], ACT.Ln).then_inc(sem("hln"), 1)
                group(0)
                E.wait("cy", i)
                s.activation(ce, cy, ACT.Tanh).then_inc(sem("cexp"), 1)
                group(1)
                E.wait("cs", i)
                s.activation(ce[:, 0:1024], cy[:, 0:8, :], ACT.Square).then_inc(sem("csq"), 1)
                E.wait("Dg", i)
                s.activation(Dl, Dl, ACT.Exp)
                s.activation(Dg, Dg, ACT.Exp, scale=-1.0)
                s.activation(eG, gc, ACT.Exp)
                s.activation(ekd, Dm[:, :, P - 1], ACT.Exp)
                s.activation(eGL, b4(0)[:, :, P - 1], ACT.Exp).then_inc(sem("gam"), 1)
                E.wait("rOU", i)
                s.activation(obuf[:, 0:256], ps[1][:, 0:256], ACT.Copy).then_inc(sem("r_out"), 1)
                group(2)
                E.wait("tkh", i)
                s.activation(khT, b4(3), ACT.Copy).then_inc(sem("khT"), 1)
                E.wait("hlev", i)
                s.activation(hE, hE, ACT.Exp)
                s.activation(hqg, hG, ACT.Exp)
                for j in range(2):
                    s.activation(hkd[:, j, :], hG[:, j, :], ACT.Exp, scale=-1.0, bias=hG[:, j, P - 1:P])
                s.activation(ehGL, hG[:, :, P - 1], ACT.Exp).then_inc(sem("hexp"), 1)
                group(3)
                if nxt:
                    E.wait("rot", i)
                group(4)
                E.wait("thk", i)
                s.activation(hkT, ps[3][:, 0:256], ACT.Copy).then_inc(sem("hkT"), 1)
                E.wait("hOU", i)
                s.activation(obuf[:, 768:1024], ps[1][:, 0:256], ACT.Copy, scale=0.5).then_inc(sem("h_out"), 1)
                E.wait("wT", i)
                s.activation(nwT, b4(0), ACT.Copy, scale=-1.0).then_inc(sem("nwT"), 1)
                if nxt:
                    E.wait("gate", i)
                group(5)
                E.wait("vnew", i)
                s.activation(vn, b4(4), ACT.Copy).then_inc(sem("vn"), 1)
                E.wait("od", i)
                s.activation(hQ[:, 0:1024], obuf, ACT.Square).then_inc(sem("o_sq"), 1)
                group(6)
                E.wait("h_ready", i)
                s.activation(hnb, hbuf[:, :], ACT.Square, accum_out=ss2).then_inc(sem("h_sq"), 1)
                group(7)
                E.wait("rt", i)
                s.activation(lg[:, i, :], ps[5][:, 32:68], ACT.Copy).then_inc(sem("logits"), 1)

            act.wait_ge(sem("params_loaded"), N_PARAMS)
            act.wait_ge(sem("lb_shifted"), 1)
            s.activation(lbt[:, 1, :], lbt[:, 0, :], ACT.Exp)
            s.activation(negA, abrow[:, 0:4], ACT.Exp).then_inc(sem("param_exp"), 1)
            E.wait("x_loaded", 0)
            s.activation(x_junk, xin[:, :], ACT.Square, accum_out=ssx[:, 0:1]).then_inc(sem("x_sq"), 1)
            for n in range(NG):
                copy_group(0, n)
                if n == 2:
                    act.wait_ge(sem("x_all_loaded"), 16)
                    for t in range(1, NT):
                        last = s.activation(x_all[:, t, :], x_all[:, t, :], ACT.Square, accum_out=ssx[:, t:t + 1])
                    last.then_inc(sem("x_sq"), 1)
            with act.Fori(0, NT - 1) as i:
                E.start(i * ACT_LINKS)
                mixer(i, True)
                E.end()
            E.start((NT - 1) * ACT_LINKS)
            mixer(NT - 1, False)

            act.wait_ge(sem("r_shift"), 1)
            s.activation(gex, gex, ACT.Exp)
            s.activation(e2, e2, ACT.Exp).then_inc(sem("r_exp"), 1)

            act.wait_ge(sem("y_zeroed"), 64)
            act.wait_ge(sem("blk_ready"), 1)
            pairs = act.value_load(blki[0:1, NB_MAX:NB_MAX + 1], min_val=NB_MIN // 2, max_val=NB_MAX // 2)
            last_pair = act.value_load(blki[0:1, NB_MAX + 1:NB_MAX + 2], min_val=NB_MIN // 2 - 1,
                                      max_val=NB_MAX // 2 - 1)
            act.sem_inc(sem("y_stored0"), 16)
            act.sem_inc(sem("y_stored1"), 16)

            def silu_tanh(b):
                act.wait_ge(sem("g_done"), b + 1)
                s.activation(eg, ps[2][:, :], ACT.Tanh, scale=0.5).then_inc(sem("eg"), 1)

            def h_copy(b):
                act.wait_ge(sem("ht_done"), b + 1)
                s.activation(hT, b4(4), ACT.Copy).then_inc(sem("hT_ready"), 1)

            def y_left(b, q, par):
                act.wait_ge(sem("down_done"), b + 1)
                act.wait_ge(sem(f"y_stored{par}"), q * 16 + 16)
                s.activation(yo[par][:, 0:512], ps[5][:, :], ACT.Copy).then_inc(sem("y0_ready"), 1)

            def y_store(b, par):
                act.wait_ge(sem("y0_ready"), b + 1)
                act.wait_ge(sem("y1_ready"), b + 1)
                act.dma_start(y_d[bass.ds(b * BLK, BLK), :], yo[par]).then_inc(sem(f"y_stored{par}"), 16)

            silu_tanh(0)
            h_copy(0)
            with act.Fori(1, pairs) as q:
                silu_tanh(2 * q - 1)
                y_left(2 * q - 2, q - 1, 0)
                h_copy(2 * q - 1)
                y_store(2 * q - 2, 0)
                silu_tanh(2 * q)
                y_left(2 * q - 1, q - 1, 1)
                h_copy(2 * q)
                y_store(2 * q - 1, 1)
            silu_tanh(last_pair * 2 + 1)
            y_left(last_pair * 2, last_pair, 0)
            h_copy(last_pair * 2 + 1)
            y_store(last_pair * 2, 0)
            y_left(last_pair * 2 + 1, last_pair, 1)
            y_store(last_pair * 2 + 1, 1)

            for t in range(NT):
                act.wait_ge(sem("c_sum"), t + 1)
                s.activation(cm_y1[t], cm_h[:, t, :], ACT.Square, accum_out=ssx[:, t:t + 1]).then_inc(sem("c_sq"), 1)
                if t >= 3 and t % 2 == 1:
                    for o in (t - 3, t - 2):
                        act.wait_ge(sem("c_out"), o + 1)
                        act.dma_start(out_v[o], cm_h[:, o, :]).then_inc(sem("out_stored"), 16)
            for o in (NT - 2, NT - 1):
                act.wait_ge(sem("c_out"), o + 1)
                act.dma_start(out_v[o], cm_h[:, o, :]).then_inc(sem("out_stored"), 16)
            act.wait_ge(sem("out_stored"), 16 * NT)

        @block.vector
        def _(dve):
            v = nc.vector
            E = Engine(dve, "dve_chain", DVE_LINKS)
            link = E.link

            def tt(o, x, y, op):
                return v.tensor_tensor(o, x, y, op)

            def rsqrt(m, y, tmp, link=link):
                link(v.tensor_scalar(y.bitcast(I32), m.bitcast(I32), -0.5, RSQRT_MAGIC, ALU.mult, ALU.add))
                for step in range(3):
                    link(v.scalar_tensor_tensor(tmp, y, -0.5, y, ALU.mult, ALU.mult))
                    link(tt(tmp, tmp, m, ALU.mult))
                    link(v.scalar_tensor_tensor(y, tmp, 1.5, y, ALU.add, ALU.mult))

            def x_norm(t0, t1):
                link(v.tensor_scalar(mx[:, t0:t1], ssx[:, t0:t1], 1.0 / DM, EPS, ALU.mult, ALU.add))
                rsqrt(mx[:, t0:t1], rx[:, t0:t1], tx_[:, t0:t1])

            def x_scale(t, r):
                E.wait("x_loaded", t)
                v.tensor_scalar(junk[:, :], xin[:, :], r, None, ALU.mult).then_inc(sem("xsc"), 1)

            def x_gain(t):
                E.wait("tx", t)
                tt(xnT[:, 0:4, :], b4(6), bc(g1c[:, 0:4], P), ALU.mult)
                tt(xnT[:, 4:8, :], b4(7), bc(g1c[:, 4:8], P), ALU.mult).then_inc(sem("xnT"), 1)

            def mixer(i, nxt):
                if nxt:
                    x_scale(i + 1, rx[:, bass.ds(i + 1, 1)])
                E.wait("proj_copied", i)
                da = pj[:, C_DA:C_DA + 4]
                link(tt(dxx, da, abrow[:, 4:8], ALU.add))
                v.scalar_tensor_tensor(dax, dxx, -1.0, dxx, ALU.mult, ALU.max).then_inc(sem("dax"), 1)
                E.wait("rot_loaded", i)
                qk = pj[:, 0:512].rearrange("p (h d) -> p h d", h=8)
                ro = rot.rearrange("p (h d) -> p h d", h=8)
                rt = rtmp.rearrange("p a b -> p (a b)").rearrange("p (h d) -> p h d", h=8)
                tt(ro, qk, heads(rtab[:, 0:64], 8), ALU.mult)
                tt(rt[:, :, 0:32], qk[:, :, 32:64], heads(rtab[:, 64:96], 8), ALU.mult)
                link(tt(rt[:, :, 32:64], qk[:, :, 0:32], heads(rtab[:, 96:128], 8), ALU.mult))
                tt(ro, ro, rt, ALU.add).then_inc(sem("rot"), 1)
                if nxt:
                    x_gain(i + 1)
                E.wait("hraw", i)
                link(v.tensor_scalar(he[:, 256:512], he[:, 256:512], 1.0, None, ALU.add))
                link(v.reciprocal(he[:, 256:512], he[:, 256:512]))
                for j in range(2):
                    last = v.tensor_scalar(hr[:, 256 + P * j:384 + P * j], he[:, 256 + P * j:384 + P * j],
                                           oml[:, j:j + 1], lbv[:, j:j + 1], ALU.mult, ALU.add)
                link(last)
                v.scalar_tensor_tensor(hr[:, 0:256], he[:, 0:256], 1.0, hr[:, 0:256], ALU.add, ALU.mult)
                link(v.tensor_scalar(he[:, 256:512], hr[:, 256:512], -1.0, 1.0, ALU.mult, ALU.add))
                v.tensor_scalar(hr[:, 256:512], hr[:, 256:512], 2.0 ** -64, None, ALU.max).then_inc(sem("hf"), 1)
                E.wait("cb_in", i)
                for j in range(4):
                    for k in range(12):
                        if j == 0:
                            last = v.tensor_scalar(cy[:, k, :], cb[:, k, 0:P], convw[:, 0, k:k + 1], None, ALU.mult)
                        else:
                            last = v.scalar_tensor_tensor(cy[:, k, :], cb[:, k, j:j + P], convw[:, j, k:k + 1],
                                                          cy[:, k, :], ALU.mult, ALU.add)
                    if j < 3:
                        link(last)
                last.then_inc(sem("cy"), 1)
                v.tensor_copy(cb[:, :, 0:3], cb[:, :, 128:131]).then_inc(sem("hist"), 1)
                E.wait("dl", i)
                link(v.scalar_tensor_tensor(dl, dxx, 0.0, dl, ALU.max, ALU.add))
                link(tt(gcol, dl, negA, ALU.mult))
                v.tensor_copy(gBr, bc(gcol, P)).then_inc(sem("gBr"), 1)
                link(v.tensor_scalar(beta, beta, 1.0, None, ALU.add))
                link(v.reciprocal(beta, beta))
                E.wait("cexp", i)
                cyf = cy.rearrange("p a b -> p (a b)")
                v.scalar_tensor_tensor(cyf, ce, 1.0, cyf, ALU.add, ALU.mult).then_inc(sem("cs"), 1)
                E.wait("rot", i)
                tt(rkz, rot[:, 256:512], cn("zeta"), ALU.mult)
                E.wait("rqT", i)
                tt(rqX, rqT[:, 0:2, :], three(cn("xi"), 2, P), ALU.mult).then_inc(sem("rqX"), 1)
                E.wait("rS", i)
                for q in range(2):
                    last = tt(rA[:, 2 * q:2 * q + 2, :], three(ps[1 + q][:, 0:256], 2, P),
                              three(cn("dmat")[:, 256 * q:256 * q + 256], 2, P), ALU.mult)
                last.then_inc(sem("rA"), 1)
                E.wait("Gsum", i)
                v.tensor_copy(gc, ps[5][:, 0:4]).then_inc(sem("gc"), 1)
                E.wait("gc", i)
                link(tt(Dm, b4(0), bc(gc, P), ALU.subtract))
                link(v.tensor_scalar(Dl, Dm, 0.0, None, ALU.min))
                tt(Dl, Dl, heads(cn("neg_up"), 4), ALU.add)
                link(v.tensor_scalar(Dg, Dm, 0.0, None, ALU.max))
                tt(Dg, Dg, heads(cn("pos_low"), 4), ALU.add).then_inc(sem("Dg"), 1)
                E.wait("ssq", i)
                link(v.tensor_scalar(mqk, ps[5][:, 8:16], 1.0, EPS, ALU.mult, ALU.add))
                rsqrt(mqk, rqk, tqk)
                E.wait("ktok", i)
                tt(khat, b4(3), bc(rqk[:, 4:8], P), ALU.mult).then_inc(sem("khat"), 1)
                E.wait("vtok", i)
                tt(vb, b4(4), bc(beta, P), ALU.mult).then_inc(sem("vb"), 1)
                E.wait("hln", i)
                for j in range(2):
                    last = v.tensor_tensor_scan(hG[:, j, :], cn("ones"), he[:, j * P:(j + 1) * P], 0.0, ALU.mult,
                                                ALU.add)
                link(last)
                hGf = hG.rearrange("p a b -> p (a b)")
                for l in range(LEVELS):
                    m = 2 ** l
                    g3 = hGf.rearrange("p (n b) -> p n b", b=2 * m)
                    last = tt(hE[:, 256 * l:256 * l + 256].rearrange("p (n b) -> p n b", b=2 * m), g3,
                              bc(g3[:, :, m - 1], 2 * m), ALU.subtract)
                link(last)
                v.scalar_tensor_tensor(hE, hE, -1.0, hE, ALU.mult, ALU.min).then_inc(sem("hlev"), 1)
                E.wait("gam", i)
                E.wait("kk", i)
                link(tt(A, b4(4), Dg, ALU.mult))
                tt(A, A, bc(beta, P), ALU.mult).then_inc(sem("A"), 1)
                link(tt(bG, beta, eG, ALU.mult))
                E.wait("A", i)
                link(tt(T, A, heads(cn("m0neg"), 4), ALU.mult))
                tt(T, T, heads(ident, 4), ALU.add)
                E.wait("tA", i)
                link(tt(U, b4(3), heads(cn("m0negT"), 4), ALU.mult))
                E.wait("qk", i)
                tt(qkm, b4(0), Dl, ALU.mult)
                tt(U, U, heads(ident, 4), ALU.add).then_inc(sem("UT"), 1)
                E.wait("hexp", i)
                hE3, hQ3 = three(hE, LEVELS, 256), three(hQ, LEVELS, 256)
                tt(hQ3, hE3, heads(hr[:, 0:256], LEVELS), ALU.mult)
                tt(hqg, hqg, three(hr[:, 0:256], 2, P), ALU.mult)
                link(tt(hkd, hkd, three(he[:, 256:512], 2, P), ALU.mult))
                tt(hE3, hE3, heads(he[:, 256:512], LEVELS), ALU.mult).then_inc(sem("hKQ"), 1)
                E.wait("khat", i)
                tt(kb, khat, bc(bG, P), ALU.mult)
                tt(kdec, khat, bc(ekd, P), ALU.mult)
                E.wait("rOU", i)
                link(tt(SrB, SrB, bc(cn("rdec"), P), ALU.mult))
                link(tt(three(rkz, 2, P), three(ps[2][:, 0:256], 2, P), heads(cn("pair"), 2), ALU.mult))
                tt(SrB, SrB, three(rkz, 2, P), ALU.add).then_inc(sem("r_state"), 1)
                for l in range(1, LEVELS):
                    E.wait("Z", i, l)
                    tt(Zs, b4(0), heads(cn("lev")[:, l * P:(l + 1) * P], 4), ALU.mult).then_inc(sem("Zs"), 1)
                    if l == 1:
                        link(v.memset(hatt, 0.0))
                    if l <= 4:
                        E.wait("hA", i, l)
                        lev = 2 * (l - 1)
                        mask0 = heads(cn("lev")[:, lev * P:(lev + 1) * P], 2)
                        mask1 = heads(cn("lev")[:, (lev + 1) * P:(lev + 2) * P].bitcast(I32), 2)
                        for q in range(2):
                            last = tt(khat[:, 2 * q:2 * q + 2, :], three(ps[1 + q][:, 0:256], 2, P), mask0, ALU.mult)
                        for q in range(2):
                            last = v.copy_predicated(hatt[:, 2 * q:2 * q + 2, :], mask1,
                                                     three(ps[1 + q][:, 256:512], 2, P))
                        link(last)
                        last = tt(hatt, hatt, khat, ALU.add)
                        last.then_inc(sem("hatt"), 1)
                    E.wait("dU", i, l)
                    last = tt(U, U, b4(4), ALU.subtract)
                    if l < LEVELS - 1:
                        E.wait("dT", i, l)
                        last = tt(T, T, b4(5), ALU.subtract)
                    last.then_inc(sem("UT"), 1)
                    if l == 5:
                        E.wait("gexp", i)
                        for g0, c0, w in ((0, C_RG, 256), (256, C_DZ, 512), (768, C_HG, 256)):
                            last = v.scalar_tensor_tensor(gt[:, g0:g0 + w], gt[:, g0:g0 + w], 1.0,
                                                          pj[:, c0:c0 + w], ALU.add, ALU.mult)
                        last.then_inc(sem("gate"), 1)
                E.wait("hOU", i)
                link(tt(ShB, ShB, bc(ehGL, P), ALU.mult))
                link(tt(three(he[:, 0:256], 2, P), three(ps[2][:, 0:256], 2, P), heads(cn("pair"), 2), ALU.mult))
                link(tt(ShB, ShB, three(he[:, 0:256], 2, P), ALU.add))
                link(v.tensor_scalar(sg4, rqk[:, 0:4], 128.0 ** -0.5, None, ALU.mult))
                od = three(obuf[:, 256:768], 4, P)
                E.wait("o1", i)
                link(tt(od, b4(5), bc(eG, P), ALU.mult))
                E.wait("o2", i)
                link(tt(od, od, b4(0), ALU.add))
                E.wait("r_out", i)
                E.wait("h_out", i)
                tt(od, od, bc(sg4, P), ALU.mult).then_inc(sem("od"), 1)
                link(tt(S, S, bc(eGL, P), ALU.mult))
                E.wait("od", i)
                tt(gt, obuf, gt, ALU.mult)
                E.wait("o_sq", i)
                link(v.reduce_sum(sh, hQ[:, 0:1024].rearrange("p (a b) -> p a b", a=16), AX.X))
                link(v.reduce_sum(th_[:, 0:4], sh[:, 4:12].rearrange("p (a b) -> p a b", a=4), AX.X))
                link(v.tensor_scalar(mh, sh, 1.0 / 64, EPS, ALU.mult, ALU.add))
                link(v.tensor_scalar(mh[:, 4:12].rearrange("p (a b) -> p a b", a=4), bc(th_[:, 0:4], 2), 1.0 / P,
                                     EPS, ALU.mult, ALU.add))
                rsqrt(mh, rh, th_)
                tt(obuf.rearrange("p (a b) -> p a b", a=16), gt.rearrange("p (a b) -> p a b", a=16), bc(rh, 64),
                   ALU.mult).then_inc(sem("mixed"), 1)
                E.wait("dS", i)
                link(tt(S, S, b4(3), ALU.add))
                E.wait("tm", i, 1)
                tt(mT[:, 0:4, :], b4(1), bc(gmc[:, 0:4], P), ALU.mult)
                E.wait("tm", i)
                tt(mT[:, 4:8, :], b4(2), bc(gmc[:, 4:8], P), ALU.mult).then_inc(sem("mT"), 1)
                E.wait("xres_loaded", i)
                E.wait("wo", i)
                tt(hbuf[:, 0:512], hbuf[:, 0:512], ps[4][:, :], ALU.add)
                tt(hbuf[:, 512:1024], hbuf[:, 512:1024], ps[5][:, :], ALU.add).then_inc(sem("h_ready"), 1)
                E.wait("h_sq", i)
                link(v.tensor_scalar(m2, ss2, 1.0 / DM, EPS, ALU.mult, ALU.add))
                rsqrt(m2, r2, t2)
                v.tensor_scalar(hnb, hbuf[:, :], r2, None, ALU.mult).then_inc(sem("hn_ready"), 1)
                E.wait("t2", i, 1)
                tt(mT[:, 0:4, :], b4(0), bc(g2c[:, 0:4], P), ALU.mult)
                E.wait("t2", i)
                tt(mT[:, 4:8, :], b4(3), bc(g2c[:, 4:8], P), ALU.mult).then_inc(sem("h2T"), 1)

            dve.wait_ge(sem("params_loaded"), N_PARAMS)
            v.tensor_tensor(lbt[:, 0, :], lbc[:, :], lbc[:, :], ALU.subtract).then_inc(sem("lb_shifted"), 1)
            dve.wait_ge(sem("param_exp"), 1)
            link(v.reciprocal(lbt[:, 2, :], lbt[:, 1, :]))
            link(v.tensor_tensor(lbt[:, 3, :], lbt[:, 1, :], lbt[:, 2, :], ALU.mult))
            link(v.tensor_tensor(lbv, lbt[:, 3, :], lbt[:, 3, :], ALU.subtract))
            v.tensor_scalar(oml, lbv, -1.0, 1.0, ALU.mult, ALU.add)
            v.tensor_scalar(negA, negA, -1.0, None, ALU.mult)
            v.tensor_scalar(convw[:, :, :], convw[:, :, :], 0.5, None, ALU.mult)
            v.tensor_scalar(gmc[:, :], gmc[:, :], 0.5, None, ALU.mult)
            v.memset(cb[:, :, 0:3], 0.0).then_inc(sem("hist"), 1)
            v.memset(SrB, 0.0)
            v.memset(ShB, 0.0)
            v.memset(S, 0.0).then_inc(sem("zeroed"), 1)
            dve.wait_ge(sem("x_sq"), 1)
            x_norm(0, 1)
            x_scale(0, rx[:, 0:1])
            x_gain(0)
            dve.wait_ge(sem("x_sq"), 2)
            x_norm(1, NT)
            SETUP = E.c
            with dve.Fori(0, NT - 1) as i:
                E.start(i * DVE_LINKS + SETUP)
                mixer(i, True)
                E.end()
            E.start((NT - 1) * DVE_LINKS + SETUP)
            mixer(NT - 1, False)

            chain = [0]

            def seq(ins):
                chain[0] += 1
                ins.then_inc(sem("route_chain"), 1)
                dve.wait_ge(sem("route_chain"), chain[0])

            def first_of(onehot, values, top, width):
                io = cn("iota")[:, 0:width]
                seq(tt(onehot, values, bc(top, width), ALU.is_equal))
                seq(tt(onehot, onehot, heads(io, NT), ALU.mult))
                seq(v.tensor_reduce(ri, onehot, AX.X, ALU.min))
                seq(tt(onehot, heads(io, NT), bc(ri, width), ALU.is_equal))

            dve.wait_ge(sem("logits"), NT)
            gl = lg[:, :, 0:NGRP]
            seq(v.reduce_max(gm, gl, AX.X))
            seq(tt(gex, gl, bc(gm, NGRP), ALU.subtract))
            first_of(goh, gl, gm, NGRP)
            seq(v.tensor_scalar(goh, goh, BIG, -BIG, ALU.mult, ALU.add))
            seq(tt(el.rearrange("p t (g e) -> p t g e", g=NGRP),
                   lg[:, :, NGRP:].rearrange("p t (g e) -> p t g e", g=NGRP), bc(goh, EPG), ALU.add))
            seq(v.reduce_max(m1, el, AX.X))
            first_of(oh1, el, m1, NE)
            seq(tt(cnd, oh1, oh1, ALU.mult))
            elf, cf = (x.rearrange("p a b -> p (a b)") for x in (el, cnd))
            seq(v.scalar_tensor_tensor(elf, cf, -BIG, elf, ALU.mult, ALU.add))
            seq(v.reduce_max(m2_, el, AX.X))
            first_of(oh2, el, m2_, NE)
            tt(e2, m2_, m1, ALU.subtract).then_inc(sem("r_shift"), 1)
            seq(tt(cnd, oh1, oh2, ALU.add))
            dve.wait_ge(sem("y_zeroed"), 64)
            seq(v.memset(mrun[:, 0, :], 0.0))
            for t in range(NT):
                seq(tt(mrun[:, t + 1, :], mrun[:, t, :], cnd[:, t, :], ALU.add))
            v.engine_nop().then_inc(sem("picked"), 1)
            dve.wait_ge(sem("r_exp"), 1)
            seq(v.reduce_sum(gm, gex, AX.X))
            seq(v.reciprocal(gm, gm))
            seq(v.tensor_scalar(m1, e2, 1.0, None, ALU.add))
            seq(v.reciprocal(m1, m1))
            seq(tt(w12[:, 0, :], gm, m1, ALU.mult))
            seq(tt(w12[:, 1, :], w12[:, 0, :], e2, ALU.mult))
            dve.wait_ge(sem("ranks"), 1)
            seq(v.tensor_copy(cnt, ps[1][:, 0:32]))
            c8 = cmp_[:, 0:256].rearrange("p (a b) -> p a b", a=32)
            seq(tt(c8, bc(cnt, 8), heads(cn("c128"), 32), ALU.is_gt))
            seq(v.reduce_sum(nblk, c8, AX.X))
            seq(v.tensor_tensor_scan(incl, cn("ones")[:, 0:32], nblk, 0.0, ALU.mult, ALU.add))
            c48 = cmp_.rearrange("p (a b) -> p a b", a=NB_MAX)
            seq(tt(c48, heads(incl, NB_MAX), bc(cn("biota"), NE), ALU.is_le))
            seq(v.reduce_sum(blkt[:, 0:NB_MAX], c48, AX.X))
            seq(v.tensor_scalar(blkt[:, 0:NB_MAX], blkt[:, 0:NB_MAX], float(NE - 1), None, ALU.min))
            seq(v.tensor_scalar(cmp_[:, 0:NB_MAX // 2], cn("biota")[:, 0:NB_MAX // 2], 2.0, incl[:, NE - 1:NE],
                                ALU.mult, ALU.is_lt))
            seq(v.reduce_sum(blkt[:, NB_MAX:NB_MAX + 1], cmp_[:, 0:NB_MAX // 2], AX.X))
            seq(v.tensor_scalar(blkt[:, NB_MAX + 1:NB_MAX + 2], blkt[:, NB_MAX:NB_MAX + 1], -1.0, None, ALU.add))
            v.tensor_copy(blki[:, :], blkt[:, :]).then_inc(sem("blk_ready"), 1)
            seq(tt(base, incl, nblk, ALU.subtract))
            seq(v.tensor_scalar(base, base, float(BLK), None, ALU.mult))
            seq(tt(rk, ps[0][:, 0:256].rearrange("p (a b) -> p a b", a=NT), heads(base, NT), ALU.add))
            for k, oh in enumerate((oh1, oh2)):
                seq(tt(el, oh, rk, ALU.mult))
                seq(v.reduce_sum(dst[:, k, :], el, AX.X))
            dsf = dst[:, :, :].rearrange("p a b -> p (a b)")
            seq(v.tensor_copy(dsti[:, :, :].rearrange("p a b -> p (a b)"), dsf))
            dsi = dsti[:, :, :].rearrange("p a b -> p (a b)")
            v.tensor_scalar(posi, dsi, BLK - 1, None, ALU.bitwise_and)
            seq(v.tensor_scalar(blockn, dsi, BLK.bit_length() - 1, None, ALU.logical_shift_right))
            v.tensor_copy(blockf, blockn)
            seq(v.tensor_copy(posf, posi))
            v.tensor_scalar(tokf, cn("c128"), cn("pcol"), None, ALU.add)
            v.tensor_scalar(posf, posf, 1.0, None, ALU.add)
            seq(v.tensor_tensor_scan(count_row, cn("ones"), cn("ones"), 0.0, ALU.mult, ALU.add))
            seq(tt(in_blk, heads(cn("biota"), 2 * NT), bc(blockf, NB_MAX), ALU.is_equal))
            for k in range(2):
                seq(tt(in_blk[:, k * NT:(k + 1) * NT, :], in_blk[:, k * NT:(k + 1) * NT, :], bc(tokf, NB_MAX),
                       ALU.mult))
            tt(in_pos, heads(count_row, 2 * NT), bc(posf, P), ALU.is_equal).then_inc(sem("dst_ready"), 1)
            dve.wait_ge(sem("slots_summed"), 1)
            v.tensor_copy(slots[:, :], ps[2][:, 0:NB_MAX]).then_inc(sem("slots_ready"), 1)
            dve.wait_ge(sem("blk_ready"), 1)
            pairs = dve.value_load(blki[0:1, NB_MAX:NB_MAX + 1], min_val=NB_MIN // 2, max_val=NB_MAX // 2)
            last_pair = dve.value_load(blki[0:1, NB_MAX + 1:NB_MAX + 2], min_val=NB_MIN // 2 - 1,
                                      max_val=NB_MAX // 2 - 1)

            def x_gain2(b):
                dve.wait_ge(sem("xt_done"), b + 1)
                tt(xT[:, 0:4, :], b4(0), bc(g2c[:, 0:4], P), ALU.mult)
                tt(xT[:, 4:8, :], b4(1), bc(g2c[:, 4:8], P), ALU.mult).then_inc(sem("xT_ready"), 1)

            def swiglu(b):
                dve.wait_ge(sem("eg"), b + 1)
                v.scalar_tensor_tensor(eg, eg, 1.0, ps[2][:, :], ALU.add, ALU.mult).then_inc(sem("swiglu_step"), 1)
                dve.wait_ge(sem("swiglu_step"), b + 1)
                dve.wait_ge(sem("gu_done"), b + 1)
                v.scalar_tensor_tensor(hact, eg, 0.5, ps[3][:, :], ALU.mult, ALU.mult) \
                    .then_inc(sem("hact_ready"), 1)

            def y_right(b, q, par):
                dve.wait_ge(sem("down_done"), b + 1)
                dve.wait_ge(sem(f"y_stored{par}"), q * 16 + 16)
                v.tensor_copy(yo[par][:, 512:1024], ps[6][:, :]).then_inc(sem("y1_ready"), 1)

            x_gain2(0)
            swiglu(0)
            x_gain2(1)
            with dve.Fori(1, pairs) as q:
                swiglu(2 * q - 1)
                x_gain2(2 * q)
                y_right(2 * q - 2, q - 1, 0)
                swiglu(2 * q)
                x_gain2(2 * q + 1)
                y_right(2 * q - 1, q - 1, 1)
            swiglu(last_pair * 2 + 1)
            y_right(last_pair * 2, last_pair, 0)
            y_right(last_pair * 2 + 1, last_pair, 1)

            dve.wait_ge(sem("ch_loaded"), 32)
            cc = [0]

            def cseq(ins):
                cc[0] += 1
                ins.then_inc(sem("comb_chain"), 1)
                dve.wait_ge(sem("comb_chain"), cc[0])

            def normed(t):
                dve.wait_ge(sem("c_sq"), t + 2)
                two = slice(t, t + 2)
                cseq(v.tensor_scalar(mx[:, two], ssx[:, two], 1.0 / DM, EPS, ALU.mult, ALU.add))
                rsqrt(mx[:, two], rx[:, two], tx_[:, two], cseq)
                for o in (t, t + 1):
                    v.scalar_tensor_tensor(cm_h[:, o, :], cm_h[:, o, :], rx[:, o:o + 1], fgain, ALU.mult, ALU.mult) \
                        .then_inc(sem("c_out"), 1)

            for t in range(NT):
                dve.wait_ge(sem(f"rows_loaded{t}"), 32)
                hrow = cm_h[:, t, :]
                cseq(v.scalar_tensor_tensor(hrow, cm_y1[t], w12[:, 0, t:t + 1], hrow, ALU.mult, ALU.add))
                v.scalar_tensor_tensor(hrow, cm_y2[t], w12[:, 1, t:t + 1], hrow, ALU.mult, ALU.add) \
                    .then_inc(sem("c_sum"), 1)
                if t >= 2 and t % 2 == 0:
                    normed(t - 2)
            normed(NT - 2)

        @block.gpsimd
        def _(pool):
            g = nc.gpsimd
            g.memset(zrow, 0.0).then_inc(sem("zeros"), 1)
            pool.wait_ge(sem("zeros"), 1)
            pool.wait_ge(sem("xsc"), 2)
            spare = y_d[NB_MIN * BLK:, :].rearrange("(p a) (h c) -> p (a h) c", p=P, c=256)
            rows = spare.shape[1] // 4
            for k in range(4):
                pool.dma_start(spare[:, k * rows:(k + 1) * rows, :],
                               heads(zrow, rows)).then_inc(sem("y_zeroed"), 16)
            pool.wait_ge(sem("y_zeroed"), 64)
            pool.wait_ge(sem("slots_ready"), 1)
            pool.wait_ge(sem("hn_stored"), 32 * NT)
            pool.wait_ge(sem("blk_ready"), 1)
            pairs = pool.value_load(blki[0:1, NB_MAX:NB_MAX + 1], min_val=NB_MIN // 2, max_val=NB_MAX // 2)

            def gather(b, par, first):
                if not first:
                    pool.wait_ge(sem("xt_done"), b - 1)
                g.tensor_copy(idxs[par][:, :], slots[:, bass.ds(b, 1)]).then_inc(sem("idx_ready"), 1)
                pool.wait_ge(sem("idx_ready"), b + 1)
                pool.sem_inc(sem("idx_seen"), 1)
                g.indirect_dma_start(xg[par], None, hn_d, bass.IndirectOffsetOnAxis(ap=idxs[par][:, :], axis=0)) \
                    .then_inc(sem(f"tok_loaded{par}"), 16)

            gather(0, 0, True)
            gather(1, 1, True)
            with pool.Fori(1, pairs) as q:
                gather(2 * q, 0, False)
                gather(2 * q + 1, 1, False)

            pool.wait_ge(sem("y_stored0"), pairs * 16 + 16)
            pool.wait_ge(sem("y_stored1"), pairs * 16 + 16)
            pool.sem_inc(sem("idx_seen"), 1)
            for t in range(NT):
                for k, rows in enumerate((cm_y1, cm_y2)):
                    g.indirect_dma_start(rows[t], None, y_d,
                                         bass.IndirectOffsetOnAxis(ap=dsti[:, k, t:t + 1], axis=0)) \
                        .then_inc(sem(f"rows_loaded{t}"), 16)


IN_NAMES = ("x", "w_in", "w_out", "gdn_conv", "gdn_a_log", "gdn_dt_bias", "ret_norm", "gdn_norm", "hgrn_norm",
            "hgrn_lower_bounds", "attn_norm", "ffn_norm", "router_group", "router_expert", "w_gate", "w_up", "w_down",
            "final_norm")


def kernel(**inputs):
    import numpy as _np
    import concourse.bacc as _bacc
    from concourse import mybir as _mybir
    from concourse.bass_utils import run_bass_kernel_spmd as _run

    nc = _bacc.Bacc("TRN2", target_bir_lowering=False, num_devices=1)
    arrays, aps = {}, {}
    given = {n: _np.ascontiguousarray(inputs[n]) for n in IN_NAMES}
    given["consts"] = host_consts()
    given["rotary"] = host_rotary()
    for name, arr in given.items():
        arrays[f"in_{name}"] = arr
        aps[name] = nc.dram_tensor(f"in_{name}", arr.shape, _mybir.dt.from_np(arr.dtype), kind="ExternalInput").ap()
    out = nc.dram_tensor("out_0", (1, SEQ, DM), F32, kind="ExternalOutput").ap()
    hn_d = nc.dram_tensor("hn_rows", (SEQ, DM), F32, kind="Internal").ap()
    h_d = nc.dram_tensor("h_rows", (SEQ, DM), F32, kind="Internal").ap()
    y_d = nc.dram_tensor("y_rows", (NB_MAX * BLK, DM), F32, kind="Internal").ap()
    build(nc, aps, out, hn_d, h_d, y_d)
    r = _run(nc, [arrays], core_ids=[0])
    return r.results[0]["out_0"]
```

```python
from contextlib import ExitStack

import numpy as np
import concourse.bass as bass
from concourse import mybir

F32 = mybir.dt.float32
I32 = mybir.dt.int32
ALU = mybir.AluOpType
ACT = mybir.ActivationFunctionType
AX = mybir.AxisListType

P = 128
SEQ = 1024
DM = 1024
NT = SEQ // P
KD = DM // P
IN_W = 4104
C_RQ, C_RV, C_RG = 0, 512, 768
C_DQ, C_DA, C_DB, C_DZ = 1024, 2560, 2564, 2568
C_HQ, C_HI, C_HG = 3080, 3592, 3848
GROUPS = ((1024, 384), (1408, 384), (1792, 384), (2176, 384), (3080, 512), (0, 512), (2560, 260), (2820, 260),
          (512, 512), (3592, 512))
NG = len(GROUPS)
NE, NGRP, EPG, DE = 32, 4, 8, 512
KE = DE // P
BLK = 128
NB_MAX = 48
NB_MIN = 16
EPS = 1e-6
BIG = 1e30
LEVELS = 7
RSQRT_MAGIC = float(0x5F3759DF)
RET_GAMMA = [1.0 - 2.0 ** (-5.0 - h) for h in range(4)]


def const_layout():
    at, off = {}, 0
    for name, n in (("ident", 128), ("tri", 128), ("dmat", 512), ("xi", 256), ("zeta", 256), ("rdec", 2),
                    ("pair", 128), ("neg_up", 128), ("pos_low", 128), ("m0neg", 128), ("m0negT", 128),
                    ("lev", 8 * 128), ("ones", 128), ("stri", 128), ("iota", 32), ("biota", NB_MAX), ("pcol", 1),
                    ("c128", 8)):
        at[name] = (off, n)
        off += n
    return at, off


def host_consts():
    at, n = const_layout()
    c = np.zeros((P, n), np.float32)

    def put(name, a):
        o, w = at[name]
        c[:, o:o + w] = np.asarray(a, np.float32).reshape(P, w)

    p, f = np.arange(P)[:, None], np.arange(P)[None, :]
    put("ident", p == f)
    put("tri", p <= f)
    put("stri", p < f)
    put("ones", np.ones((P, P)))
    lg = np.log(np.array(RET_GAMMA))
    d = np.zeros((P, 4, P))
    for h in range(4):
        d[:, h] = np.where(f >= p, np.exp(lg[h] * np.maximum(f - p, 0)), 0) * 0.125
    put("dmat", d[:, [0, 2, 1, 3]])
    xi = np.zeros((P, 2, P))
    dec = np.zeros((P, 2))
    for j in range(2):
        for q in range(2):
            xi[64 * q:64 * q + 64, j] = np.exp(lg[2 * j + q] * (np.arange(P) + 1))[None]
            dec[64 * q:64 * q + 64, j] = np.exp(lg[2 * j + q] * P)
    put("xi", xi)
    put("rdec", dec)
    put("zeta", np.repeat(np.exp(lg[None] * (P - 1 - np.arange(P))[:, None]) * 0.125, 64, axis=1))
    put("pair", (p // 64) == (f // 64))
    put("neg_up", np.where(f >= p, 0, -BIG))
    put("pos_low", np.where(f < p, 0, BIG))
    lev = np.zeros((P, 8, P))
    for l in range(LEVELS):
        m = 2 ** l
        lev[:, l] = (p // (2 * m) == f // (2 * m)) & (p % (2 * m) < m) & (f % (2 * m) >= m)
    lev[:, 7] = p == f
    put("lev", lev)
    put("m0negT", -lev[:, 0])
    put("m0neg", -lev[:, 0].T)
    put("iota", np.broadcast_to(np.arange(32) - 64, (P, 32)))
    put("biota", np.broadcast_to(np.arange(NB_MAX), (P, NB_MAX)))
    put("pcol", np.arange(P))
    put("c128", np.broadcast_to(np.arange(8) * BLK, (P, 8)))
    return c


def host_rotary():
    inv = (np.float32(10000.0) ** (-np.arange(0, 64, 2, dtype=np.float32) / np.float32(64))).astype(np.float32)
    ang = np.arange(SEQ, dtype=np.float32)[:, None] * inv[None]
    cos, sin = np.cos(ang), np.sin(ang)
    return np.concatenate([cos, cos, -sin, sin], axis=1).astype(np.float32)


def bc(ap, n):
    return ap.unsqueeze(ap.ndim).to_broadcast(list(ap.shape) + [n])


def heads(ap, n):
    return ap.unsqueeze(1).to_broadcast([ap.shape[0], n, ap.shape[1]])


def build(nc, a, out, hn_d, h_d, y_d):
    ctx = ExitStack()
    with ctx:
        def sb(name, shape, dt=F32):
            return ctx.enter_context(nc.sbuf_tensor(name, shape, dt))

        sems = {}

        def sem(name):
            if name not in sems:
                sems[name] = ctx.enter_context(nc.semaphore(name))
            return sems[name]

        C_AT, C_N = const_layout()
        cst = sb("cst", [P, C_N])

        def cn(name):
            o, w = C_AT[name]
            return cst[:, o:o + w]

        ident = cn("ident")
        g1c = sb("g1c", [P, KD])
        g2c = sb("g2c", [P, KD])
        gmc = sb("gmc", [P, KD])
        convw = sb("convw", [P, 4, 12])
        abrow = sb("abrow", [P, 8])
        lbc = sb("lbc", [P, 2])
        lbw = sb("lbw", [P, 4, 2])
        wr = sb("wr", [P, KD, 36])
        xin = sb("xin", [P, DM])
        junk = sb("junk", [P, DM])
        hbuf = sb("hbuf", [P, DM])
        sc = sb("sc", [P, 192])
        lg = sb("lg", [P, NT, 36])

        BIG_N = 45400
        big = sb("big", [P, BIG_N])
        used = [0]

        def part(n):
            o = used[0]
            used[0] += n
            assert used[0] <= BIG_N, used[0]
            return big[:, o:o + n]

        def three(ap, x, y):
            return ap.rearrange("p (a b) -> p a b", a=x, b=y)

        wg = [part(KD * max(w for _, w in GROUPS)) for _ in range(2)]
        wout = three(part(KD * DM), KD, DM)
        pj = part(IN_W)
        cb = three(part(12 * 131), 12, 131)
        cy = three(part(1536), 12, 128)
        ce = part(1536)
        xnT = three(part(1024), KD, P)
        gt = part(1024)
        rot = part(512)
        rtab = part(128)
        rqT = three(part(512), 4, P)
        rqX = three(part(256), 2, P)
        rkz = part(256)
        rA = three(part(512), 4, P)
        hatt = three(part(512), 4, P)
        SrB = three(part(256), 2, P)
        ShB = three(part(256), 2, P)
        S = three(part(512), 4, P)
        Dm, Dl, Dg, A, T, U, Zs, khat, khT, kb, kdec, vb, qkm = [three(part(512), 4, P) for _ in range(13)]
        gBr, nwT, vn = Zs, khT, Dm
        hr = part(512)
        he = part(512)
        hG = three(part(256), 2, P)
        hE = part(LEVELS * 256)
        hQ = part(LEVELS * 256)
        hqg = three(part(256), 2, P)
        hkd = three(part(256), 2, P)
        hkT = part(256)
        obuf = part(1024)
        hnb = part(1024)
        rtmp = three(hQ[:, 1024:1536], 4, P)
        mT = three(hE[:, 0:1024], KD, P)
        mix_used = used[0]
        x_all = wout.rearrange("p a b -> p (a b)").rearrange("p (t d) -> p t d", t=NT)
        x_junk = hE[:, 0:DM]
        used[0] = 0
        wexp = [[three(part(4096), KD, DE), three(part(4096), KD, DE), three(part(4096), KE, DM)] for _ in range(2)]
        xg = [part(DM) for _ in range(2)]
        xT = three(part(DM), KD, P)
        eg = part(DE)
        hact = part(DE)
        hT = three(part(DE), KE, P)
        yo = [part(DM) for _ in range(2)]
        moe_used = used[0]
        el, oh1, oh2, cnd, rk = [three(part(256), NT, 32) for _ in range(5)]
        goh, gex = [three(part(NGRP * NT), NT, NGRP) for _ in range(2)]
        gm, m1, m2_, e2, ri = [part(NT) for _ in range(5)]
        cnt, nblk, incl, base = [part(NE) for _ in range(4)]
        cmp_ = part(NB_MAX * 32)
        count_row = part(P)
        in_pos = three(part(2 * NT * P), 2 * NT, P)
        in_blk = three(part(2 * NT * NB_MAX), 2 * NT, NB_MAX)
        posi, blockn = [part(2 * NT).bitcast(I32) for _ in range(2)]
        posf, blockf = [part(2 * NT) for _ in range(2)]
        tokf = part(NT)
        used[0] = 0
        cm_y1 = [part(DM) for _ in range(NT)]
        cm_y2 = [part(DM) for _ in range(NT)]
        assert used[0] <= 2 * 3 * 4096
        used[0] = moe_used
        cm_h = three(part(NT * DM), NT, DM)
        fgain = part(DM)
        mrun = sb("mrun", [P, NT + 1, 32])
        w12 = sb("w12", [P, 2, NT])
        dst = sb("dst", [P, 2, NT])
        dsti = sb("dsti", [P, 2, NT], I32)
        blkt = sb("blkt", [P, NB_MAX + 2])
        blki = sb("blki", [P, NB_MAX + 2], I32)
        slots = sb("slots", [P, NB_MAX], I32)
        zrow = mrun[:, 0:NT, :].rearrange("p a b -> p (a b)")
        idxs = [sb(f"idx{k}", [P, 1], I32) for k in range(2)]

        ps = [ctx.enter_context(nc.psum_tensor(f"ps{k}", [P, 512], F32)) for k in range(8)]

        def b4(k):
            return ps[k][:, :].rearrange("p (a b) -> p a b", a=4)

        ssx, mx, rx, tx_ = [sc[:, 160 + NT * k:160 + NT * (k + 1)] for k in range(4)]
        dax, dae, dl, gcol, beta, gc, eG, eGL, ekd, bG, dxx = [sc[:, 8 + 4 * k:12 + 4 * k] for k in range(11)]
        mqk, rqk, tqk = [sc[:, 56 + 8 * k:64 + 8 * k] for k in range(3)]
        mh, rh, th_, sh = [sc[:, 80 + 16 * k:96 + 16 * k] for k in range(4)]
        ehGL = sc[:, 144:146]
        ss2, m2, r2, t2 = [sc[:, 150 + k:151 + k] for k in range(4)]
        sg4 = sc[:, 154:158]
        negA, lbv, oml = lbw[:, 0:2, :].rearrange("p a b -> p (a b)"), lbw[:, 2, :], lbw[:, 3, :]
        lbt = sb("lbt", [P, 4, 2])

        w_view = a["w_in"][0].rearrange("(k p) n -> p k n", p=P)
        x_view = a["x"][0].rearrange("(t p) d -> t p d", p=P)
        hn_v = hn_d.rearrange("(t p) d -> t p d", p=P)
        h_v = h_d.rearrange("(t p) d -> t p d", p=P)
        out_v = out[0].rearrange("(t p) d -> t p d", p=P)
        rot_v = a["rotary"].rearrange("(t p) d -> t p d", p=P)

        PER = {"proj_filled": NG, "proj_copied": NG, "x_loaded": 16, "xres_loaded": 16, "rot_loaded": 16,
               "hn_stored": 32, "UT": LEVELS, "Z": LEVELS - 1, "Zs": LEVELS - 1, "dU": LEVELS - 1,
               "dT": LEVELS - 2, "tconv": 3, "cb_in": 3, "cy": 3, "cexp": 3, "cs": 3, "hKQ": 4, "tm": 2,
               "t2": 2, "tx": 2, "hA": 4, "hatt": 4}

        def at(name, i, k=None):
            per = PER.get(name, 1)
            return i * per + (per if k is None else k)

        class Engine:

            def __init__(self, eng, chain, per):
                self.eng, self.chain, self.per, self.c, self.base = eng, chain, per, 0, 0

            def wait(self, name, i, k=None):
                self.eng.wait_ge(sem(name), at(name, i, k))

            def link(self, ins):
                self.c += 1
                ins.then_inc(sem(self.chain), 1)
                self.eng.wait_ge(sem(self.chain), self.base + self.c)

            def start(self, base):
                self.c, self.base = 0, base

            def end(self):
                assert self.c == self.per, (self.chain, self.c)

        N_PARAMS = 16 * 18
        DVE_LINKS, ACT_LINKS = 77, 1
        block = ctx.enter_context(nc.Block())

        @block.sync
        def _(sp):
            loads = [0]

            def ld(dst_, src):
                loads[0] += 16
                sp.dma_start(dst_, src).then_inc(sem("params_loaded"), 16)

            sp.dma_start(xin[:, :], x_view[0]).then_inc(sem("x_loaded"), 16)
            ld(cst[:, :], a["consts"])
            with nc.allow_non_contiguous_dma(reason="small parameter vectors"):
                ld(g1c[:, :], a["attn_norm"][0].rearrange("(k p) -> p k", p=P))
                ld(g2c[:, :], a["ffn_norm"][0].rearrange("(k p) -> p k", p=P))
                ld(gmc[:, 0:2], a["ret_norm"][0].rearrange("(k p) -> p k", p=P))
                gd = a["gdn_norm"][0].rearrange("(p o) -> p o", o=1)
                for h in range(4):
                    ld(gmc[:, 2 + h:3 + h], gd)
                ld(gmc[:, 6:8], a["hgrn_norm"][0].rearrange("(k p) -> p k", p=P))
                ld(lbc[:, :], a["hgrn_lower_bounds"][0].rearrange("(k p) -> p k", p=P))
                for j in range(4):
                    ld(convw[:, j, :], a["gdn_conv"][0, j].rearrange("(k p) -> p k", p=P))
                ld(abrow[:, 0:4], a["gdn_a_log"].to_broadcast([P, 4]))
                ld(abrow[:, 4:8], a["gdn_dt_bias"].to_broadcast([P, 4]))
                ld(wr[:, :, 0:4], a["router_group"][0].rearrange("(k p) n -> p k n", p=P))
            ld(wr[:, :, 4:36], a["router_expert"][0].rearrange("(k p) n -> p k n", p=P))
            assert loads[0] == N_PARAMS, loads[0]

            def load_w(t, n, nxt):
                if nxt or n >= 2:
                    sp.wait_ge(sem("proj_filled"), at("proj_filled", t, n - 1))
                c0, w = GROUPS[n]
                sp.dma_start(three(wg[n % 2][:, 0:KD * w], KD, w), w_view[:, :, c0:c0 + w]) \
                    .then_inc(sem(f"w_in_loaded{n % 2}"), 16)

            def first_expert():
                for m, name in enumerate(("w_gate", "w_up")):
                    sp.dma_start(wexp[0][m], a[name][0, 0].rearrange("(k p) n -> p k n", p=P)) \
                        .then_inc(sem("gu_loaded0"), 16)

            def load_w_out(k0):
                sp.wait_ge(sem("x_sq"), 2)
                sp.dma_start(wout[:, k0:k0 + KD // 2, :],
                             a["w_out"][0].rearrange("(k p) n -> p k n", p=P)[:, k0:k0 + KD // 2, :]) \
                    .then_inc(sem("w_out_loaded"), 16)

            def tile_steps(i, nxt, nxt2, first=False):
                if nxt2:
                    sp.wait_ge(sem("xsc"), i + 2)
                    sp.dma_start(xin[:, :], x_view[i + 2]).then_inc(sem("x_loaded"), 16)
                if nxt:
                    sp.wait_ge(sem("rot"), i + 1)
                    sp.dma_start(rtab, rot_v[i + 1]).then_inc(sem("rot_loaded"), 16)
                sp.wait_ge(sem("hbuf_free"), i + 1)
                sp.dma_start(hbuf[:, :], x_view[i]).then_inc(sem("xres_loaded"), 16)
                if nxt:
                    for n in range(2, NG):
                        load_w(i + 1, n, True)
                        if first and n in (5, 6):
                            load_w_out((n - 5) * KD // 2)
                else:
                    sp.wait_ge(sem("proj_filled"), NG * NT)
                    first_expert()
                    sp.wait_ge(sem("wo"), NT)
                    sp.dma_start(wexp[0][2], a["w_down"][0, 0].rearrange("(k p) n -> p k n", p=P)) \
                        .then_inc(sem("down_loaded0"), 16)
                sp.wait_ge(sem("h_ready"), i + 1)
                sp.dma_start(h_v[i], hbuf[:, :]).then_inc(sem("hn_stored"), 16)
                if nxt2:
                    load_w(i + 2, 0, True)
                sp.wait_ge(sem("hn_ready"), i + 1)
                sp.dma_start(hn_v[i], hnb).then_inc(sem("hn_stored"), 16)
                if nxt2:
                    load_w(i + 2, 1, True)
                sp.wait_ge(sem("hn_stored"), at("hn_stored", i))
                sp.sem_inc(sem("hbuf_free"), 1)

            load_w(0, 0, False)
            load_w(0, 1, False)
            sp.wait_ge(sem("xsc"), 1)
            sp.dma_start(xin[:, :], x_view[1]).then_inc(sem("x_loaded"), 16)
            sp.dma_start(rtab, rot_v[0]).then_inc(sem("rot_loaded"), 16)
            for n in range(2, NG):
                load_w(0, n, False)
                for t in ((1,), (2,), (3,), (4,), (5, 6), (7,), (), ())[n - 2]:
                    sp.dma_start(x_all[:, t, :], x_view[t]).then_inc(sem(f"x_all_loaded{t // 6}"), 16)
            load_w(1, 0, True)
            load_w(1, 1, True)
            sp.sem_inc(sem("hbuf_free"), 1)
            tile_steps(0, True, True, True)
            with sp.Fori(1, NT - 2) as i:
                tile_steps(i, True, True)
            tile_steps(NT - 2, True, False)
            tile_steps(NT - 1, False, False)

            def load_matrix(m, par, e):
                name, rows = (("w_gate", "gu_loaded"), ("w_up", "gu_loaded"), ("w_down", "down_loaded"))[m]
                sp.dma_start(wexp[par][m], a[name][0, e].rearrange("(k p) n -> p k n", p=P)) \
                    .then_inc(sem(f"{rows}{par}"), 16)

            def load_expert(b, par):
                e = sp.value_load(blki[0:1, bass.ds(b, 1)], min_val=0, max_val=NE - 1)
                sp.wait_ge(sem("gu_done"), b - 1)
                load_matrix(0, par, e)
                load_matrix(1, par, e)
                sp.wait_ge(sem("down_done"), b - 1)
                load_matrix(2, par, e)

            sp.wait_ge(sem("blk_ready"), 1)
            pairs = sp.value_load(blki[0:1, NB_MAX:NB_MAX + 1], min_val=NB_MIN // 2, max_val=NB_MAX // 2)
            second = sp.value_load(blki[0:1, 1:2], min_val=0, max_val=NE - 1)
            sp.wait_ge(sem("idx_seen"), 2)
            for m in range(3):
                load_matrix(m, 1, second)
            with sp.Fori(1, pairs) as q:
                load_expert(2 * q, 0)
                load_expert(2 * q + 1, 1)
            sp.wait_ge(sem("slots_ready"), 1)
            sp.dma_start(cm_h, h_d.rearrange("(t p) d -> p t d", p=P)).then_inc(sem("ch_loaded"), 16)
            sp.dma_start(fgain, a["final_norm"].partition_broadcast(P)).then_inc(sem("gain_loaded"), 16)
            for t in range(NT):
                sp.wait_ge(sem("c_out"), t + 1)
                sp.dma_start(out_v[t], cm_y1[t]).then_inc(sem("out_stored"), 16)
            sp.wait_ge(sem("out_stored"), 16 * NT)

        @block.tensor
        def _(pe):
            t_ = nc.tensor
            E = Engine(pe, "pe_chain", 0)

            def transposes(bank, blocks, name):
                for k, blk in enumerate(blocks):
                    last = t_.transpose(ps[bank][:, k * P:(k + 1) * P], blk, ident)
                last.then_inc(sem(name), 1)

            def each_head(bank, lhs, rhs, name):
                for h in range(4):
                    last = t_.matmul(b4(bank)[:, h, :], lhs[:, h, :], rhs[:, h, :], start=True, stop=True)
                last.then_inc(sem(name), 1)

            def cols(ap, k0, n):
                return [ap[:, k * P:(k + 1) * P] for k in range(k0, k0 + n)]

            def x_transposes(t):
                E.wait("xsc", t)
                transposes(6, cols(junk, 0, 4), "tx")
                transposes(7, cols(junk, 4, 4), "tx")

            def project(t, n, nxt, k0, k1):
                c0, w = GROUPS[n]
                if k0 == 0:
                    if n == 0:
                        E.wait("xnT", t)
                    pe.wait_ge(sem(f"w_in_loaded{n % 2}"), 16 * (t * (NG // 2) + n // 2 + 1))
                    if nxt or n >= 2:
                        E.wait("proj_copied", t, n - 1)
                wv = three(wg[n % 2][:, 0:KD * w], KD, w)
                for k in range(k0, k1):
                    last = t_.matmul(ps[6 + n % 2][:, 0:w], xnT[:, k, :], wv[:, k, :], start=k == 0, stop=k == KD - 1)
                if k1 == KD:
                    last.then_inc(sem("proj_filled"), 1)

            def two_heads_out(bank, qx, Sx, att, v0):
                for j in range(2):
                    t_.matmul(ps[bank][:, j * P:(j + 1) * P], qx[:, j, :], Sx[:, j, :], start=True, stop=False)
                    for q in range(2):
                        c = v0 + P * j + 64 * q
                        t_.matmul(ps[bank][:, j * P + 64 * q:j * P + 64 * q + 64], att[:, 2 * q + j, :],
                                  pj[:, c:c + 64], start=False, stop=q == 1)

            def mixer(i, nxt):
                def group(n, k0=0, k1=KD):
                    if nxt:
                        project(i + 1, n, True, k0, k1)

                E.wait("proj_copied", i)
                if nxt:
                    x_transposes(i + 1)
                transposes(0, cols(pj, C_DQ // P, 4), "tconv")
                transposes(1, cols(pj, C_DQ // P + 4, 4), "tconv")
                transposes(2, cols(pj, C_DQ // P + 8, 4), "tconv")
                transposes(3, [pj[:, C_HQ + k * P:C_HQ + (k + 1) * P] for k in range(4)], "th")
                E.wait("rot", i)
                transposes(4, cols(rot, 0, 4), "tr")
                group(0)
                group(1, 0, 3)
                E.wait("cb_in", i)
                E.wait("rqT", i)
                for q in range(2):
                    for j in range(2):
                        last = t_.matmul(ps[1 + q][:, j * P:(j + 1) * P], rqT[64 * q:64 * q + 64, 2 + j, :],
                                         rqT[64 * q:64 * q + 64, j, :], start=True, stop=True)
                last.then_inc(sem("rS"), 1)
                E.wait("gBr", i)
                for h in range(4):
                    last = t_.matmul(b4(0)[:, h, :], gBr[:, h, :], cn("tri"), start=True, stop=True)
                t_.matmul(ps[5][:, 0:4], cn("tri"), gcol, start=True, stop=True).then_inc(sem("Gsum"), 1)
                group(1, 3, 8)
                group(2, 0, 5)
                E.wait("hraw", i)
                E.wait("cs", i, 2)
                transposes(3, [cy[:, 4 + k, :] for k in range(4)], "ktok")
                group(2, 5, 8)
                E.wait("csq", i)
                E.wait("gc", i)
                cq = ce[:, 0:1024].rearrange("p (a b) -> p a b", a=8)
                for h in range(8):
                    last = t_.matmul(ps[5][:, 8 + h:9 + h], cq[:, h, :], cn("ones")[:, 0:1], start=True, stop=True)
                last.then_inc(sem("ssq"), 1)
                E.wait("rA", i)
                E.wait("rqX", i)
                two_heads_out(1, rqX, SrB, rA, C_RV)
                for j in range(2):
                    last = t_.matmul(ps[2][:, j * P:(j + 1) * P], rkz[:, j * P:(j + 1) * P],
                                     pj[:, C_RV + P * j:C_RV + P * j + P], start=True, stop=True)
                last.then_inc(sem("rOU"), 1)
                group(3)
                E.wait("cs", i, 3)
                transposes(4, [cy[:, 8 + k, :] for k in range(4)], "vtok")
                group(4, 0, 2)
                E.wait("khat", i)
                transposes(3, [khat[:, h, :] for h in range(4)], "tkh")
                group(4, 2, 4)
                E.wait("khT", i)
                E.wait("vb", i)
                each_head(4, khT, khT, "kk")
                group(4, 4, 6)
                E.wait("gam", i)
                each_head(0, khT, cy, "qk")
                E.wait("A", i)
                transposes(3, [A[:, h, :] for h in range(4)], "tA")
                group(4, 6, 8)
                group(5, 0, 2)
                for l in range(1, LEVELS):
                    E.wait("UT", i, l)
                    each_head(0, A, U, "Z")
                    if l <= 4:
                        E.wait("hKQ", i, l)
                        if l > 1:
                            E.wait("hatt", i, l - 1)
                        if l == 1:
                            E.wait("r_out", i)
                            E.wait("r_state", i)
                        for q in range(2):
                            rows = slice(64 * q, 64 * q + 64)
                            for m in range(2):
                                lev = 2 * (l - 1) + m
                                for j in range(2):
                                    o = (2 * lev + j) * P
                                    if lev < LEVELS:
                                        kq, qq = hE[rows, o:o + P], hQ[rows, o:o + P]
                                    else:
                                        kq, qq = he[rows, 256 + j * P:384 + j * P], hr[rows, j * P:(j + 1) * P]
                                    last = t_.matmul(ps[1 + q][:, (2 * m + j) * P:(2 * m + j + 1) * P], kq, qq,
                                                     start=True, stop=True)
                        last.then_inc(sem("hA"), 1)
                    if l == 5:
                        transposes(3, [hkd[:, j, :] for j in range(2)], "thk")
                        group(6, 0, 2)
                    if l == 6:
                        E.wait("hatt", i, 4)
                        two_heads_out(1, hqg, ShB, hatt, C_HI)
                        E.wait("hkT", i)
                        for j in range(2):
                            last = t_.matmul(ps[2][:, j * P:(j + 1) * P], hkT[:, j * P:(j + 1) * P],
                                             pj[:, C_HI + P * j:C_HI + P * j + P], start=True, stop=True)
                        last.then_inc(sem("hOU"), 1)
                    E.wait("Zs", i, l)
                    each_head(4, T, Zs, "dU")
                    if l < LEVELS - 1:
                        each_head(5, Zs, T, "dT")
                    if l <= 4:
                        group(5, (2, 4, 5, 6)[l - 1], (4, 5, 6, 8)[l - 1])
                    elif l == 5:
                        group(6, 2, 6)
                    else:
                        group(6, 6, 8)
                        group(7, 0, 2)
                E.wait("UT", i, LEVELS)
                E.wait("keys", i)
                each_head(0, kb, U, "wT")
                group(7, 2, 8)
                E.wait("nwT", i)
                for h in range(4):
                    t_.matmul(b4(4)[:, h, :], U[:, h, :], vb[:, h, :], start=True, stop=False)
                    last = t_.matmul(b4(4)[:, h, :], nwT[:, h, :], S[:, h, :], start=False, stop=True)
                last.then_inc(sem("vnew"), 1)
                each_head(5, cy, S, "o1")
                E.wait("vn", i)
                each_head(0, qkm, vn, "o2")
                each_head(3, kdec, vn, "dS")
                group(8)
                group(9, 0, 1)
                E.wait("mixed", i)
                transposes(1, cols(obuf, 0, 4), "tm")
                transposes(2, cols(obuf, 4, 4), "tm")
                group(9, 1, 2)
                pe.wait_ge(sem("w_out_loaded"), 32)
                E.wait("mT", i)
                for n in range(2):
                    for k in range(KD):
                        last = t_.matmul(ps[4 + n][:, :], mT[:, k, :], wout[:, k, n * 512:(n + 1) * 512],
                                         start=k == 0, stop=k == KD - 1)
                last.then_inc(sem("wo"), 1)
                group(9, 2, 7)
                E.wait("hn_ready", i)
                transposes(0, cols(hnb, 0, 4), "t2")
                transposes(3, cols(hnb, 4, 4), "t2")
                group(9, 7, 8)
                E.wait("h2T", i)
                for k in range(KD):
                    last = t_.matmul(ps[5][:, 32:68], mT[:, k, :], wr[:, k, :], start=k == 0, stop=k == KD - 1)
                last.then_inc(sem("rt"), 1)

            pe.wait_ge(sem("params_loaded"), N_PARAMS)
            x_transposes(0)
            for n in range(NG):
                project(0, n, False, 0, KD)
            pe.wait_ge(sem("zeroed"), 1)
            with pe.Fori(0, NT - 1) as i:
                mixer(i, True)
            mixer(NT - 1, False)

            pe.wait_ge(sem("picked"), 1)
            t_.matmul(ps[0][:, 0:256], cn("stri"), cnd, start=True, stop=False)
            t_.matmul(ps[0][:, 0:256], cn("ones"), mrun[:, 0:NT, :], start=False, stop=True)
            t_.matmul(ps[1][:, 0:32], cn("ones"), mrun[:, NT, :], start=True, stop=True).then_inc(sem("ranks"), 1)
            for k in range(2 * NT):
                if k % NT == 0:
                    pe.wait_ge(sem("dst_ready"), k // NT + 1)
                last = t_.matmul(ps[2][:, 0:NB_MAX], in_pos[:, k, :], in_blk[:, k, :], start=k == 0,
                                 stop=k == 2 * NT - 1)
            last.then_inc(sem("slots_summed"), 1)

            pe.wait_ge(sem("blk_ready"), 1)
            pairs = pe.value_load(blki[0:1, NB_MAX:NB_MAX + 1], min_val=NB_MIN // 2, max_val=NB_MAX // 2)
            last_pair = pe.value_load(blki[0:1, NB_MAX + 1:NB_MAX + 2], min_val=NB_MIN // 2 - 1,
                                      max_val=NB_MAX // 2 - 1)

            def x_block(b, q, par):
                pe.wait_ge(sem(f"tok_loaded{par}"), q * 16 + 16)
                for k in range(KD):
                    last = t_.transpose(ps[k // 4][:, (k % 4) * P:(k % 4 + 1) * P], xg[par][:, k * P:(k + 1) * P],
                                        ident)
                last.then_inc(sem("xt_done"), 1)

            def gate_up(b, q, par):
                pe.wait_ge(sem("xT_ready"), b + 1)
                pe.wait_ge(sem(f"gu_loaded{par}"), q * 32 + 32)
                for m, name in enumerate(("g_done", "gu_done")):
                    for k in range(KD):
                        last = t_.matmul(ps[2 + m][:, :], xT[:, k, :], wexp[par][m][:, k, :], start=k == 0,
                                         stop=k == KD - 1)
                    last.then_inc(sem(name), 1)

            def h_block(b):
                pe.wait_ge(sem("hact_ready"), b + 1)
                for k in range(KE):
                    last = t_.transpose(ps[4][:, k * P:(k + 1) * P], hact[:, k * P:(k + 1) * P], ident)
                last.then_inc(sem("ht_done"), 1)

            def down(b, q, par):
                pe.wait_ge(sem("hT_ready"), b + 1)
                pe.wait_ge(sem(f"down_loaded{par}"), q * 16 + 16)
                for n in range(2):
                    for k in range(KE):
                        last = t_.matmul(ps[5 + n][:, :], hT[:, k, :], wexp[par][2][:, k, n * 512:(n + 1) * 512],
                                         start=k == 0, stop=k == KE - 1)
                last.then_inc(sem("down_done"), 1)

            x_block(0, 0, 0)
            gate_up(0, 0, 0)
            x_block(1, 0, 1)
            h_block(0)
            with pe.Fori(1, pairs) as q:
                gate_up(2 * q - 1, q - 1, 1)
                x_block(2 * q, q, 0)
                pe.wait_ge(sem("y0_ready"), 2 * q - 1)
                pe.wait_ge(sem("y1_ready"), 2 * q - 1)
                down(2 * q - 2, q - 1, 0)
                h_block(2 * q - 1)
                gate_up(2 * q, q, 0)
                x_block(2 * q + 1, q, 1)
                pe.wait_ge(sem("y0_ready"), 2 * q)
                pe.wait_ge(sem("y1_ready"), 2 * q)
                down(2 * q - 1, q - 1, 1)
                h_block(2 * q)
            gate_up(last_pair * 2 + 1, last_pair, 1)
            pe.wait_ge(sem("y0_ready"), last_pair * 2 + 1)
            pe.wait_ge(sem("y1_ready"), last_pair * 2 + 1)
            down(last_pair * 2, last_pair, 0)
            h_block(last_pair * 2 + 1)
            pe.wait_ge(sem("y0_ready"), last_pair * 2 + 2)
            pe.wait_ge(sem("y1_ready"), last_pair * 2 + 2)
            down(last_pair * 2 + 1, last_pair, 1)

        @block.scalar
        def _(act):
            s = nc.scalar
            E = Engine(act, "act_chain", ACT_LINKS)

            def copy_group(t, n):
                c0, w = GROUPS[n]
                E.wait("proj_filled", t, n + 1)
                s.activation(pj[:, c0:c0 + w], ps[6 + n % 2][:, 0:w], ACT.Copy).then_inc(sem("proj_copied"), 1)

            def mixer(i, nxt):
                def group(n):
                    if nxt:
                        copy_group(i + 1, n)

                E.wait("hist", i)
                for k in range(3):
                    E.wait("tconv", i, k + 1)
                    s.activation(cb[:, 4 * k:4 * k + 4, 3:131], b4(k), ACT.Copy).then_inc(sem("cb_in"), 1)
                E.wait("th", i)
                s.activation(he[:, 256:512], ps[3][:, 256:512], ACT.Exp, scale=-1.0)
                s.activation(he[:, 0:256], ps[3][:, 0:256], ACT.Tanh, scale=0.5)
                s.activation(hr, ps[3][:, :], ACT.Copy).then_inc(sem("hraw"), 1)
                E.wait("tr", i)
                s.activation(rqT, b4(4), ACT.Copy).then_inc(sem("rqT"), 1)
                E.wait("dax", i)
                E.link(s.activation(dae, dax, ACT.Exp, scale=-1.0))
                s.activation(beta, pj[:, C_DB:C_DB + 4], ACT.Exp, scale=-1.0)
                s.activation(gt[:, 0:256], pj[:, C_RG:C_RG + 256], ACT.Tanh, scale=0.5)
                s.activation(gt[:, 256:768], pj[:, C_DZ:C_DZ + 512], ACT.Tanh, scale=0.5)
                s.activation(gt[:, 768:1024], pj[:, C_HG:C_HG + 256], ACT.Tanh, scale=0.5).then_inc(sem("gexp"), 1)
                s.activation(dl, dae, ACT.Ln, bias=1.0).then_inc(sem("dl"), 1)
                group(0)
                ce12 = three(ce, 12, P)

                def conv_tanh(part_):
                    E.wait("cy", i, part_ + 1)
                    c4 = slice(4 * part_, 4 * part_ + 4)
                    s.activation(ce12[:, c4, :], cy[:, c4, :], ACT.Tanh).then_inc(sem("cexp"), 1)

                conv_tanh(0)
                conv_tanh(1)
                group(1)
                E.wait("cs", i, 2)
                s.activation(ce[:, 0:1024], cy[:, 0:8, :], ACT.Square).then_inc(sem("csq"), 1)
                group(2)
                conv_tanh(2)
                E.wait("hf", i)
                s.activation(he[:, 0:256], hr[:, 256:512], ACT.Ln).then_inc(sem("hln"), 1)
                E.wait("Dg", i)
                s.activation(Dl, Dl, ACT.Exp)
                s.activation(Dg, Dg, ACT.Exp, scale=-1.0)
                s.activation(eG, gc, ACT.Exp)
                s.activation(ekd, Dm[:, :, P - 1], ACT.Exp)
                s.activation(eGL, b4(0)[:, :, P - 1], ACT.Exp).then_inc(sem("gam"), 1)
                E.wait("rOU", i)
                s.activation(obuf[:, 0:256], ps[1][:, 0:256], ACT.Copy).then_inc(sem("r_out"), 1)
                group(3)
                E.wait("tkh", i)
                s.activation(khT, b4(3), ACT.Copy).then_inc(sem("khT"), 1)
                E.wait("hlev", i)
                s.activation(hE, hE, ACT.Exp)
                s.activation(hqg, hG, ACT.Exp)
                for j in range(2):
                    s.activation(hkd[:, j, :], hG[:, j, :], ACT.Exp, scale=-1.0, bias=hG[:, j, P - 1:P])
                s.activation(ehGL, hG[:, :, P - 1], ACT.Exp).then_inc(sem("hexp"), 1)
                group(4)
                if nxt:
                    E.wait("rot", i)
                group(5)
                E.wait("thk", i)
                s.activation(hkT, ps[3][:, 0:256], ACT.Copy).then_inc(sem("hkT"), 1)
                E.wait("hOU", i)
                s.activation(obuf[:, 768:1024], ps[1][:, 0:256], ACT.Copy, scale=0.5).then_inc(sem("h_out"), 1)
                E.wait("wT", i)
                s.activation(nwT, b4(0), ACT.Copy, scale=-1.0).then_inc(sem("nwT"), 1)
                if nxt:
                    E.wait("gate", i)
                group(6)
                group(7)
                E.wait("vnew", i)
                s.activation(vn, b4(4), ACT.Copy).then_inc(sem("vn"), 1)
                E.wait("od", i)
                s.activation(hQ[:, 0:1024], obuf, ACT.Square).then_inc(sem("o_sq"), 1)
                group(8)
                E.wait("h_ready", i)
                s.activation(hnb, hbuf[:, :], ACT.Square, accum_out=ss2).then_inc(sem("h_sq"), 1)
                group(9)
                E.wait("rt", i)
                s.activation(lg[:, i, :], ps[5][:, 32:68], ACT.Copy).then_inc(sem("logits"), 1)

            E.wait("x_loaded", 0)
            s.activation(x_junk, xin[:, :], ACT.Square, accum_out=ssx[:, 0:1]).then_inc(sem("x_sq"), 1)
            act.wait_ge(sem("params_loaded"), N_PARAMS)
            act.wait_ge(sem("lb_shifted"), 1)
            s.activation(lbt[:, 1, :], lbt[:, 0, :], ACT.Exp)
            s.activation(negA, abrow[:, 0:4], ACT.Exp).then_inc(sem("param_exp"), 1)
            for n in range(NG):
                copy_group(0, n)
                if n in (NG - 3, NG - 2):
                    act.wait_ge(sem(f"x_all_loaded{n - NG + 3}"), (80, 32)[n - NG + 3])
                    for t in ((1, 2, 3, 4, 5), (6, 7))[n - NG + 3]:
                        last = s.activation(x_all[:, t, :], x_all[:, t, :], ACT.Square, accum_out=ssx[:, t:t + 1])
                    if n == NG - 2:
                        last.then_inc(sem("x_sq"), 1)
            with act.Fori(0, NT - 1) as i:
                E.start(i * ACT_LINKS)
                mixer(i, True)
                E.end()
            E.start((NT - 1) * ACT_LINKS)
            mixer(NT - 1, False)

            act.wait_ge(sem("r_shift"), 1)
            s.activation(gex, gex, ACT.Exp)
            s.activation(e2, e2, ACT.Exp).then_inc(sem("r_exp"), 1)

            act.wait_ge(sem("y_zeroed"), 16 * NT)
            act.wait_ge(sem("blk_ready"), 1)
            pairs = act.value_load(blki[0:1, NB_MAX:NB_MAX + 1], min_val=NB_MIN // 2, max_val=NB_MAX // 2)
            last_pair = act.value_load(blki[0:1, NB_MAX + 1:NB_MAX + 2], min_val=NB_MIN // 2 - 1,
                                      max_val=NB_MAX // 2 - 1)
            act.sem_inc(sem("y_stored0"), 16)
            act.sem_inc(sem("y_stored1"), 16)
            act.sem_inc(sem("y0_ready"), 1)
            act.sem_inc(sem("y1_ready"), 1)

            def silu_tanh(b):
                act.wait_ge(sem("g_done"), b + 1)
                s.activation(eg, ps[2][:, :], ACT.Tanh, scale=0.5).then_inc(sem("eg"), 1)

            def h_copy(b):
                act.wait_ge(sem("ht_done"), b + 1)
                s.activation(hT, b4(4), ACT.Copy).then_inc(sem("hT_ready"), 1)

            def y_left(b, q, par):
                act.wait_ge(sem("down_done"), b + 1)
                act.wait_ge(sem(f"y_stored{par}"), q * 16 + 16)
                s.activation(yo[par][:, 0:512], ps[5][:, :], ACT.Copy).then_inc(sem("y0_ready"), 1)

            def y_store(b, par):
                act.wait_ge(sem("y0_ready"), b + 2)
                act.wait_ge(sem("y1_ready"), b + 2)
                act.dma_start(y_d[bass.ds(b * BLK, BLK), :], yo[par]).then_inc(sem(f"y_stored{par}"), 16)

            silu_tanh(0)
            h_copy(0)
            with act.Fori(1, pairs) as q:
                silu_tanh(2 * q - 1)
                y_left(2 * q - 2, q - 1, 0)
                h_copy(2 * q - 1)
                y_store(2 * q - 2, 0)
                silu_tanh(2 * q)
                y_left(2 * q - 1, q - 1, 1)
                h_copy(2 * q)
                y_store(2 * q - 1, 1)
            silu_tanh(last_pair * 2 + 1)
            y_left(last_pair * 2, last_pair, 0)
            h_copy(last_pair * 2 + 1)
            y_store(last_pair * 2, 0)
            y_left(last_pair * 2 + 1, last_pair, 1)
            y_store(last_pair * 2 + 1, 1)

            def scaled(t):
                act.wait_ge(sem("c_root"), t // 2 + 1)
                for o in (t, t + 1):
                    s.activation(cm_y2[o], cm_h[:, o, :], ACT.Copy, scale=rx[:, o:o + 1]).then_inc(sem("c_scaled"), 1)

            for t in range(NT):
                act.wait_ge(sem("c_sum"), t + 1)
                s.activation(cm_y1[t], cm_h[:, t, :], ACT.Square, accum_out=ssx[:, t:t + 1]).then_inc(sem("c_sq"), 1)
                if t >= 3 and t % 2 == 1:
                    scaled(t - 3)
            scaled(NT - 2)

        @block.vector
        def _(dve):
            v = nc.vector
            E = Engine(dve, "dve_chain", DVE_LINKS)
            link = E.link

            def tt(o, x, y, op):
                return v.tensor_tensor(o, x, y, op)

            def rsqrt(m, y, tmp, link=link):
                link(v.tensor_scalar(y.bitcast(I32), m.bitcast(I32), -0.5, RSQRT_MAGIC, ALU.mult, ALU.add))
                for step in range(3):
                    link(v.scalar_tensor_tensor(tmp, y, -0.5, y, ALU.mult, ALU.mult))
                    link(tt(tmp, tmp, m, ALU.mult))
                    link(v.scalar_tensor_tensor(y, tmp, 1.5, y, ALU.add, ALU.mult))

            chain = [0]

            def seq(ins):
                chain[0] += 1
                ins.then_inc(sem("route_chain"), 1)
                dve.wait_ge(sem("route_chain"), chain[0])

            def pick(t0, t1):
                n, at_ = t1 - t0, slice(t0, t1)
                dve.wait_ge(sem("logits"), t1)

                def first_of(onehot, values, top, width):
                    io = cn("iota")[:, 0:width]
                    seq(tt(onehot, values, bc(top, width), ALU.is_equal))
                    seq(tt(onehot, onehot, heads(io, n), ALU.mult))
                    seq(v.tensor_reduce(ri[:, at_], onehot, AX.X, ALU.min))
                    seq(tt(onehot, heads(io, n), bc(ri[:, at_], width), ALU.is_equal))

                gl, go = lg[:, at_, 0:NGRP], goh[:, at_, :]
                elt, first, second, both = [x[:, at_, :] for x in (el, oh1, oh2, cnd)]
                seq(v.reduce_max(gm[:, at_], gl, AX.X))
                seq(tt(gex[:, at_, :], gl, bc(gm[:, at_], NGRP), ALU.subtract))
                first_of(go, gl, gm[:, at_], NGRP)
                seq(v.tensor_scalar(go, go, BIG, -BIG, ALU.mult, ALU.add))
                seq(tt(elt.rearrange("p t (g e) -> p t g e", g=NGRP),
                       lg[:, at_, NGRP:].rearrange("p t (g e) -> p t g e", g=NGRP), bc(go, EPG), ALU.add))
                seq(v.reduce_max(m1[:, at_], elt, AX.X))
                first_of(first, elt, m1[:, at_], NE)
                seq(v.scalar_tensor_tensor(elt, first, -BIG, elt, ALU.mult, ALU.add))
                seq(v.reduce_max(m2_[:, at_], elt, AX.X))
                first_of(second, elt, m2_[:, at_], NE)
                seq(tt(e2[:, at_], m2_[:, at_], m1[:, at_], ALU.subtract))
                seq(tt(both, first, second, ALU.add))

            def count_before():
                dve.wait_ge(sem("y_zeroed"), 16 * NT)
                seq(v.memset(mrun[:, 0, :], 0.0))
                for t in range(NT - 1):
                    seq(tt(mrun[:, t + 1, :], mrun[:, t, :], cnd[:, t, :], ALU.add))

            def x_norm(t0, t1):
                link(v.tensor_scalar(mx[:, t0:t1], ssx[:, t0:t1], 1.0 / DM, EPS, ALU.mult, ALU.add))
                rsqrt(mx[:, t0:t1], rx[:, t0:t1], tx_[:, t0:t1])

            def x_scale(t, r):
                E.wait("x_loaded", t)
                v.tensor_scalar(junk[:, :], xin[:, :], r, None, ALU.mult).then_inc(sem("xsc"), 1)

            def x_gain(t):
                E.wait("tx", t)
                tt(xnT[:, 0:4, :], b4(6), bc(g1c[:, 0:4], P), ALU.mult)
                tt(xnT[:, 4:8, :], b4(7), bc(g1c[:, 4:8], P), ALU.mult).then_inc(sem("xnT"), 1)

            def mixer(i, nxt):
                if nxt:
                    x_scale(i + 1, rx[:, bass.ds(i + 1, 1)])
                E.wait("proj_copied", i)
                da = pj[:, C_DA:C_DA + 4]
                link(tt(dxx, da, abrow[:, 4:8], ALU.add))
                v.scalar_tensor_tensor(dax, dxx, -1.0, dxx, ALU.mult, ALU.max).then_inc(sem("dax"), 1)
                E.wait("rot_loaded", i)
                qk = pj[:, 0:512].rearrange("p (h d) -> p h d", h=8)
                ro = rot.rearrange("p (h d) -> p h d", h=8)
                rt = rtmp.rearrange("p a b -> p (a b)").rearrange("p (h d) -> p h d", h=8)
                tt(ro, qk, heads(rtab[:, 0:64], 8), ALU.mult)
                tt(rt[:, :, 0:32], qk[:, :, 32:64], heads(rtab[:, 64:96], 8), ALU.mult)
                link(tt(rt[:, :, 32:64], qk[:, :, 0:32], heads(rtab[:, 96:128], 8), ALU.mult))
                tt(ro, ro, rt, ALU.add).then_inc(sem("rot"), 1)
                if nxt:
                    x_gain(i + 1)
                cyf = cy.rearrange("p a b -> p (a b)")

                def conv(part_):
                    E.wait("cb_in", i, part_ + 1)
                    for j in range(4):
                        for k in range(4 * part_, 4 * part_ + 4):
                            if j == 0:
                                last = v.tensor_scalar(cy[:, k, :], cb[:, k, 0:P], convw[:, 0, k:k + 1], None,
                                                       ALU.mult)
                            else:
                                last = v.scalar_tensor_tensor(cy[:, k, :], cb[:, k, j:j + P], convw[:, j, k:k + 1],
                                                              cy[:, k, :], ALU.mult, ALU.add)
                        if j < 3:
                            link(last)
                    last.then_inc(sem("cy"), 1)

                def conv_silu(part_):
                    E.wait("cexp", i, part_ + 1)
                    c4 = slice(512 * part_, 512 * part_ + 512)
                    v.scalar_tensor_tensor(cyf[:, c4], ce[:, c4], 1.0, cyf[:, c4], ALU.add, ALU.mult) \
                        .then_inc(sem("cs"), 1)

                conv(0)
                E.wait("dl", i)
                link(v.scalar_tensor_tensor(dl, dxx, 0.0, dl, ALU.max, ALU.add))
                link(tt(gcol, dl, negA, ALU.mult))
                v.tensor_copy(gBr, bc(gcol, P)).then_inc(sem("gBr"), 1)
                v.tensor_scalar(beta, beta, 1.0, None, ALU.add)
                conv(1)
                v.reciprocal(beta, beta)
                E.wait("hraw", i)
                link(v.tensor_scalar(he[:, 256:512], he[:, 256:512], 1.0, None, ALU.add))
                link(v.reciprocal(he[:, 256:512], he[:, 256:512]))
                for j in range(2):
                    last = v.tensor_scalar(hr[:, 256 + P * j:384 + P * j], he[:, 256 + P * j:384 + P * j],
                                           oml[:, j:j + 1], lbv[:, j:j + 1], ALU.mult, ALU.add)
                link(last)
                v.scalar_tensor_tensor(hr[:, 0:256], he[:, 0:256], 1.0, hr[:, 0:256], ALU.add, ALU.mult)
                link(v.tensor_scalar(he[:, 256:512], hr[:, 256:512], -1.0, 1.0, ALU.mult, ALU.add))
                v.tensor_scalar(hr[:, 256:512], hr[:, 256:512], 2.0 ** -64, None, ALU.max).then_inc(sem("hf"), 1)
                conv_silu(0)
                conv_silu(1)
                E.wait("rS", i)
                for q in range(2):
                    last = tt(rA[:, 2 * q:2 * q + 2, :], three(ps[1 + q][:, 0:256], 2, P),
                              three(cn("dmat")[:, 256 * q:256 * q + 256], 2, P), ALU.mult)
                last.then_inc(sem("rA"), 1)
                E.wait("Gsum", i)
                v.tensor_copy(gc, ps[5][:, 0:4]).then_inc(sem("gc"), 1)
                conv(2)
                v.tensor_copy(cb[:, :, 0:3], cb[:, :, 128:131]).then_inc(sem("hist"), 1)
                E.wait("ssq", i)
                link(v.tensor_scalar(mqk, ps[5][:, 8:16], 1.0, EPS, ALU.mult, ALU.add))
                rsqrt(mqk, rqk, tqk)
                conv_silu(2)
                E.wait("ktok", i)
                tt(khat, b4(3), bc(rqk[:, 4:8], P), ALU.mult).then_inc(sem("khat"), 1)
                E.wait("rOU", i)
                tt(SrB, SrB, bc(cn("rdec"), P), ALU.mult)
                link(tt(three(rkz, 2, P), three(ps[2][:, 0:256], 2, P), heads(cn("pair"), 2), ALU.mult))
                tt(SrB, SrB, three(rkz, 2, P), ALU.add).then_inc(sem("r_state"), 1)
                E.wait("gc", i)
                link(tt(Dm, b4(0), bc(gc, P), ALU.subtract))
                v.tensor_scalar(Dl, Dm, 0.0, None, ALU.min)
                link(v.tensor_scalar(Dg, Dm, 0.0, None, ALU.max))
                tt(Dl, Dl, heads(cn("neg_up"), 4), ALU.add)
                tt(Dg, Dg, heads(cn("pos_low"), 4), ALU.add).then_inc(sem("Dg"), 1)
                E.wait("vtok", i)
                tt(vb, b4(4), bc(beta, P), ALU.mult).then_inc(sem("vb"), 1)
                E.wait("hln", i)
                for j in range(2):
                    last = v.tensor_tensor_scan(hG[:, j, :], cn("ones"), he[:, j * P:(j + 1) * P], 0.0, ALU.mult,
                                                ALU.add)
                link(last)
                hGf = hG.rearrange("p a b -> p (a b)")
                for l in range(LEVELS):
                    m = 2 ** l
                    g3 = hGf.rearrange("p (n b) -> p n b", b=2 * m)
                    last = tt(hE[:, 256 * l:256 * l + 256].rearrange("p (n b) -> p n b", b=2 * m), g3,
                              bc(g3[:, :, m - 1], 2 * m), ALU.subtract)
                link(last)
                v.scalar_tensor_tensor(hE, hE, -1.0, hE, ALU.mult, ALU.min).then_inc(sem("hlev"), 1)
                E.wait("gam", i)
                E.wait("kk", i)
                link(tt(A, b4(4), Dg, ALU.mult))
                tt(A, A, bc(beta, P), ALU.mult).then_inc(sem("A"), 1)
                E.wait("A", i)
                link(tt(T, A, heads(cn("m0neg"), 4), ALU.mult))
                tt(T, T, heads(ident, 4), ALU.add)
                E.wait("tA", i)
                link(tt(U, b4(3), heads(cn("m0negT"), 4), ALU.mult))
                E.wait("qk", i)
                tt(qkm, b4(0), Dl, ALU.mult)
                tt(U, U, heads(ident, 4), ALU.add).then_inc(sem("UT"), 1)
                E.wait("hexp", i)
                hE3, hQ3 = three(hE, LEVELS, 256), three(hQ, LEVELS, 256)

                def h_queries_keys(l):
                    lev = slice(2 * l - 2, min(2 * l, LEVELS))
                    n = lev.stop - lev.start
                    if l == 4:
                        tt(hqg, hqg, three(hr[:, 0:256], 2, P), ALU.mult)
                        tt(hkd, hkd, three(he[:, 256:512], 2, P), ALU.mult)
                    link(tt(hQ3[:, lev, :], hE3[:, lev, :], heads(hr[:, 0:256], n), ALU.mult))
                    tt(hE3[:, lev, :], hE3[:, lev, :], heads(he[:, 256:512], n), ALU.mult).then_inc(sem("hKQ"), 1)

                h_queries_keys(1)
                for l in range(1, LEVELS):
                    E.wait("Z", i, l)
                    tt(Zs, b4(0), heads(cn("lev")[:, l * P:(l + 1) * P], 4), ALU.mult).then_inc(sem("Zs"), 1)
                    if l <= 3:
                        h_queries_keys(l + 1)
                    if l <= 4:
                        E.wait("hA", i, l)
                        if l == 1:
                            E.wait("keys", i)
                        lev = 2 * (l - 1)
                        mask0 = heads(cn("lev")[:, lev * P:(lev + 1) * P], 2)
                        mask1 = heads(cn("lev")[:, (lev + 1) * P:(lev + 2) * P].bitcast(I32), 2)
                        for q in range(2):
                            last = tt(khat[:, 2 * q:2 * q + 2, :], three(ps[1 + q][:, 0:256], 2, P), mask0, ALU.mult)
                        for q in range(2):
                            last = v.copy_predicated(hatt[:, 2 * q:2 * q + 2, :], mask1,
                                                     three(ps[1 + q][:, 256:512], 2, P))
                        link(last)
                        last = tt(hatt, hatt, khat, ALU.add)
                        last.then_inc(sem("hatt"), 1)
                    E.wait("dU", i, l)
                    last = tt(U, U, b4(4), ALU.subtract)
                    if l < LEVELS - 1:
                        E.wait("dT", i, l)
                        last = tt(T, T, b4(5), ALU.subtract)
                    last.then_inc(sem("UT"), 1)
                    if l == 5:
                        E.wait("gexp", i)
                        for g0, c0, w in ((0, C_RG, 256), (256, C_DZ, 512), (768, C_HG, 256)):
                            last = v.scalar_tensor_tensor(gt[:, g0:g0 + w], gt[:, g0:g0 + w], 1.0,
                                                          pj[:, c0:c0 + w], ALU.add, ALU.mult)
                        last.then_inc(sem("gate"), 1)
                E.wait("hOU", i)
                link(tt(ShB, ShB, bc(ehGL, P), ALU.mult))
                link(tt(three(he[:, 0:256], 2, P), three(ps[2][:, 0:256], 2, P), heads(cn("pair"), 2), ALU.mult))
                link(tt(ShB, ShB, three(he[:, 0:256], 2, P), ALU.add))
                link(v.tensor_scalar(sg4, rqk[:, 0:4], 128.0 ** -0.5, None, ALU.mult))
                od = three(obuf[:, 256:768], 4, P)
                E.wait("o1", i)
                link(tt(od, b4(5), bc(eG, P), ALU.mult))
                E.wait("o2", i)
                link(tt(od, od, b4(0), ALU.add))
                E.wait("r_out", i)
                E.wait("h_out", i)
                tt(od, od, bc(sg4, P), ALU.mult).then_inc(sem("od"), 1)
                link(tt(S, S, bc(eGL, P), ALU.mult))
                E.wait("od", i)
                tt(gt, obuf, gt, ALU.mult)
                E.wait("o_sq", i)
                link(v.reduce_sum(sh, hQ[:, 0:1024].rearrange("p (a b) -> p a b", a=16), AX.X))
                link(v.reduce_sum(th_[:, 0:4], sh[:, 4:12].rearrange("p (a b) -> p a b", a=4), AX.X))
                link(v.tensor_scalar(mh, sh, 1.0 / 64, EPS, ALU.mult, ALU.add))
                link(v.tensor_scalar(mh[:, 4:12].rearrange("p (a b) -> p a b", a=4), bc(th_[:, 0:4], 2), 1.0 / P,
                                     EPS, ALU.mult, ALU.add))
                rsqrt(mh, rh, th_)
                tt(obuf.rearrange("p (a b) -> p a b", a=16), gt.rearrange("p (a b) -> p a b", a=16), bc(rh, 64),
                   ALU.mult).then_inc(sem("mixed"), 1)
                E.wait("dS", i)
                link(tt(S, S, b4(3), ALU.add))
                E.wait("tm", i, 1)
                tt(mT[:, 0:4, :], b4(1), bc(gmc[:, 0:4], P), ALU.mult)
                E.wait("tm", i)
                tt(mT[:, 4:8, :], b4(2), bc(gmc[:, 4:8], P), ALU.mult).then_inc(sem("mT"), 1)
                if nxt:
                    v.memset(hatt, 0.0)
                else:
                    pick(0, NT - 1)
                    count_before()
                E.wait("xres_loaded", i)
                E.wait("wo", i)
                tt(hbuf[:, 0:512], hbuf[:, 0:512], ps[4][:, :], ALU.add)
                tt(hbuf[:, 512:1024], hbuf[:, 512:1024], ps[5][:, :], ALU.add).then_inc(sem("h_ready"), 1)
                E.wait("h_sq", i)
                link(v.tensor_scalar(m2, ss2, 1.0 / DM, EPS, ALU.mult, ALU.add))
                rsqrt(m2, r2, t2)
                v.tensor_scalar(hnb, hbuf[:, :], r2, None, ALU.mult).then_inc(sem("hn_ready"), 1)
                E.wait("t2", i, 1)
                tt(mT[:, 0:4, :], b4(0), bc(g2c[:, 0:4], P), ALU.mult)
                E.wait("t2", i)
                tt(mT[:, 4:8, :], b4(3), bc(g2c[:, 4:8], P), ALU.mult).then_inc(sem("h2T"), 1)

            dve.wait_ge(sem("x_sq"), 1)
            x_norm(0, 1)
            x_scale(0, rx[:, 0:1])
            dve.wait_ge(sem("params_loaded"), N_PARAMS)
            v.tensor_tensor(lbt[:, 0, :], lbc[:, :], lbc[:, :], ALU.subtract).then_inc(sem("lb_shifted"), 1)
            x_gain(0)
            dve.wait_ge(sem("param_exp"), 1)
            link(v.reciprocal(lbt[:, 2, :], lbt[:, 1, :]))
            link(v.tensor_tensor(lbt[:, 3, :], lbt[:, 1, :], lbt[:, 2, :], ALU.mult))
            link(v.tensor_tensor(lbv, lbt[:, 3, :], lbt[:, 3, :], ALU.subtract))
            v.tensor_scalar(oml, lbv, -1.0, 1.0, ALU.mult, ALU.add)
            v.tensor_scalar(negA, negA, -1.0, None, ALU.mult)
            v.tensor_scalar(convw[:, :, :], convw[:, :, :], 0.5, None, ALU.mult)
            v.tensor_scalar(gmc[:, :], gmc[:, :], 0.5, None, ALU.mult)
            v.memset(cb[:, :, 0:3], 0.0).then_inc(sem("hist"), 1)
            v.memset(SrB, 0.0)
            v.memset(ShB, 0.0)
            v.memset(hatt, 0.0)
            v.memset(S, 0.0).then_inc(sem("zeroed"), 1)
            dve.wait_ge(sem("x_sq"), 2)
            x_norm(1, NT)
            SETUP = E.c
            with dve.Fori(0, NT - 1) as i:
                E.start(i * DVE_LINKS + SETUP)
                mixer(i, True)
                E.end()
            E.start((NT - 1) * DVE_LINKS + SETUP)
            mixer(NT - 1, False)

            pick(NT - 1, NT)
            v.engine_nop().then_inc(sem("r_shift"), 1)
            seq(tt(mrun[:, NT, :], mrun[:, NT - 1, :], cnd[:, NT - 1, :], ALU.add))
            v.engine_nop().then_inc(sem("picked"), 1)
            dve.wait_ge(sem("r_exp"), 1)
            seq(v.reduce_sum(gm, gex, AX.X))
            seq(v.reciprocal(gm, gm))
            seq(v.tensor_scalar(m1, e2, 1.0, None, ALU.add))
            seq(v.reciprocal(m1, m1))
            seq(tt(w12[:, 0, :], gm, m1, ALU.mult))
            seq(tt(w12[:, 1, :], w12[:, 0, :], e2, ALU.mult))
            dve.wait_ge(sem("ranks"), 1)
            seq(v.tensor_copy(cnt, ps[1][:, 0:32]))
            c8 = cmp_[:, 0:256].rearrange("p (a b) -> p a b", a=32)
            seq(tt(c8, bc(cnt, 8), heads(cn("c128"), 32), ALU.is_gt))
            seq(v.reduce_sum(nblk, c8, AX.X))
            seq(v.tensor_scalar(nblk[:, 0:1], nblk[:, 0:1], 1.0, None, ALU.max))
            seq(v.tensor_tensor_scan(incl, cn("ones")[:, 0:32], nblk, 0.0, ALU.mult, ALU.add))
            seq(tt(base, incl, nblk, ALU.subtract))
            seq(v.tensor_scalar(base, base, float(BLK), None, ALU.mult))
            seq(tt(rk, ps[0][:, 0:256].rearrange("p (a b) -> p a b", a=NT), heads(base, NT), ALU.add))
            for k, oh in enumerate((oh1, oh2)):
                seq(tt(el, oh, rk, ALU.mult))
                seq(v.reduce_sum(dst[:, k, :], el, AX.X))
            dsf = dst[:, :, :].rearrange("p a b -> p (a b)")
            seq(v.tensor_copy(dsti[:, :, :].rearrange("p a b -> p (a b)"), dsf))
            dsi = dsti[:, :, :].rearrange("p a b -> p (a b)")
            v.tensor_scalar(posi, dsi, BLK - 1, None, ALU.bitwise_and)
            seq(v.tensor_scalar(blockn, dsi, BLK.bit_length() - 1, None, ALU.logical_shift_right))
            v.tensor_copy(blockf, blockn)
            seq(v.tensor_copy(posf, posi))
            v.tensor_scalar(tokf, cn("c128"), cn("pcol"), None, ALU.add)
            v.tensor_scalar(posf, posf, 1.0, None, ALU.add)
            seq(v.tensor_tensor_scan(count_row, cn("ones"), cn("ones"), 0.0, ALU.mult, ALU.add))
            seq(tt(in_blk, heads(cn("biota"), 2 * NT), bc(blockf, NB_MAX), ALU.is_equal))
            for k in range(2):
                seq(tt(in_blk[:, k * NT:(k + 1) * NT, :], in_blk[:, k * NT:(k + 1) * NT, :], bc(tokf, NB_MAX),
                       ALU.mult))
            for k in range(2):
                tt(in_pos[:, k * NT:(k + 1) * NT, :], heads(count_row, NT), bc(posf[:, k * NT:(k + 1) * NT], P),
                   ALU.is_equal).then_inc(sem("dst_ready"), 1)
            c48 = cmp_.rearrange("p (a b) -> p a b", a=NB_MAX)
            seq(tt(c48, heads(incl, NB_MAX), bc(cn("biota"), NE), ALU.is_le))
            seq(v.reduce_sum(blkt[:, 0:NB_MAX], c48, AX.X))
            seq(v.tensor_scalar(blkt[:, 0:NB_MAX], blkt[:, 0:NB_MAX], float(NE - 1), None, ALU.min))
            seq(v.tensor_scalar(cmp_[:, 0:NB_MAX // 2], cn("biota")[:, 0:NB_MAX // 2], 2.0, incl[:, NE - 1:NE],
                                ALU.mult, ALU.is_lt))
            seq(v.reduce_sum(blkt[:, NB_MAX:NB_MAX + 1], cmp_[:, 0:NB_MAX // 2], AX.X))
            seq(v.tensor_scalar(blkt[:, NB_MAX + 1:NB_MAX + 2], blkt[:, NB_MAX:NB_MAX + 1], -1.0, None, ALU.add))
            v.tensor_copy(blki[:, :], blkt[:, :]).then_inc(sem("blk_ready"), 1)
            dve.wait_ge(sem("slots_summed"), 1)
            v.tensor_copy(slots[:, :], ps[2][:, 0:NB_MAX]).then_inc(sem("slots_ready"), 1)
            dve.wait_ge(sem("blk_ready"), 1)
            pairs = dve.value_load(blki[0:1, NB_MAX:NB_MAX + 1], min_val=NB_MIN // 2, max_val=NB_MAX // 2)
            last_pair = dve.value_load(blki[0:1, NB_MAX + 1:NB_MAX + 2], min_val=NB_MIN // 2 - 1,
                                      max_val=NB_MAX // 2 - 1)

            def x_gain2(b):
                dve.wait_ge(sem("xt_done"), b + 1)
                tt(xT[:, 0:4, :], b4(0), bc(g2c[:, 0:4], P), ALU.mult)
                tt(xT[:, 4:8, :], b4(1), bc(g2c[:, 4:8], P), ALU.mult).then_inc(sem("xT_ready"), 1)

            def swiglu(b):
                dve.wait_ge(sem("eg"), b + 1)
                v.scalar_tensor_tensor(eg, eg, 1.0, ps[2][:, :], ALU.add, ALU.mult).then_inc(sem("swiglu_step"), 1)
                dve.wait_ge(sem("swiglu_step"), b + 1)
                dve.wait_ge(sem("gu_done"), b + 1)
                v.scalar_tensor_tensor(hact, eg, 0.5, ps[3][:, :], ALU.mult, ALU.mult) \
                    .then_inc(sem("hact_ready"), 1)

            def y_right(b, q, par):
                dve.wait_ge(sem("down_done"), b + 1)
                dve.wait_ge(sem(f"y_stored{par}"), q * 16 + 16)
                v.tensor_copy(yo[par][:, 512:1024], ps[6][:, :]).then_inc(sem("y1_ready"), 1)

            x_gain2(0)
            swiglu(0)
            x_gain2(1)
            with dve.Fori(1, pairs) as q:
                swiglu(2 * q - 1)
                x_gain2(2 * q)
                y_right(2 * q - 2, q - 1, 0)
                swiglu(2 * q)
                x_gain2(2 * q + 1)
                y_right(2 * q - 1, q - 1, 1)
            swiglu(last_pair * 2 + 1)
            y_right(last_pair * 2, last_pair, 0)
            y_right(last_pair * 2 + 1, last_pair, 1)

            dve.wait_ge(sem("ch_loaded"), 16)
            cc = [0]

            def cseq(ins):
                cc[0] += 1
                ins.then_inc(sem("comb_chain"), 1)
                dve.wait_ge(sem("comb_chain"), cc[0])

            def normed(t):
                dve.wait_ge(sem("c_sq"), t + 2)
                two = slice(t, t + 2)
                cseq(v.tensor_scalar(mx[:, two], ssx[:, two], 1.0 / DM, EPS, ALU.mult, ALU.add))
                rsqrt(mx[:, two], rx[:, two], tx_[:, two], cseq)
                v.engine_nop().then_inc(sem("c_root"), 1)

            for t in range(NT):
                dve.wait_ge(sem(f"rows_loaded{t}"), 32)
                hrow = cm_h[:, t, :]
                cseq(v.scalar_tensor_tensor(hrow, cm_y1[t], w12[:, 0, t:t + 1], hrow, ALU.mult, ALU.add))
                v.scalar_tensor_tensor(hrow, cm_y2[t], w12[:, 1, t:t + 1], hrow, ALU.mult, ALU.add) \
                    .then_inc(sem("c_sum"), 1)
                if t >= 2 and t % 2 == 0:
                    normed(t - 2)
            normed(NT - 2)

        @block.gpsimd
        def _(pool):
            g = nc.gpsimd
            g.memset(zrow, 0.0).then_inc(sem("zeros"), 1)
            pool.wait_ge(sem("zeros"), 1)
            spare = y_d[NB_MIN * BLK:, :].rearrange("(p a) (h c) -> p (a h) c", p=P, c=256)
            rows = spare.shape[1] // NT
            E = Engine(pool, "pool_chain", 1)

            def mixer(i):
                E.wait("rot", i)
                g.tensor_tensor(rkz, rot[:, 256:512], cn("zeta"), ALU.mult)
                E.wait("rqT", i)
                g.tensor_tensor(rqX, rqT[:, 0:2, :], three(cn("xi"), 2, P), ALU.mult).then_inc(sem("rqX"), 1)
                E.wait("gam", i)
                E.wait("khat", i)
                g.tensor_tensor(kdec, khat, bc(ekd, P), ALU.mult)
                E.link(g.tensor_tensor(bG, beta, eG, ALU.mult))
                g.tensor_tensor(kb, khat, bc(bG, P), ALU.mult).then_inc(sem("keys"), 1)
                pool.dma_start(spare[:, bass.ds(i * rows, rows), :], heads(zrow, rows)).then_inc(sem("y_zeroed"), 16)

            with pool.Fori(0, NT) as i:
                E.start(i)
                mixer(i)
                E.end()
            pool.wait_ge(sem("y_zeroed"), 16 * NT)
            pool.wait_ge(sem("slots_ready"), 1)
            pool.wait_ge(sem("hn_stored"), 32 * NT)

            def gather(b, par, first):
                if not first:
                    pool.wait_ge(sem("xt_done"), b - 1)
                g.tensor_copy(idxs[par][:, :], slots[:, bass.ds(b, 1)]).then_inc(sem("idx_ready"), 1)
                pool.wait_ge(sem("idx_ready"), b + 1)
                pool.sem_inc(sem("idx_seen"), 1)
                g.indirect_dma_start(xg[par], None, hn_d, bass.IndirectOffsetOnAxis(ap=idxs[par][:, :], axis=0)) \
                    .then_inc(sem(f"tok_loaded{par}"), 16)

            gather(0, 0, True)
            gather(1, 1, True)
            pool.wait_ge(sem("blk_ready"), 1)
            pairs = pool.value_load(blki[0:1, NB_MAX:NB_MAX + 1], min_val=NB_MIN // 2, max_val=NB_MAX // 2)
            with pool.Fori(1, pairs) as q:
                gather(2 * q, 0, False)
                gather(2 * q + 1, 1, False)

            pool.wait_ge(sem("y_stored0"), pairs * 16 + 16)
            pool.wait_ge(sem("y_stored1"), pairs * 16 + 16)
            pool.sem_inc(sem("idx_seen"), 1)
            for t in range(NT):
                for k, rows in enumerate((cm_y1, cm_y2)):
                    g.indirect_dma_start(rows[t], None, y_d,
                                         bass.IndirectOffsetOnAxis(ap=dsti[:, k, t:t + 1], axis=0)) \
                        .then_inc(sem(f"rows_loaded{t}"), 16)
            pool.wait_ge(sem("gain_loaded"), 16)
            for t in range(NT):
                pool.wait_ge(sem("c_scaled"), t + 1)
                g.tensor_tensor(cm_y1[t], cm_y2[t], fgain, ALU.mult).then_inc(sem("c_out"), 1)


IN_NAMES = ("x", "w_in", "w_out", "gdn_conv", "gdn_a_log", "gdn_dt_bias", "ret_norm", "gdn_norm", "hgrn_norm",
            "hgrn_lower_bounds", "attn_norm", "ffn_norm", "router_group", "router_expert", "w_gate", "w_up", "w_down",
            "final_norm")


def kernel(**inputs):
    import numpy as _np
    import concourse.bacc as _bacc
    from concourse import mybir as _mybir
    from concourse.bass_utils import run_bass_kernel_spmd as _run

    nc = _bacc.Bacc("TRN2", target_bir_lowering=False, num_devices=1)
    arrays, aps = {}, {}
    given = {n: _np.ascontiguousarray(inputs[n]) for n in IN_NAMES}
    given["consts"] = host_consts()
    given["rotary"] = host_rotary()
    for name, arr in given.items():
        arrays[f"in_{name}"] = arr
        aps[name] = nc.dram_tensor(f"in_{name}", arr.shape, _mybir.dt.from_np(arr.dtype), kind="ExternalInput").ap()
    out = nc.dram_tensor("out_0", (1, SEQ, DM), F32, kind="ExternalOutput").ap()
    hn_d = nc.dram_tensor("hn_rows", (SEQ, DM), F32, kind="Internal").ap()
    h_d = nc.dram_tensor("h_rows", (SEQ, DM), F32, kind="Internal").ap()
    y_d = nc.dram_tensor("y_rows", (NB_MAX * BLK, DM), F32, kind="Internal").ap()
    build(nc, aps, out, hn_d, h_d, y_d)
    r = _run(nc, [arrays], core_ids=[0])
    return r.results[0]["out_0"]
```
